# Optimizing a Trainium2 kernel written in Bass

```python
import math
import jax, jax.numpy as jnp
from jax import lax
import numpy as np

D_MODEL = 1024
BATCH = 1
SEQ = 256
DEPTH = 1

PLE_DIM = 256
D_FF = 2816
FFN_RES_WEIGHT = 0.5
NORM_EPS = 1e-6
Q_BLOCK = 128

MLA_HEADS = 8
MLA_NOPE = 64
MLA_ROPE = 32
MLA_QK = MLA_NOPE + MLA_ROPE
MLA_V = 64
Q_LORA = 384
KV_LORA = 256
ROPE_BASE = 10000.0

SB_HEADS = 8
SB_HEAD_DIM = 64
SB_WIDTH = SB_HEADS * SB_HEAD_DIM
MLA_WIDTH = MLA_HEADS * MLA_V

COL_CQ = Q_LORA
COL_CKV = KV_LORA
COL_KROPE = MLA_ROPE
COL_SB = 3 * SB_WIDTH
COL_GATES = 2 * D_MODEL
IN_COLS = COL_CQ + COL_CKV + COL_KROPE + COL_SB + COL_GATES
SPLITS = list(np.cumsum([COL_CQ, COL_CKV, COL_KROPE, COL_SB])[:])


def rms_norm(x, g):
    xf = x.astype(jnp.float32)
    r = lax.rsqrt(jnp.mean(xf * xf, axis=-1, keepdims=True) + NORM_EPS)
    return (xf * r).astype(x.dtype) * g

def apply_rope(x, positions):
    r = x.shape[-1]
    inv_freq = ROPE_BASE ** (-jnp.arange(0, r, 2, dtype=jnp.float32) / r)
    ang = positions.astype(jnp.float32)[..., None] * inv_freq
    cos = jnp.cos(ang)[:, :, None, :].astype(x.dtype)
    sin = jnp.sin(ang)[:, :, None, :].astype(x.dtype)
    x1, x2 = x[..., : r // 2], x[..., r // 2:]
    return jnp.concatenate([x1 * cos - x2 * sin, x2 * cos + x1 * sin], axis=-1)

def swiglu(u, w_in, w_out):
    a, b = jnp.split(u @ w_in, 2, axis=-1)
    return (jax.nn.silu(a) * b) @ w_out

def causal_softmax_attention(q, k, v):
    s_len = q.shape[2]
    scale = 1.0 / math.sqrt(q.shape[-1])
    outs = []
    for i in range(s_len // Q_BLOCK):
        k_len = (i + 1) * Q_BLOCK
        qb = q[:, :, i * Q_BLOCK:(i + 1) * Q_BLOCK]
        kb, vb = k[:, :, :k_len], v[:, :, :k_len]
        sc = jnp.einsum('bhqd,bhkd->bhqk', qb, kb).astype(jnp.float32) * scale
        q_pos = i * Q_BLOCK + jnp.arange(Q_BLOCK)
        mask = jnp.arange(k_len)[None, :] <= q_pos[:, None]
        w = jax.nn.softmax(jnp.where(mask, sc, -jnp.inf), axis=-1)
        outs.append(jnp.einsum('bhqk,bhkd->bhqd', w.astype(vb.dtype), vb))
    return jnp.concatenate(outs, axis=2)

def stick_breaking_attention(q, k, v):
    s_len = q.shape[2]
    scale = 1.0 / math.sqrt(q.shape[-1])
    outs = []
    for i in range(s_len // Q_BLOCK):
        k_len = (i + 1) * Q_BLOCK
        qb = q[:, :, i * Q_BLOCK:(i + 1) * Q_BLOCK]
        kb, vb = k[:, :, :k_len], v[:, :, :k_len]
        z = jnp.einsum('bhqd,bhkd->bhqk', qb, kb).astype(jnp.float32) * scale
        q_pos = i * Q_BLOCK + jnp.arange(Q_BLOCK)
        mask = jnp.arange(k_len)[None, :] < q_pos[:, None]
        log_1m = jnp.where(mask, jax.nn.log_sigmoid(-z), 0.0)
        suffix = lax.cumsum(log_1m, axis=3, reverse=True) - log_1m
        a = jnp.where(mask, jnp.exp(jax.nn.log_sigmoid(z) + suffix), 0.0)
        outs.append(jnp.einsum('bhqk,bhkd->bhqd', a.astype(vb.dtype), vb))
    return jnp.concatenate(outs, axis=2)

def first_inputs(seed: int = 0) -> dict:
    key = jax.random.key(seed)
    ks = iter(jax.random.split(key, 32))
    f32 = jnp.float32

    def w(shape, fan_in):
        return jax.random.normal(next(ks), (DEPTH,) + shape, f32) * fan_in ** -0.5

    def gain(n):
        return 1.0 + 0.02 * jax.random.normal(next(ks), (DEPTH, n), f32)

    x = jax.random.normal(next(ks), (BATCH, SEQ, D_MODEL), f32)
    p = jax.random.normal(next(ks), (DEPTH, BATCH, SEQ, PLE_DIM), f32)
    offset = jax.random.randint(next(ks), (BATCH, 1), 0, 1024, dtype=jnp.int32)
    positions = offset + jnp.arange(SEQ, dtype=jnp.int32)[None, :]
    return {
        "x": x,
        "p": p,
        "positions": positions,
        "ffn1_norm": gain(D_MODEL),
        "ffn1_w_in": w((D_MODEL, 2 * D_FF), D_MODEL),
        "ffn1_w_out": w((D_FF, D_MODEL), D_FF),
        "mix_norm": gain(D_MODEL),
        "w_in": w((D_MODEL, IN_COLS), D_MODEL),
        "q_latent_norm": gain(Q_LORA),
        "w_q_up": w((Q_LORA, MLA_HEADS * MLA_QK), Q_LORA),
        "kv_latent_norm": gain(KV_LORA),
        "w_kv_up": w((KV_LORA, MLA_HEADS * (MLA_NOPE + MLA_V)), KV_LORA),
        "q_head_norm": gain(MLA_QK),
        "k_head_norm": gain(MLA_QK),
        "w_branch_mla": w((MLA_WIDTH, D_MODEL), MLA_WIDTH),
        "w_branch_sb": w((SB_WIDTH, D_MODEL), SB_WIDTH),
        "w_out": w((D_MODEL, D_MODEL), D_MODEL),
        "ffn2_norm": gain(D_MODEL),
        "ffn2_w_in": w((D_MODEL, 2 * D_FF), D_MODEL),
        "ffn2_w_out": w((D_FF, D_MODEL), D_FF),
        "ple_norm": gain(D_MODEL),
        "w_ple_gate": w((D_MODEL, D_MODEL), D_MODEL),
        "w_ple_proj": w((PLE_DIM, D_MODEL), PLE_DIM),
    }

def first_block(x, p, positions, ffn1_norm, ffn1_w_in, ffn1_w_out, mix_norm, w_in,
              q_latent_norm, w_q_up, kv_latent_norm, w_kv_up, q_head_norm, k_head_norm,
              w_branch_mla, w_branch_sb, w_out, ffn2_norm, ffn2_w_in, ffn2_w_out,
              ple_norm, w_ple_gate, w_ple_proj):
    b, s, _ = x.shape
    h = x
    for i in range(DEPTH):
        h = h + FFN_RES_WEIGHT * swiglu(rms_norm(h, ffn1_norm[i]), ffn1_w_in[i], ffn1_w_out[i])

        u = rms_norm(h, mix_norm[i])
        proj = u @ w_in[i]
        c_q, c_kv, k_rope, sb_qkv, gates = jnp.split(proj, SPLITS, axis=-1)

        q = (rms_norm(c_q, q_latent_norm[i]) @ w_q_up[i]).reshape(b, s, MLA_HEADS, MLA_QK)
        kv = (rms_norm(c_kv, kv_latent_norm[i]) @ w_kv_up[i]).reshape(b, s, MLA_HEADS, MLA_NOPE + MLA_V)
        k_nope, v_mla = kv[..., :MLA_NOPE], kv[..., MLA_NOPE:]
        k_r = jnp.broadcast_to(k_rope[:, :, None, :], (b, s, MLA_HEADS, MLA_ROPE))
        k = jnp.concatenate([k_nope, k_r], axis=-1)
        q = rms_norm(q, q_head_norm[i])
        k = rms_norm(k, k_head_norm[i])
        q = jnp.concatenate([q[..., :MLA_NOPE], apply_rope(q[..., MLA_NOPE:], positions)], axis=-1)
        k = jnp.concatenate([k[..., :MLA_NOPE], apply_rope(k[..., MLA_NOPE:], positions)], axis=-1)
        o_mla = causal_softmax_attention(q.transpose(0, 2, 1, 3), k.transpose(0, 2, 1, 3),
                                         v_mla.transpose(0, 2, 1, 3))
        o_mla = o_mla.transpose(0, 2, 1, 3).reshape(b, s, MLA_WIDTH)

        sq, sk, sv = [t.reshape(b, s, SB_HEADS, SB_HEAD_DIM).transpose(0, 2, 1, 3)
                      for t in jnp.split(sb_qkv, 3, axis=-1)]
        o_sb = stick_breaking_attention(sq, sk, sv)
        o_sb = o_sb.transpose(0, 2, 1, 3).reshape(b, s, SB_WIDTH)

        g_mla, g_sb = jnp.split(jax.nn.sigmoid(gates), 2, axis=-1)
        merged = g_mla * (o_mla @ w_branch_mla[i]) + g_sb * (o_sb @ w_branch_sb[i])
        h = h + merged @ w_out[i]

        h = h + FFN_RES_WEIGHT * swiglu(rms_norm(h, ffn2_norm[i]), ffn2_w_in[i], ffn2_w_out[i])

        ple_gate = jax.nn.sigmoid(rms_norm(h, ple_norm[i]) @ w_ple_gate[i])
        h = h + ple_gate * (p[i] @ w_ple_proj[i])
    return h


DEPTH_2 = 2

N_A_LAYERS = DEPTH_2 // 2
N_B_LAYERS = DEPTH_2 - N_A_LAYERS
N_HEADS = 16
HEAD_DIM = 64
N_KV_GROUPS = 4
HEADS_PER_GROUP = N_HEADS // N_KV_GROUPS
D_FF_2 = 4 * D_MODEL
CONV_WIDTH = 3
CMP_BLOCK = 32
CMP_STRIDE = 16
SEL_BLOCK = 64
SEL_TOP_N = 16
WINDOW = 512
PHI_HIDDEN = 256
N_BUCKETS = 32
MAX_DISTANCE = 128
EPS = 1e-6
NEG_INF = -1e30
FORCED_SCORE = 1e9


def rms_norm_2(x, g):
    xf = x.astype(jnp.float32)
    y = xf * lax.rsqrt(jnp.mean(xf * xf, axis=-1, keepdims=True) + EPS)
    return (y * g.astype(jnp.float32)).astype(x.dtype)

def t5_bucket(dist):
    dist = jnp.maximum(dist, 0)
    max_exact = N_BUCKETS // 2
    logd = jnp.log(jnp.maximum(dist, 1).astype(jnp.float32) / max_exact)
    large = max_exact + (logd / math.log(MAX_DISTANCE / max_exact)
                         * (N_BUCKETS - max_exact)).astype(jnp.int32)
    large = jnp.minimum(large, N_BUCKETS - 1)
    return jnp.where(dist < max_exact, dist, large)

def short_conv_mixer(h, w_in, conv_w, w_out):
    S = h.shape[1]
    b_gate, c_gate, u = jnp.split(h @ w_in, 3, axis=-1)
    v = c_gate * u
    vp = jnp.pad(v, ((0, 0), (CONV_WIDTH - 1, 0), (0, 0)))
    conv = sum(conv_w[k] * vp[:, k:k + S] for k in range(CONV_WIDTH))
    return (b_gate * conv) @ w_out

def squared_relu_mlp(h, w1, w2):
    return jnp.square(jax.nn.relu(h @ w1)) @ w2

def compress_blocks(t, pe, w1, w2):
    B, S, G, dh = t.shape
    chunks = t.reshape(B, S // CMP_STRIDE, CMP_STRIDE, G, dh)
    blocks = jnp.concatenate([chunks[:, :-1], chunks[:, 1:]], axis=2)
    blocks = blocks + pe[None, None, :, None, :]
    n_cmp = blocks.shape[1]
    flat = jnp.moveaxis(blocks, 2, 3).reshape(B, n_cmp, G, CMP_BLOCK * dh)
    return jax.nn.silu(flat @ w1) @ w2

def nsa_shared_kv(h, w_kv, cmp_pe_k, cmp_pe_v, phi_k_w1, phi_k_w2, phi_v_w1, phi_v_w2):
    B, S, _ = h.shape
    kv = (h @ w_kv).reshape(B, S, 6, N_KV_GROUPS, HEAD_DIM)
    k_raw, v_raw = kv[:, :, 0], kv[:, :, 1]
    k_sel, v_sel = kv[:, :, 2], kv[:, :, 3]
    k_win, v_win = kv[:, :, 4], kv[:, :, 5]
    k_cmp = compress_blocks(k_raw, cmp_pe_k, phi_k_w1, phi_k_w2)
    v_cmp = compress_blocks(v_raw, cmp_pe_v, phi_v_w1, phi_v_w2)
    return (k_cmp, v_cmp, k_sel, v_sel, k_win, v_win)

def nsa_attention(q, gates, k_cmp, v_cmp, k_sel, v_sel, k_win, v_win, rel_bias):
    B, S, G, Hg, dh = q.shape
    n_cmp = k_cmp.shape[1]
    n_selb = S // SEL_BLOCK
    top_n = min(SEL_TOP_N, n_selb)
    n_qb = S // Q_BLOCK
    bias_g = rel_bias.reshape(N_BUCKETS, G, Hg)

    cmp_end = jnp.arange(n_cmp) * CMP_STRIDE + CMP_BLOCK - 1
    ratio = SEL_BLOCK // CMP_STRIDE
    span = CMP_BLOCK // CMP_STRIDE
    offs = (jnp.arange(ratio)[:, None] - jnp.arange(span)[None, :]).reshape(-1)
    map_idx = ratio * jnp.arange(n_selb)[:, None] + offs[None, :]
    map_ok = (map_idx >= 0) & (map_idx < n_cmp)
    map_idx = jnp.clip(map_idx, 0, n_cmp - 1)

    k_sel_bg = jnp.transpose(k_sel.reshape(B, n_selb, SEL_BLOCK, G, dh), (0, 3, 1, 2, 4))
    v_sel_bg = jnp.transpose(v_sel.reshape(B, n_selb, SEL_BLOCK, G, dh), (0, 3, 1, 2, 4))
    k_win_p = jnp.pad(k_win, ((0, 0), (WINDOW, 0), (0, 0), (0, 0)))
    v_win_p = jnp.pad(v_win, ((0, 0), (WINDOW, 0), (0, 0), (0, 0)))
    b_ix = jnp.arange(B)[:, None, None, None]
    g_ix = jnp.arange(G)[None, None, :, None]
    jb = jnp.arange(n_selb)

    def one_block(qb):
        t0 = qb * Q_BLOCK
        qt = lax.dynamic_slice_in_dim(q, t0, Q_BLOCK, axis=1)
        gt = lax.dynamic_slice_in_dim(gates, t0, Q_BLOCK, axis=1)
        pos = t0 + jnp.arange(Q_BLOCK)

        d_c = pos[:, None] - cmp_end[None, :]
        valid_c = d_c >= 0
        bias_c = jnp.transpose(bias_g[t5_bucket(d_c)], (0, 2, 3, 1)).astype(jnp.float32)
        logit_c = jnp.einsum('bqghd,bngd->bqghn', qt, k_cmp).astype(jnp.float32) + bias_c[None]
        logit_c = jnp.where(valid_c[None, :, None, None, :], logit_c, NEG_INF)
        has_any = jnp.any(valid_c, axis=-1).astype(jnp.float32)
        p_c = jax.nn.softmax(logit_c, axis=-1) * has_any[None, :, None, None, None]
        o_c = jnp.einsum('bqghn,bngd->bqghd', p_c.astype(v_cmp.dtype), v_cmp)

        imp = p_c.sum(axis=3)
        imp_s = jnp.sum(jnp.where(map_ok, jnp.take(imp, map_idx, axis=-1), 0.0), axis=-1)
        cb = pos // SEL_BLOCK
        forced = (jb[None, :] == 0) | (jb[None, :] == cb[:, None]) | (jb[None, :] == cb[:, None] - 1)
        future = jb[None, :] > cb[:, None]
        score = jnp.where(forced[None, :, None, :], FORCED_SCORE, imp_s)
        score = jnp.where(future[None, :, None, :], NEG_INF, score)
        top_s, top_idx = lax.top_k(score, top_n)
        blk_ok = top_s > NEG_INF * 0.5

        ks = k_sel_bg[b_ix, g_ix, top_idx].reshape(B, Q_BLOCK, G, top_n * SEL_BLOCK, dh)
        vs = v_sel_bg[b_ix, g_ix, top_idx].reshape(B, Q_BLOCK, G, top_n * SEL_BLOCK, dh)
        kpos = (top_idx[..., None] * SEL_BLOCK + jnp.arange(SEL_BLOCK)).reshape(B, Q_BLOCK, G, -1)
        blk_ok_k = jnp.repeat(blk_ok, SEL_BLOCK, axis=-1)
        d_s = pos[None, :, None, None] - kpos
        valid_s = blk_ok_k & (d_s >= 0)
        bias_s = jnp.transpose(bias_g[t5_bucket(d_s), g_ix], (0, 1, 2, 4, 3)).astype(jnp.float32)
        logit_s = jnp.einsum('bqghd,bqgkd->bqghk', qt, ks).astype(jnp.float32) + bias_s
        logit_s = jnp.where(valid_s[:, :, :, None, :], logit_s, NEG_INF)
        p_s = jax.nn.softmax(logit_s, axis=-1)
        o_s = jnp.einsum('bqghk,bqgkd->bqghd', p_s.astype(vs.dtype), vs)

        kw = lax.dynamic_slice_in_dim(k_win_p, t0, Q_BLOCK + WINDOW, axis=1)
        vw = lax.dynamic_slice_in_dim(v_win_p, t0, Q_BLOCK + WINDOW, axis=1)
        wpos = t0 - WINDOW + jnp.arange(Q_BLOCK + WINDOW)
        d_w = pos[:, None] - wpos[None, :]
        valid_w = (d_w >= 0) & (d_w < WINDOW) & (wpos[None, :] >= 0)
        bias_w = jnp.transpose(bias_g[t5_bucket(d_w)], (0, 2, 3, 1)).astype(jnp.float32)
        logit_w = jnp.einsum('bqghd,bkgd->bqghk', qt, kw).astype(jnp.float32) + bias_w[None]
        logit_w = jnp.where(valid_w[None, :, None, None, :], logit_w, NEG_INF)
        p_w = jax.nn.softmax(logit_w, axis=-1)
        o_w = jnp.einsum('bqghk,bkgd->bqghd', p_w.astype(vw.dtype), vw)

        o = gt[..., 0:1] * o_c + gt[..., 1:2] * o_s + gt[..., 2:3] * o_w
        return o.astype(q.dtype)

    o = lax.map(one_block, jnp.arange(n_qb))
    return jnp.moveaxis(o, 0, 1).reshape(B, S, G, Hg, dh)

def nsa_mixer(h, w_qg, w_o, shared, rel_bias):
    B, S, _ = h.shape
    qg = h @ w_qg
    q = qg[..., :N_HEADS * HEAD_DIM].reshape(B, S, N_KV_GROUPS, HEADS_PER_GROUP, HEAD_DIM)
    q = q * (HEAD_DIM ** -0.5)
    gates = jax.nn.sigmoid(qg[..., N_HEADS * HEAD_DIM:].astype(jnp.float32))
    gates = gates.reshape(B, S, N_KV_GROUPS, HEADS_PER_GROUP, 3)
    k_cmp, v_cmp, k_sel, v_sel, k_win, v_win = shared
    o = nsa_attention(q, gates, k_cmp, v_cmp, k_sel, v_sel, k_win, v_win, rel_bias)
    return o.reshape(B, S, N_HEADS * HEAD_DIM) @ w_o

def second_inputs(seed: int = 0) -> dict:
    key = jax.random.key(seed)
    ks = jax.random.split(key, 22)
    f32 = jnp.float32
    D, H, G, dh = D_MODEL, N_HEADS, N_KV_GROUPS, HEAD_DIM

    def nrm(k, shape, scale):
        return jax.random.normal(k, shape, f32) * scale

    return {
        "x": nrm(ks[0], (BATCH, SEQ, D), 1.0),
        "rel_bias": nrm(ks[1], (N_BUCKETS, H), 0.5),
        "norm_mix": 1.0 + nrm(ks[2], (DEPTH_2, D), 0.1),
        "norm_mlp": 1.0 + nrm(ks[3], (DEPTH_2, D), 0.1),
        "mlp_w1": nrm(ks[4], (DEPTH_2, D, D_FF_2), D ** -0.5),
        "mlp_w2": nrm(ks[5], (DEPTH_2, D_FF_2, D), 0.5 * D_FF_2 ** -0.5),
        "a_w_in": nrm(ks[6], (N_A_LAYERS, D, 3 * D), D ** -0.5),
        "a_conv_w": nrm(ks[7], (N_A_LAYERS, CONV_WIDTH, D), CONV_WIDTH ** -0.5),
        "a_w_out": nrm(ks[8], (N_A_LAYERS, D, D), D ** -0.5),
        "kv_norm": 1.0 + nrm(ks[9], (D,), 0.1),
        "w_kv": nrm(ks[10], (D, 6 * G * dh), D ** -0.5),
        "cmp_pe_k": nrm(ks[11], (CMP_BLOCK, dh), 0.1),
        "cmp_pe_v": nrm(ks[12], (CMP_BLOCK, dh), 0.1),
        "phi_k_w1": nrm(ks[13], (CMP_BLOCK * dh, PHI_HIDDEN), (CMP_BLOCK * dh) ** -0.5),
        "phi_k_w2": nrm(ks[14], (PHI_HIDDEN, dh), PHI_HIDDEN ** -0.5),
        "phi_v_w1": nrm(ks[15], (CMP_BLOCK * dh, PHI_HIDDEN), (CMP_BLOCK * dh) ** -0.5),
        "phi_v_w2": nrm(ks[16], (PHI_HIDDEN, dh), PHI_HIDDEN ** -0.5),
        "b_w_qg": nrm(ks[17], (N_B_LAYERS, D, H * dh + 3 * H), D ** -0.5),
        "b_w_o": nrm(ks[18], (N_B_LAYERS, H * dh, D), (H * dh) ** -0.5),
        "final_norm": 1.0 + nrm(ks[19], (D,), 0.1),
    }

def second_block(x, rel_bias, norm_mix, norm_mlp, mlp_w1, mlp_w2, a_w_in, a_conv_w, a_w_out,
              kv_norm, w_kv, cmp_pe_k, cmp_pe_v, phi_k_w1, phi_k_w2, phi_v_w1, phi_v_w2,
              b_w_qg, b_w_o, final_norm):
    shared = None
    for layer in range(DEPTH_2):
        h = rms_norm_2(x, norm_mix[layer])
        if layer < N_A_LAYERS:
            x = x + short_conv_mixer(h, a_w_in[layer], a_conv_w[layer], a_w_out[layer])
        else:
            i = layer - N_A_LAYERS
            x = x + nsa_mixer(h, b_w_qg[i], b_w_o[i], shared, rel_bias)
        x = x + squared_relu_mlp(rms_norm_2(x, norm_mlp[layer]), mlp_w1[layer], mlp_w2[layer])
        if layer == N_A_LAYERS - 1:
            shared = nsa_shared_kv(rms_norm_2(x, kv_norm), w_kv, cmp_pe_k, cmp_pe_v,
                                   phi_k_w1, phi_k_w2, phi_v_w1, phi_v_w2)
    return rms_norm_2(x, final_norm)


def setup_inputs(seed=0):
    out = dict(first_inputs(seed))
    for name, value in second_inputs(seed + 1).items():
        if name != "x":
            out[name + "_2"] = value
    return out


def reference(
    x, p, positions, ffn1_norm, ffn1_w_in, ffn1_w_out, mix_norm, w_in, q_latent_norm, w_q_up,
    kv_latent_norm, w_kv_up, q_head_norm, k_head_norm, w_branch_mla, w_branch_sb, w_out,
    ffn2_norm, ffn2_w_in, ffn2_w_out, ple_norm, w_ple_gate, w_ple_proj, rel_bias_2, norm_mix_2,
    norm_mlp_2, mlp_w1_2, mlp_w2_2, a_w_in_2, a_conv_w_2, a_w_out_2, kv_norm_2, w_kv_2,
    cmp_pe_k_2, cmp_pe_v_2, phi_k_w1_2, phi_k_w2_2, phi_v_w1_2, phi_v_w2_2, b_w_qg_2, b_w_o_2,
    final_norm_2,
):
    x = first_block(
        x, p, positions, ffn1_norm, ffn1_w_in, ffn1_w_out, mix_norm, w_in, q_latent_norm,
        w_q_up, kv_latent_norm, w_kv_up, q_head_norm, k_head_norm, w_branch_mla, w_branch_sb,
        w_out, ffn2_norm, ffn2_w_in, ffn2_w_out, ple_norm, w_ple_gate, w_ple_proj,
    )
    return second_block(
        x, rel_bias_2, norm_mix_2, norm_mlp_2, mlp_w1_2, mlp_w2_2, a_w_in_2, a_conv_w_2,
        a_w_out_2, kv_norm_2, w_kv_2, cmp_pe_k_2, cmp_pe_v_2, phi_k_w1_2, phi_k_w2_2,
        phi_v_w1_2, phi_v_w2_2, b_w_qg_2, b_w_o_2, final_norm_2,
    )


_drawn_inputs = setup_inputs


def setup_inputs(seed=0):
    import zlib

    import numpy as np

    out = dict(_drawn_inputs(seed))
    spreads = {}
    factors = {'ffn1_norm': 5.319,
     'mix_norm': 4.787,
     'q_latent_norm': 8.0,
     'kv_latent_norm': 8.0,
     'q_head_norm': 8.0,
     'k_head_norm': 8.0,
     'ffn2_norm': 16.116,
     'ple_norm': 200.0,
     'kv_norm_2': 10.466,
     'cmp_pe_k_2': 200.0,
     'cmp_pe_v_2': 155.781,
     'rel_bias_2': 9.742,
     'norm_mix_2': 3.404,
     'norm_mlp_2': 8.0,
     'p': 5.334,
     'w_ple_gate': 7.445,
     'w_ple_proj': 5.198}
    for name, (base, spread) in spreads.items():
        noise = np.random.default_rng([zlib.crc32(name.encode()), seed]).standard_normal(out[name].shape)
        drawn = base * np.exp(spread * noise) if base else spread * noise
        out[name] = __import__('jax').numpy.asarray(drawn.astype(out[name].dtype))
    for name, factor in factors.items():
        out[name] = (out[name] * factor).astype(out[name].dtype)
    return out
```

```python
from contextlib import ExitStack

import numpy as np

import concourse.bass as bass
from concourse import mybir

F32 = mybir.dt.float32
F32R = mybir.dt.float32r
BF16 = mybir.dt.bfloat16
I32 = mybir.dt.int32
ALU = mybir.AluOpType
ACT = mybir.ActivationFunctionType
AX = mybir.AxisListType

P = 128
S = 256
D = 1024
KT = D // P
FF = 2816 // P
MF = 4096 // P // 2
EPS = 1e-6
NEG = -1e30
RING = 3
CH = 2048
HEADS, NOPE, ROPE = 8, 64, 32
QK = NOPE + ROPE
NCMP = S // 16 - 1
NVALID0 = 7
G_HEADS = 16
UPDATES = 4

_sizes = [("ffn1", FF + FF // 2), ("latent", 3), ("sb_q", 2), ("sb_k", 2), ("sb_v", 2), ("gates", 8),
          ("q_up", 2), ("kv_up", 1), ("branch", 4), ("w_out", 4), ("ffn2", FF + FF // 2),
          ("ple_gate", 4), ("ple_proj", 1), ("conv_in", 12), ("conv_out", 4), ("mlp0", 2 * MF),
          ("kv_raw", 2), ("k_att", 2), ("v_att", 2), ("phi", 4), ("nsa_q", 4), ("nsa_gate", 1),
          ("nsa_out", 4), ("mlp1", 2 * MF)]
C, _at = {}, 0
for _name, _n in _sizes:
    C[_name] = _at
    _at += _n
N_CHUNKS = _at
assert N_CHUNKS % RING == 0

_pieces = [("ffn1", 4), ("mix", 4), ("c_q", 2), ("c_kv", 1), ("o_mla", 2), ("o_sb", 2), ("merged", 4),
           ("ffn2", 4), ("ple", 4), ("p", 1), ("mix0", 4), ("conv", 4), ("mlp0", 4), ("kv", 4),
           ("blk_k", 1), ("blk_v", 1), ("mix1", 4), ("o_nsa", 4), ("mlp1", 4)]
PC, _at = {}, 0
for _name, _n in _pieces:
    PC[_name] = _at
    _at += _n

_small = [("ffn1", 8), ("mix", 8), ("c_q", 3), ("c_kv", 2), ("ffn2", 8), ("ple", 8), ("mix0", 8),
          ("mlp0", 8), ("kv", 8), ("mix1", 8), ("mlp1", 8), ("final", 8), ("conv_w", 24),
          ("q_head", 1), ("k_head", 1), ("pe_k", 16), ("pe_v", 16), ("phi_k2", 128), ("phi_v2", 128)]
SM, _at = {}, 0
for _name, _n in _small:
    SM[_name] = _at
    _at += _n
N_SMALL = _at

_const = [("ident", 128), ("tri", 128), ("sb_neg", 384), ("mla_neg", 256), ("rot", 32), ("bucket", 384),
          ("pick", 31), ("flip", 128), ("inv_freq", 1), ("has_any", 1)]
CN, _at = {}, 0
for _name, _n in _const:
    CN[_name] = _at
    _at += _n
N_CONST = _at

ACC, TURN, SUMS = 0, 4, 7
HID = {"ffn1": 0, "ffn2": FF, "mlp0": 2 * FF, "mlp1": 2 * FF + MF}
ENDS = {"ffn1": 0, "ffn2": 3, "mlp0": 6, "mlp1": 9}
UPD = {"ffn1": 0, "mix": 4, "ffn2": 8, "ple": 12, "mix0": 16, "mlp0": 20, "kv": 24, "mlp1": 28, "final": 32}
NORMS = ["ffn1", "mix", "c_q", "c_kv", "head", "ffn2", "ple", "mix0", "mlp0", "kv", "mlp1", "final"]
NO = {n: i for i, n in enumerate(NORMS)}
_sq, _at = {}, 0
for _n, _c in (("ffn1", 4), ("mix", 4), ("c_q", 2), ("c_kv", 1), ("head", 8), ("ffn2", 4), ("ple", 4),
               ("mix0", 4), ("mlp0", 4), ("kv", 4), ("mlp1", 4), ("final", 4)):
    _sq[_n] = _at
    _at += _c
SQ = _sq
DRAIN = {"latent": 0, "sb": 3, "gates": 7, "conv": 15}


class Steps:

    def __init__(self, eng, sem):
        self.eng, self.sem, self.n = eng, sem, 0

    def inc(self, ins):
        ins.then_inc(self.sem, 1)
        self.n = self.n + 1

    def wait(self):
        self.eng.wait_ge(self.sem, self.n)

    def done(self, ins):
        self.inc(ins)
        self.wait()


def program(nc, x_t, p_t, positions, weights, small, consts, rel_bias, bias_rows, out):
    with ExitStack() as ctx:
        def sb(name, shape, dt=F32):
            return ctx.enter_context(nc.sbuf_tensor(name, shape, dt))

        def sem(name):
            return ctx.enter_context(nc.semaphore(name))

        bank = ctx.enter_context(nc.psum_tensor("bank", [P, 8, 512], F32))

        raw = sb("raw", [P, RING, CH])
        w_hi = sb("w_hi", [P, RING, CH], F32R)
        w_lo = sb("w_lo", [P, RING, CH], F32R)
        h = sb("h", [P, KT, S])
        x_f, x_h, x_l = sb("x_f", [P, KT, S]), sb("x_h", [P, KT, S], F32R), sb("x_l", [P, KT, S], F32R)
        y_f, y_h, y_l = sb("y_f", [P, KT, S]), sb("y_h", [P, KT, S], F32R), sb("y_l", [P, KT, S], F32R)
        sq = sb("sq", [P, KT, S])
        hid_f, hid_h, hid_l = sb("hid_f", [P, 2, S]), sb("hid_h", [P, 2, S], F32R), sb("hid_l", [P, 2, S], F32R)
        t_exp, t_a, t_b, r_sb = sb("t_exp", [P, S]), sb("t_a", [P, S]), sb("t_b", [P, S]), sb("r_sb", [P, S])
        t_m = sb("t_m", [P, S])
        heads = sb("heads", [P, 16, S])
        gate_or_bias = sb("gate_or_bias", [P, 16, S])
        sv = sb("sv", [P, 2, 512])
        mv = sb("mv", [P, 2, 512])
        par = sb("par", [P, N_SMALL])
        con = sb("con", [P, N_CONST])
        ones = sb("ones", [P, P])
        zeros = sb("zeros", [P, 512], BF16)
        relb = sb("relb", [33, 16])
        bias_1d = sb("bias_1d", [16, 384])
        pos_i, rope_tab = sb("pos_i", [P, S], I32), sb("rope_tab", [P, 2, S])
        v_pad = sb("v_pad", [P, 2, S + 2])
        cmp_hid = sb("cmp_hid", [P, 2, 2, 60])
        k_cmp = sb("k_cmp", [P, 2, 16])
        v_cmp = sb("v_cmp", [16, 256])
        nsa_g = sb("nsa_g", [P, 2, 48])
        stat = sb("stat", [P, 64])

        raw_landed = [sem(f"raw_landed{i}") for i in range(RING)]
        hi_split, lo_split, chunk_used = sem("hi_split"), sem("lo_split"), sem("chunk_used")
        x_in, small_in, con_in, relb_in, pos_in, p_in = (
            sem("x_in"), sem("small_in"), sem("con_in"), sem("relb_in"), sem("pos_in"), sem("p_in"))
        setup = sem("setup")
        sq_ready, ss_ready, ms_ready, r0_ready = sem("sq_ready"), sem("ss_ready"), sem("ms_ready"), sem("r0_ready")
        full_ready, op_hi, op_lo = sem("full_ready"), sem("op_hi"), sem("op_lo")
        ffn_sig, hid_full, hid_hi, hid_lo = sem("ffn_sig"), sem("hid_full"), sem("hid_hi"), sem("hid_lo")
        acc_ready, h_upd, drained = sem("acc_ready"), sem("h_upd"), sem("drained")
        dve_step, act_step = sem("dve_step"), sem("act_step")
        conv_c = sem("conv_c")
        rope_ang, rope_sin = sem("rope_ang"), sem("rope_sin")
        sv_done, qk_raw, ss_head = sem("sv_done"), sem("qk_raw"), sem("ss_head")
        r_head, bc_ready, normed, rot_ready, rope_cos, roped = (
            sem("r_head"), sem("bc_ready"), sem("normed"), sem("rot_ready"), sem("rope_cos"), sem("roped"))
        m_scores, m_max, m_exp, m_prob, m_pt, m_ptc, m_pv = (
            sem("m_scores"), sem("m_max"), sem("m_exp"), sem("m_prob"), sem("m_pt"), sem("m_ptc"), sem("m_pv"))
        s_z, s_abs, s_min, s_ln, s_l, s_e, s_x, s_a, s_pv = (
            sem("s_z"), sem("s_abs"), sem("s_min"), sem("s_ln"), sem("s_l"), sem("s_e"), sem("s_x"), sem("s_a"),
            sem("s_pv"))
        merged_done = sem("merged_done")
        ple_sig = sem("ple_sig")
        bias_ready, bias_out, bias_in = sem("bias_ready"), sem("bias_out"), sem("bias_in")
        bias_mm, flipped, unflipped = sem("bias_mm"), sem("flipped"), sem("unflipped")
        kv_done, blk_ready = sem("kv_done"), sem("blk_ready")
        phi_sig, phi_hid, phi_mm, cmp_done = sem("phi_sig"), sem("phi_hid"), sem("phi_mm"), sem("cmp_done")
        q_done, g_sig = sem("q_done"), sem("g_sig")
        n_scores, n_max, n_exp, n_prob, n_pt, n_ptc, n_ptd, n_pv = (
            sem("n_scores"), sem("n_max"), sem("n_exp"), sem("n_prob"), sem("n_pt"), sem("n_ptc"), sem("n_ptd"),
            sem("n_pv"))
        y_ready, stored = sem("y_ready"), sem("stored")

        def col(name, i=0, n=1):
            return par[:, SM[name] + i:SM[name] + i + n]

        def cst(name, n, i=0):
            return con[:, CN[name] + i:CN[name] + i + n]

        ident = cst("ident", P)
        flat = lambda t: t[:, :, :].rearrange("p a b -> p (a b)")
        x_flat, sq_flat, y_flat = flat(x_f), flat(sq), flat(y_f)

        m_p = [x_flat[:, 384 * i:384 * i + 384] for i in range(2)]
        m_t = [x_flat[:, 768 + 384 * i:1152 + 384 * i] for i in range(2)]
        s_t1 = x_flat[:, 1536:1920]
        s_t2, s_m, s_lm = (sq_flat[:, 384 * i:384 * i + 384] for i in range(3))
        s_p = [sq_flat[:, 1152 + 384 * i:1536 + 384 * i] for i in range(2)]
        n_pa = [x_flat[:, 512 * i:512 * i + 512] for i in range(2)]
        n_pb = [x_flat[:, 1024 + 288 * i:1312 + 288 * i] for i in range(2)]
        n_t = [sq_flat[:, 1024 * i:1024 * i + 1024] for i in range(2)]
        sb_q, sb_k = y_f[:, 0:4, :], y_f[:, 4:8, :]
        gate = gate_or_bias
        lat_f = gate_or_bias[:, 0:5, :]
        lat_raw = heads[:, 0:5, :]
        n_q, n_ks, n_kw, n_vs, n_vw = heads[:, 0:8, :], heads[:, 8:10, :], heads[:, 10:12, :], heads[:, 12:14, :], heads[:, 14:16, :]
        k_rope = t_b

        block = ctx.enter_context(nc.Block())

        @block.sync
        def _(sp):
            sp.dma_start(h[:, :, :], x_t).then_inc(x_in, 16)
            sp.dma_start(par[:, :], small).then_inc(small_in, 16)
            for c in range(RING):
                sp.dma_start(raw[:, c, :], weights[c]).then_inc(raw_landed[c], 16)
            sp.dma_start(con[:, :], consts).then_inc(con_in, 16)
            sp.dma_start(relb[0:32, :], rel_bias).then_inc(relb_in, 16)
            sp.dma_start(pos_i[64:96, :], positions.partition_broadcast(32)).then_inc(pos_in, 16)
            with sp.Fori(1, N_CHUNKS // RING) as i:
                for j in range(RING):
                    sp.wait_ge(lo_split, RING * i + (j - RING + 1))
                    sp.dma_start(raw[:, j, :], weights[i * RING + j]).then_inc(raw_landed[j], 16)
            for j in range(UPDATES):
                sp.wait_ge(y_ready, j + 1)
                sp.dma_start(out[:, 2 * j:2 * j + 2, :], x_f[:, 2 * j:2 * j + 2, :]).then_inc(stored, 16)
            sp.wait_ge(stored, 16 * UPDATES)

        @block.gpsimd
        def _(pool):
            for n, (t, value) in enumerate(((ones[:, :], 1.0), (zeros[:, :], 0.0), (v_pad[:, :, :], 0.0),
                                            (relb[32:33, :], NEG), (v_cmp[:, :], 0.0))):
                if n >= 1:
                    pool.wait_ge(setup, n)
                nc.gpsimd.memset(t, value).then_inc(setup, 1)
            pool.wait_ge(setup, 5)
            for p in range(8):
                pool.wait_ge(normed, p + 1)
                pool.wait_ge(rope_sin, 2)
                if p >= 1:
                    pool.wait_ge(roped, p)
                y = heads[64:96, 2 * p:2 * p + 2, :]
                cos = rope_tab[64:96, 0:1, :].to_broadcast([32, 2, S])
                nc.gpsimd.tensor_tensor(v_pad[64:96, :, 0:S], y, cos, ALU.mult).then_inc(rope_cos, 1)
            pool.wait_ge(roped, 8)
            nc.gpsimd.memset(v_pad[:, :, 0:2], 0.0).then_inc(setup, 1)
            pool.wait_ge(bias_ready, 1)
            pool.dma_start(bias_rows.ap(), bias_1d[:, :]).then_inc(bias_out, 16)
            pool.wait_ge(bias_out, 16)
            pool.wait_ge(merged_done, UPDATES)
            hankel = bass.AP(tensor=bias_rows, offset=0, ap=[[1, P], [384, G_HEADS], [1, S]])
            pool.dma_start(gate_or_bias[:, :, :], hankel).then_inc(bias_in, 16)
            pool.wait_ge(m_pv, 2 * HEADS)
            pool.dma_start(heads[:, 0:2, :], p_t).then_inc(p_in, 16)
            pool.wait_ge(bias_in, 16)
            pool.wait_ge(p_in, 16)

        @block.scalar
        def _(act):
            st = Steps(act, act_step)

            def split(c, s, turn):
                act.wait_ge(raw_landed[s], 16 * turn)
                nc.scalar.activation(w_hi[:, s, :], raw[:, s, :], ACT.Copy).then_inc(hi_split, 1)

            def nxt(c):
                if c + RING < N_CHUNKS:
                    act.wait_ge(chunk_used, c + 1)
                    split(c + RING, c % RING, (c + RING) // RING + 1)

            def nxt_in(c0, j, i, step):
                c = c0 + j
                if isinstance(i, int):
                    nxt(c + i * step)
                    return
                act.wait_ge(chunk_used, i * step + (c + 1))
                split(None, c % RING, i * (step // RING) + (c // RING + 2))

            def hi(dst, src, full_sem, full_value, free=None):
                act.wait_ge(full_sem, full_value)
                if free is not None:
                    act.wait_ge(chunk_used, free)
                nc.scalar.activation(dst, src, ACT.Copy).then_inc(op_hi, 1)

            def squares(name, src, pieces, upd=None, free=None):
                for j, (a, b) in enumerate(pieces):
                    if upd is not None:
                        act.wait_ge(h_upd, upd + j + 1)
                    nc.scalar.activation(sq[:, a:b, :], src[:, a:b, :], ACT.Square).then_inc(sq_ready, 1)

            def rsqrt(name, rows=slice(0, P)):
                act.wait_ge(ms_ready, NO[name] + 1)
                st.done(nc.scalar.activation(t_a[rows, :], t_m[rows, :], ACT.Ln))
                nc.scalar.activation(t_exp[rows, :], t_a[rows, :], ACT.Exp, scale=-0.5).then_inc(r0_ready, 1)

            PAIRS = [(2 * j, 2 * j + 2) for j in range(4)]

            def norm(name, last_chunk, free=None, final=False):
                if name == "ffn1":
                    act.wait_ge(x_in, 16)
                    squares(name, h, PAIRS)
                else:
                    squares(name, h, PAIRS, UPD[name] - UPDATES)
                rsqrt(name)
                if last_chunk is not None:
                    nxt(last_chunk)
                if not final:
                    normed_hi(name, free)

            def normed_hi(name, free=None):
                for j in range(4):
                    hi(x_h[:, 2 * j:2 * j + 2, :], x_f[:, 2 * j:2 * j + 2, :], full_ready, FULL[name] + j + 1, free)

            def ffn(name):
                c0, b = C[name], HID[name]

                def hid(slot, value, used=None):
                    act.wait_ge(hid_full, value)
                    if used is not None:
                        act.wait_ge(chunk_used, used)
                    nc.scalar.activation(hid_h[:, slot, :], hid_f[:, slot, :], ACT.Copy).then_inc(hid_hi, 1)

                for f in range(2):
                    act.wait_ge(chunk_used, c0 + f + 1)
                    nc.scalar.activation(t_exp[:, :], bank[:, TURN + f, 0:S], ACT.Sigmoid).then_inc(ffn_sig, 1)
                    hid(f, b + f + 1)
                    nxt(c0 + f)
                c1 = c0 + 2
                with act.Fori(0, FF // 2 - 1) as i:
                    act.wait_ge(chunk_used, i * 3 + (c1 + 1))
                    nc.scalar.activation(t_exp[:, :], bank[:, TURN, 0:S], ACT.Sigmoid).then_inc(ffn_sig, 1)
                    nxt_in(c1, 0, i, 3)
                    hid(0, i * 2 + (b + 3), i * 3 + (c1 + 2))
                    nxt_in(c1, 1, i, 3)
                    act.wait_ge(chunk_used, i * 3 + (c1 + 3))
                    nc.scalar.activation(t_exp[:, :], bank[:, TURN + 1, 0:S], ACT.Sigmoid).then_inc(ffn_sig, 1)
                    hid(1, i * 2 + (b + 4))
                    nxt_in(c1, 2, i, 3)

            def mlp(name):
                c0, b = C[name], HID[name]
                act.wait_ge(hid_full, b + 1)
                nc.scalar.activation(hid_h[:, :, :], hid_f[:, :, :], ACT.Copy).then_inc(hid_hi, 1)
                nxt(c0)

                def body(i):
                    for r in range(3):
                        nxt_in(c0 + 1, 2 * r, i, 6)
                        act.wait_ge(hid_full, i * 3 + (b + r + 2))
                        act.wait_ge(chunk_used, i * 6 + (c0 + 1 + 2 * r + 2))
                        nc.scalar.activation(hid_h[:, :, :], hid_f[:, :, :], ACT.Copy).then_inc(hid_hi, 1)
                        nxt_in(c0 + 1, 2 * r + 1, i, 6)

                turns = (MF - 1) // 3 - 1
                with act.Fori(0, turns) as i:
                    body(i)
                body(turns)

            for c in range(RING):
                split(c, c, 1)
            norm("ffn1", None)
            ffn("ffn1")

            act.wait_ge(rope_ang, 2)
            nc.scalar.activation(rope_tab[64:96, 0, :], rope_tab[64:96, 0, :], ACT.Sin).then_inc(rope_sin, 1)
            nc.scalar.activation(rope_tab[64:96, 1, :], rope_tab[64:96, 1, :], ACT.Sin).then_inc(rope_sin, 1)
            norm("mix", C["latent"] - 1, C["latent"] - 1)
            for j in range(3):
                nxt(C["latent"] + j)
            act.wait_ge(drained, DRAIN["latent"] + 3)
            squares("c_q", lat_raw, [(0, 2), (2, 3)])
            squares("c_kv", lat_raw, [(3, 5)])
            for j in range(4):
                nxt(C["sb_q"] + j)
            rsqrt("c_q")
            hi(y_h[:, 0:2, :], lat_f[:, 0:2, :], full_ready, FULL["c_q"] + 1)
            hi(y_h[:, 2:3, :], lat_f[:, 2:3, :], full_ready, FULL["c_q"] + 2)
            rsqrt("c_kv")
            hi(y_h[:, 3:5, :], lat_f[:, 3:5, :], full_ready, FULL["c_kv"] + 1)
            for j in range(2):
                nxt(C["sb_v"] + j)
            for j in range(8):
                act.wait_ge(chunk_used, C["gates"] + j + 1)
                nc.scalar.activation(gate[:, 2 * j:2 * j + 2, :],
                                     bank[:, TURN + (DRAIN["gates"] + j) % 3, :].rearrange("p (a b) -> p a b", a=2),
                                     ACT.Sigmoid).then_inc(drained, 1)
                nxt(C["gates"] + j)
            for j in range(3):
                nxt(C["q_up"] + j)
            act.wait_ge(qk_raw, 8 + 2)
            for p in range(8):
                dst = sq if p < 4 else x_f
                nc.scalar.activation(dst[0:QK, 2 * (p % 4):2 * (p % 4) + 2, :], heads[0:QK, 2 * p:2 * p + 2, :],
                                     ACT.Square).then_inc(sq_ready, 1)
            rsqrt("head", slice(0, 16))

            def m_front(hd):
                act.wait_ge(m_max, hd + 1)
                for q in range(2):
                    c = slice(0, 128) if q == 0 else slice(128, 384)
                    o = 4 * (hd % 2) + q
                    nc.scalar.activation(m_p[hd % 2][:, c], m_p[hd % 2][:, c], ACT.Exp, scale=float(QK) ** -0.5,
                                         bias=stat[:, 8 + o:9 + o], accum_out=stat[:, 16 + o:17 + o]).then_inc(m_exp, 1)

            for hd in range(HEADS + 1):
                if hd < HEADS:
                    act.wait_ge(s_z, hd + 1)
                    if hd >= 1:
                        act.wait_ge(s_l, hd)
                    nc.scalar.activation(s_t1, bank[:, 1, 0:384], ACT.Abs).then_inc(s_abs, 1)
                    act.wait_ge(s_abs, hd + 1)
                    st.done(nc.scalar.activation(s_t1, s_t1, ACT.Exp, scale=-1.0))
                    nc.scalar.activation(s_t2, s_t1, ACT.Ln, bias=1.0).then_inc(s_ln, 1)
                    m_front(hd)
                if hd >= 1:
                    act.wait_ge(s_x, hd)
                    nc.scalar.activation(s_p[(hd - 1) % 2], s_p[(hd - 1) % 2], ACT.Exp).then_inc(s_a, 1)
            for j in range(2):
                hi(y_h[:, 2 * j:2 * j + 2, :], y_f[:, 2 * j:2 * j + 2, :], full_ready, FULL["o_mla"] + j + 1)
            for j in range(2, 4):
                hi(y_h[:, 2 * j:2 * j + 2, :], y_f[:, 2 * j:2 * j + 2, :], full_ready, FULL["o_mla"] + j + 1)
            for j in range(4):
                nxt(C["branch"] + j)
            for j in range(4):
                hi(x_h[:, 2 * j:2 * j + 2, :], x_f[:, 2 * j:2 * j + 2, :], merged_done, j + 1)
            for j in range(3):
                nxt(C["w_out"] + j)

            norm("ffn2", C["w_out"] + 3, C["w_out"] + 4)
            ffn("ffn2")

            norm("ple", C["ple_gate"] - 1, C["ple_gate"] - 1)
            hi(y_h[:, 0:2, :], heads[:, 0:2, :], p_in, 16)
            for j in range(4):
                act.wait_ge(chunk_used, C["ple_gate"] + j + 1)
                nc.scalar.activation(y_f[:, 2 * j:2 * j + 2, :],
                                     bank[:, ACC + j, :].rearrange("p (a b) -> p a b", a=2),
                                     ACT.Sigmoid).then_inc(ple_sig, 1)
                nxt(C["ple_gate"] + j)

            norm("mix0", C["ple_proj"], C["ple_proj"] + 1)
            with act.Fori(0, 4) as i:
                c0 = C["conv_in"]
                for j in range(2):
                    act.wait_ge(chunk_used, i * 3 + (c0 + j + 1))
                    act.wait_ge(drained, i * 3 + (DRAIN["conv"] + j - (1 if j == 0 else 0)))
                    nc.scalar.activation(t_a[:, :], bank[:, TURN + j, 0:S], ACT.Copy).then_inc(conv_c, 1)
                    nxt_in(c0, j, i, 3)
                act.wait_ge(drained, i * 3 + (DRAIN["conv"] + 3))
                nc.scalar.activation(y_h[:, bass.ds(i * 2, 2), :], y_f[:, bass.ds(i * 2, 2), :], ACT.Copy).then_inc(op_hi, 1)
                nxt_in(c0, 2, i, 3)
            for j in range(3):
                nxt(C["conv_out"] + j)

            norm("mlp0", C["conv_out"] + 3, C["conv_out"])
            mlp("mlp0")

            norm("kv", C["kv_raw"] - 1, C["kv_raw"] - 1)
            for j in range(6):
                nxt(C["kv_raw"] + j)
            hi(y_h.rearrange("p a b -> p (a b)")[:, 0:960], y_flat[:, 0:960], blk_ready, 4)
            hi(y_h.rearrange("p a b -> p (a b)")[:, 960:1920], y_flat[:, 960:1920], blk_ready, 8)
            normed_hi("mix1", C["phi"])
            for j in range(4):
                nxt(C["phi"] + j)
                if j % 2 == 1:
                    nc.scalar.activation(t_exp[:, 0:120], bank[:, SUMS, 0:120], ACT.Sigmoid).then_inc(phi_sig, 1)
                    act.wait_ge(phi_hid, j // 2 + 1)
            for j in range(4):
                nxt(C["nsa_q"] + j)
            act.wait_ge(chunk_used, C["nsa_gate"] + 1)
            nc.scalar.activation(nsa_g[:, :, :], bank[:, SUMS, 0:96].rearrange("p (a b) -> p a b", a=2),
                                 ACT.Sigmoid).then_inc(g_sig, 1)
            nxt(C["nsa_gate"])

            for hd in range(G_HEADS + 1):
                if hd >= 1:
                    o = (hd - 1) % 2
                    act.wait_ge(n_pt, 2 * (hd - 1) + 1)
                    if hd >= 3:
                        act.wait_ge(n_pv, hd - 2)
                    nc.scalar.activation(n_t[o][:, 0:512], bank[:, 6, :], ACT.Copy).then_inc(n_ptc, 1)
                if hd < G_HEADS:
                    act.wait_ge(n_max, hd + 1)
                    pa, pb, o = n_pa[hd % 2], n_pb[hd % 2], 24 * (hd % 2)
                    for k, ap in enumerate((pa[:, 0:256], pa[:, 256:512], pb[:, 0:128], pb[:, 128:256],
                                            pb[:, 256:256 + NVALID0], pb[:, 272:272 + NCMP])):
                        nc.scalar.activation(ap, ap, ACT.Exp, bias=stat[:, o + 6 + k:o + 7 + k],
                                             accum_out=stat[:, o + 12 + k:o + 13 + k]).then_inc(n_exp, 1)
            for j in range(4):
                hi(y_h[:, 2 * j:2 * j + 2, :], y_f[:, 2 * j:2 * j + 2, :], full_ready, FULL["o_nsa"] + j + 1)
            for j in range(3):
                nxt(C["nsa_out"] + j)

            norm("mlp1", C["nsa_out"] + 3, C["nsa_gate"] + 1)
            mlp("mlp1")
            norm("final", None, final=True)

        @block.vector
        def _(dve):
            st = Steps(dve, dve_step)
            V = nc.vector

            def split(s, count):
                dve.wait_ge(hi_split, count)
                V.tensor_tensor(w_lo[:, s, :], raw[:, s, :], w_hi[:, s, :].bitcast(F32), ALU.subtract).then_inc(lo_split, 1)

            def nxt(c):
                if c + RING < N_CHUNKS:
                    split(c % RING, c + RING + 1)

            def nxt_in(c0, j, i, step):
                if isinstance(i, int):
                    nxt(c0 + j + i * step)
                    return
                split((c0 + j) % RING, i * step + (c0 + j + RING + 1))

            made = [0]

            def lo(dst, src, hi_part):
                made[0] += 1
                dve.wait_ge(op_hi, made[0])
                V.tensor_tensor(dst, src, hi_part.bitcast(F32), ALU.subtract).then_inc(op_lo, 1)

            def rsqrt(name, ss, rows=slice(0, P), width=D, r_out=None, last=None):
                dve.wait_ge(ss_ready, NO[name] + 1)
                V.tensor_scalar(t_m[rows, :], ss, 1.0 / width, EPS, ALU.mult, ALU.add).then_inc(ms_ready, 1)
                dve.wait_ge(r0_ready, NO[name] + 1)
                st.done(V.tensor_tensor(t_a[rows, :], t_exp[rows, :], t_exp[rows, :], ALU.mult))
                st.done(V.scalar_tensor_tensor(out=t_a[rows, :], in0=t_a[rows, :], scalar=-0.5, in1=t_m[rows, :],
                                               op0=ALU.mult, op1=ALU.mult))
                ins = V.scalar_tensor_tensor(out=r_out, in0=t_a[rows, :], scalar=1.5, in1=t_exp[rows, :],
                                             op0=ALU.add, op1=ALU.mult)
                if last is None:
                    st.done(ins)
                else:
                    ins.then_inc(last, 1)

            def scaled(name, dst, src, i, done):
                ins = V.scalar_tensor_tensor(out=dst, in0=src, scalar=col(name, i), in1=r_sb[:, :],
                                             op0=ALU.mult, op1=ALU.mult)
                if done is not None:
                    ins.then_inc(done, 1)

            def normed_set(name, free=None):
                def full(j):
                    scaled(name, x_f[:, 2 * j, :], h[:, 2 * j, :], 2 * j, None)
                    scaled(name, x_f[:, 2 * j + 1, :], h[:, 2 * j + 1, :], 2 * j + 1, full_ready)

                def low(j):
                    lo(x_l[:, 2 * j:2 * j + 2, :], x_f[:, 2 * j:2 * j + 2, :], x_h[:, 2 * j:2 * j + 2, :])

                assert made[0] == PC[name]
                full(0)
                full(1)
                low(0)
                full(2)
                low(1)
                full(3)
                low(2)
                low(3)

            def norm(name, last_chunk):
                rsqrt(name, bank[:, SUMS, 0:S], r_out=r_sb[:, :])
                normed_set(name)
                if last_chunk is not None:
                    nxt(last_chunk)

            def update(name, scale, last_chunk):
                for j in range(4):
                    if j < 3 and name in ENDS:
                        dve.wait_ge(acc_ready, ENDS[name] + j + 1)
                    else:
                        dve.wait_ge(chunk_used, last_chunk + 1 if name in ENDS else last_chunk - 3 + j + 1)
                    hj = h[:, 2 * j:2 * j + 2, :]
                    a = bank[:, ACC + j, :].rearrange("p (a b) -> p a b", a=2)
                    V.scalar_tensor_tensor(out=hj, in0=a, scalar=scale, in1=hj, op0=ALU.mult,
                                           op1=ALU.add).then_inc(h_upd, 1)
                    if name not in ENDS and j < 3:
                        nxt(last_chunk - 3 + j)

            def ffn(name):
                c0, b = C[name], HID[name]

                def swiglu(f, count):
                    dve.wait_ge(ffn_sig, count)
                    st.done(V.tensor_tensor(t_a[:, :], bank[:, TURN + f, 0:S], t_exp[:, :], ALU.mult))
                    V.tensor_tensor(hid_f[:, f, :], bank[:, TURN + f, S:2 * S], t_a[:, :], ALU.mult).then_inc(hid_full, 1)

                def hid(f, count):
                    dve.wait_ge(hid_hi, count)
                    V.tensor_tensor(hid_l[:, f, :], hid_f[:, f, :], hid_h[:, f, :].bitcast(F32),
                                    ALU.subtract).then_inc(hid_lo, 1)

                e0 = 0 if name == "ffn1" else FF
                for f in range(2):
                    swiglu(f, e0 + f + 1)
                    hid(f, b + f + 1)
                    nxt(c0 + f)
                c1, n = c0 + 2, st.n
                with dve.Fori(0, FF // 2 - 1) as i:
                    st.n = i * 2 + n
                    swiglu(0, i * 2 + (e0 + 3))
                    nxt_in(c1, 0, i, 3)
                    hid(0, i * 2 + (b + 3))
                    nxt_in(c1, 1, i, 3)
                    swiglu(1, i * 2 + (e0 + 4))
                    hid(1, i * 2 + (b + 4))
                    nxt_in(c1, 2, i, 3)
                st.n = n + 2 * (FF // 2 - 1)
                update(name, 0.5, c0 + FF + FF // 2 - 1)

            def mlp(name):
                c0, b = C[name], HID[name]

                def act_fn(bk, used):
                    dve.wait_ge(chunk_used, used)
                    a = bank[:, TURN + bk, :].rearrange("p (a b) -> p a b", a=2)
                    st.done(V.tensor_scalar(y_f[:, 0:2, :], a, 0.0, None, ALU.max))
                    V.tensor_tensor(hid_f[:, :, :], y_f[:, 0:2, :], y_f[:, 0:2, :], ALU.mult).then_inc(hid_full, 1)

                def hid(count):
                    dve.wait_ge(hid_hi, count)
                    V.tensor_tensor(hid_l[:, :, :], hid_f[:, :, :], hid_h[:, :, :].bitcast(F32),
                                    ALU.subtract).then_inc(hid_lo, 1)

                act_fn(0, c0 + 1)
                hid(b + 1)
                nxt(c0)
                n = st.n

                def body(i):
                    st.n = i * 3 + n
                    for r in range(3):
                        act_fn((r + 1) % 3, i * 6 + (c0 + 2 * r + 2))
                        nxt_in(c0 + 1, 2 * r, i, 6)
                        hid(i * 3 + (b + r + 2))
                        nxt_in(c0 + 1, 2 * r + 1, i, 6)

                turns = (MF - 1) // 3 - 1
                with dve.Fori(0, turns) as i:
                    body(i)
                body(turns)
                st.n = n + (MF - 1)
                update(name, 1.0, c0 + 2 * MF - 1)

            def angles():
                R = slice(64, 96)
                two_pi = 2.0 * np.pi
                c1 = float(np.float32(6.28125))
                rest = two_pi - 6.28125
                c2 = float((np.array([rest], np.float32).view(np.uint32) & np.uint32(0xFFFFF000)).view(np.float32)[0])
                c3 = float(np.float32(rest - c2))
                dve.wait_ge(pos_in, 16)
                dve.wait_ge(con_in, 16)
                st.done(V.tensor_copy(t_a[R, :], pos_i[R, :]))
                st.done(V.tensor_scalar(t_a[R, :], t_a[R, :], con[R, CN["inv_freq"]:CN["inv_freq"] + 1], None, ALU.mult))
                for which, turn in ((1, 0.0), (0, 0.25)):
                    tab = rope_tab[R, which, :]
                    st.done(V.tensor_scalar(t_b[R, :], t_a[R, :], float(1.0 / two_pi), turn, ALU.mult, ALU.add))
                    st.done(V.tensor_scalar(t_b[R, :], t_b[R, :], 12582912.0, None, ALU.add))
                    st.done(V.tensor_scalar(t_b[R, :], t_b[R, :], 12582912.0, None, ALU.subtract))
                    st.done(V.scalar_tensor_tensor(out=tab, in0=t_b[R, :], scalar=-c1, in1=t_a[R, :],
                                                   op0=ALU.mult, op1=ALU.add))
                    st.done(V.scalar_tensor_tensor(out=tab, in0=t_b[R, :], scalar=-c2, in1=tab,
                                                   op0=ALU.mult, op1=ALU.add))
                    st.done(V.scalar_tensor_tensor(out=tab, in0=t_b[R, :], scalar=-c3, in1=tab,
                                                   op0=ALU.mult, op1=ALU.add))
                    if which == 0:
                        st.done(V.tensor_scalar(tab, tab, float(np.pi / 2), None, ALU.add))
                    pi = float(np.nextafter(np.float32(np.pi), np.float32(0)))
                    V.tensor_scalar(tab, tab, pi, -pi, ALU.min, ALU.max).then_inc(rope_ang, 1)

            dve.wait_ge(small_in, 16)
            dve.wait_ge(x_in, 16)
            for c in range(RING):
                split(c, c + 1)
            norm("ffn1", None)
            angles()
            dve.wait_ge(bias_mm, 1)
            V.tensor_copy(bias_1d[:, :], bank[0:16, 6, 0:384]).then_inc(bias_ready, 1)
            ffn("ffn1")

            norm("mix", C["latent"] - 1)
            for j in range(3):
                dve.wait_ge(chunk_used, C["latent"] + j + 1)
                b = bank[:, TURN + j, :].rearrange("p (a b) -> p a b", a=2)
                if j < 2:
                    V.tensor_copy(lat_raw[:, 2 * j:2 * j + 2, :], b).then_inc(drained, 1)
                else:
                    V.tensor_copy(lat_raw[:, 4, :], b[:, 0, :])
                    V.tensor_copy(k_rope[0:ROPE, :], b[0:ROPE, 1, :]).then_inc(drained, 1)
                nxt(C["latent"] + j)
            for j in range(4):
                c = C["sb_q"] + j
                dve.wait_ge(chunk_used, c + 1)
                b = bank[:, TURN + (DRAIN["sb"] + j) % 3, :].rearrange("p (a b) -> p a b", a=2)
                V.tensor_scalar(y_f[:, 2 * j:2 * j + 2, :], b, 0.125 if j < 2 else 1.0, None,
                                ALU.mult).then_inc(drained, 1)
                nxt(c)
            rsqrt("c_q", bank[:, SUMS, 0:S], width=384, r_out=r_sb[:, :])
            for t in range(3):
                scaled("c_q", lat_f[:, t, :], lat_raw[:, t, :], t, full_ready if t > 0 else None)
            lo(y_l[:, 0:2, :], lat_f[:, 0:2, :], y_h[:, 0:2, :])
            lo(y_l[:, 2:3, :], lat_f[:, 2:3, :], y_h[:, 2:3, :])
            rsqrt("c_kv", bank[:, 3, 0:S], width=256, r_out=r_sb[:, :])
            for t in range(2):
                scaled("c_kv", lat_f[:, 3 + t, :], lat_raw[:, 3 + t, :], t, full_ready if t > 0 else None)
            lo(y_l[:, 3:5, :], lat_f[:, 3:5, :], y_h[:, 3:5, :])
            for j in range(2):
                nxt(C["sb_v"] + j)
            dve.wait_ge(chunk_used, C["sb_v"] + 2)
            for t in range(2):
                V.tensor_copy(sv[:, t, :], bank[:, t, :]).then_inc(sv_done, 1)
            for j in range(8):
                nxt(C["gates"] + j)
            for j in range(2):
                dve.wait_ge(chunk_used, C["q_up"] + j + 1)
                for t in range(2):
                    b = bank[0:QK, 2 * j + t, :].rearrange("p (a b) -> p a b", a=2)
                    hd = 4 * j + 2 * t
                    V.tensor_copy(heads[0:QK, hd:hd + 2, :], b).then_inc(qk_raw, 1)
                nxt(C["q_up"] + j)
            dve.wait_ge(chunk_used, C["kv_up"] + 1)
            V.tensor_copy(heads[64:96, 8:16, :], k_rope[0:ROPE, :].rearrange("p (a b) -> p a b", a=1).to_broadcast([ROPE, 8, S])).then_inc(qk_raw, 1)
            for t in range(2):
                b = bank[:, 4 + t, :].rearrange("p (a b) -> p a b", a=2)
                for e in range(2):
                    k = heads[0:NOPE, 8 + 4 * t + e:8 + 4 * t + e + 3:2, :]
                    V.tensor_copy(k, b[64 * e:64 * e + 64]).then_inc(qk_raw, 1)
            for t in range(2):
                ins = V.tensor_copy(mv[:, t, :], bank[:, 6 + t, :])
                if t == 1:
                    ins.then_inc(qk_raw, 1)
            nxt(C["kv_up"])
            dve.wait_ge(ss_ready, NO["head"] + 1)
            rsqrt("head", bank[0:16, 0, 0:S], slice(0, 16), QK, r_sb[0:16, :], r_head)

            def rope(p):
                y = heads[64:96, 2 * p:2 * p + 2, :]
                dve.wait_ge(rot_ready, p + 1)
                if p >= 1:
                    dve.wait_ge(roped, p)
                b = bank[64:96, p, :].rearrange("p (a b) -> p a b", a=2)
                sin = rope_tab[64:96, 1:2, :].to_broadcast([32, 2, S])
                st.done(V.tensor_tensor(hid_f[64:96, :, :], b, sin, ALU.mult))
                dve.wait_ge(rope_cos, p + 1)
                V.tensor_tensor(y, hid_f[64:96, :, :], v_pad[64:96, :, 0:S], ALU.add).then_inc(roped, 1)

            dve.wait_ge(rope_sin, 2)
            for p in range(8):
                dve.wait_ge(bc_ready, p + 1)
                b = bank[0:QK, p, :].rearrange("p (a b) -> p a b", a=2)
                y = heads[0:QK, 2 * p:2 * p + 2, :]
                V.scalar_tensor_tensor(out=y, in0=y, scalar=col("q_head" if p < 4 else "k_head")[0:QK], in1=b,
                                       op0=ALU.mult, op1=ALU.mult).then_inc(normed, 1)
                if p >= 1:
                    rope(p - 1)
            rope(7)

            for hd in range(HEADS + 1):
                o = 4 * (hd % 2)
                if hd < HEADS:
                    dve.wait_ge(s_z, hd + 1)
                    dve.wait_ge(s_abs, hd + 1)
                    V.tensor_scalar(s_m, bank[:, 1, 0:384], -1.0, 0.0, ALU.mult, ALU.min).then_inc(s_min, 1)
                    dve.wait_ge(m_scores, hd + 1)
                    mp = m_p[hd % 2]
                    if hd >= 2:
                        dve.wait_ge(m_pt, hd - 1)
                    for q in range(2):
                        c = slice(0, 128) if q == 0 else slice(128, 384)
                        neg = cst("mla_neg", 128, 128) if q == 0 else cst("mla_neg", 256)
                        st.inc(V.tensor_tensor_reduce(mp[:, c], bank[:, 0, c], neg, 1.0, -3e38, ALU.add, ALU.max,
                                                      stat[:, o + q:o + q + 1]))
                    st.wait()
                    V.tensor_scalar(stat[:, 8 + o:10 + o], stat[:, o:o + 2], -float(QK) ** -0.5, None,
                                    ALU.mult).then_inc(m_max, 1)
                if hd >= 1:
                    dve.wait_ge(s_e, hd)
                    if hd >= 3:
                        dve.wait_ge(s_pv, hd - 2)
                    V.tensor_tensor(s_p[(hd - 1) % 2], bank[:, 3, 0:384], cst("sb_neg", 384), ALU.add).then_inc(s_x, 1)
                    dve.wait_ge(m_pt, hd)
                    if hd >= 3:
                        dve.wait_ge(m_pv, 2 * (hd - 2))
                    V.tensor_copy(m_t[(hd - 1) % 2], bank[:, 2, 0:384]).then_inc(m_ptc, 1)
                if hd < HEADS:
                    dve.wait_ge(s_ln, hd + 1)
                    dve.wait_ge(s_min, hd + 1)
                    if hd >= 1:
                        dve.wait_ge(s_e, hd)
                    st.done(V.tensor_tensor(s_lm, s_m, s_t2, ALU.subtract))
                    lm = s_lm.rearrange("p (a b) -> p a b", a=3)[:, 0:3:2, :]
                    one = con[:, CN["tri"]:CN["tri"] + P].rearrange("p (a b) -> p a b", a=1).to_broadcast([P, 2, P])
                    st.done(V.tensor_tensor(s_m.rearrange("p (a b) -> p a b", a=3)[:, 0:3:2, :], lm, one, ALU.mult))
                    V.tensor_tensor(lm, lm, s_m.rearrange("p (a b) -> p a b", a=3)[:, 0:3:2, :],
                                    ALU.subtract).then_inc(s_l, 1)
                    dve.wait_ge(m_exp, 2 * hd + 2)
                    st.done(V.reciprocal(stat[:, 24 + o:26 + o], stat[:, 16 + o:18 + o]))
                    V.tensor_scalar(mp[:, 0:128], mp[:, 0:128], stat[:, 24 + o:25 + o], None, ALU.mult)
                    V.tensor_scalar(mp[:, 128:384], mp[:, 128:384], stat[:, 25 + o:26 + o], None,
                                    ALU.mult).then_inc(m_prob, 1)
            dve.wait_ge(m_pv, 2 * HEADS)
            dve.wait_ge(s_pv, HEADS)
            for j in range(4):
                V.tensor_copy(y_f[:, 2 * j:2 * j + 2, :],
                              bank[:, 4 + j, :].rearrange("p (a b) -> p a b", a=2)).then_inc(full_ready, 1)
            for j in range(4):
                lo(y_l[:, 2 * j:2 * j + 2, :], y_f[:, 2 * j:2 * j + 2, :], y_h[:, 2 * j:2 * j + 2, :])
            dve.wait_ge(drained, DRAIN["gates"] + 8)
            for half in range(2):
                for t in range(2):
                    m = 4 - 4 * half + t
                    j = 2 * half + t
                    dve.wait_ge(chunk_used, C["branch"] + 2 * half + 1)
                    bm = bank[:, m, :].rearrange("p (a b) -> p a b", a=2)
                    bs = bank[:, m + 2, :].rearrange("p (a b) -> p a b", a=2)
                    if j >= 1:
                        dve.wait_ge(merged_done, j)
                    st.done(V.tensor_tensor(hid_f[:, :, :], bm, gate[:, 2 * j:2 * j + 2, :], ALU.mult))
                    dve.wait_ge(chunk_used, C["branch"] + 2 * half + 2)
                    st.done(V.tensor_tensor(sq[:, 0:2, :], bs, gate[:, 8 + 2 * j:10 + 2 * j, :], ALU.mult))
                    V.tensor_tensor(x_f[:, 2 * j:2 * j + 2, :], hid_f[:, :, :], sq[:, 0:2, :],
                                    ALU.add).then_inc(merged_done, 1)
                for j in range(2 * half, 2 * half + 2):
                    nxt(C["branch"] + j)
            for j in range(4):
                lo(x_l[:, 2 * j:2 * j + 2, :], x_f[:, 2 * j:2 * j + 2, :], x_h[:, 2 * j:2 * j + 2, :])
            update("w_out", 1.0, C["w_out"] + 3)

            norm("ffn2", C["w_out"] + 3)
            ffn("ffn2")

            norm("ple", C["ple_gate"] - 1)
            lo(y_l[:, 0:2, :], heads[:, 0:2, :], y_h[:, 0:2, :])
            for j in range(4):
                y = y_f[:, 2 * j:2 * j + 2, :]
                nxt(C["ple_gate"] + j)
            dve.wait_ge(chunk_used, C["ple_proj"] + 1)
            dve.wait_ge(ple_sig, 4)
            for j in range(4):
                y, hj = y_f[:, 2 * j:2 * j + 2, :], h[:, 2 * j:2 * j + 2, :]
                st.done(V.tensor_tensor(y, bank[:, 4 + j, :].rearrange("p (a b) -> p a b", a=2), y, ALU.mult))
                V.tensor_tensor(hj, hj, y, ALU.add).then_inc(h_upd, 1)

            def unflip(half):
                for m in range(4):
                    dve.wait_ge(flipped, 4 * half + m + 1)
                    t = 2 * (4 * half + m)
                    V.tensor_copy(gate_or_bias[:, t:t + 2, :],
                                  bank[:, m, :].rearrange("p (a b) -> p a b", a=2)).then_inc(unflipped, 1)

            norm("mix0", C["ple_proj"])
            unflip(0)
            n = st.n
            dve.wait_ge(setup, 6)
            with dve.Fori(0, 4) as i:
                c0 = C["conv_in"]
                st.n = i * 6 + n
                for j in range(2):
                    dve.wait_ge(conv_c, i * 2 + (j + 1))
                    V.tensor_tensor(v_pad[:, j, 2:S + 2], t_a[:, :], bank[:, TURN + j, S:2 * S],
                                    ALU.mult).then_inc(drained, 1)
                    nxt_in(c0, j, i, 3)
                dve.wait_ge(chunk_used, i * 3 + (c0 + 3))
                dve.wait_ge(drained, i * 3 + (DRAIN["conv"] + 2))
                for k in range(3):
                    tap = 2 - k
                    for j in range(2):
                        w = par[:, bass.ds(i * 2 + (SM["conv_w"] + 8 * tap + j), 1)]
                        src = v_pad[:, j, tap:tap + S]
                        if k == 0:
                            st.inc(V.tensor_scalar(hid_f[:, j, :], src, w, None, ALU.mult))
                        else:
                            st.inc(V.scalar_tensor_tensor(out=hid_f[:, j, :], in0=src, scalar=w, in1=hid_f[:, j, :],
                                                          op0=ALU.mult, op1=ALU.add))
                    st.wait()
                V.tensor_tensor(y_f[:, bass.ds(i * 2, 2), :], bank[:, TURN + 2, :].rearrange("p (a b) -> p a b", a=2),
                                hid_f[:, :, :], ALU.mult).then_inc(drained, 1)
                dve.wait_ge(op_hi, i * 1 + (PC["conv"] + 1))
                V.tensor_tensor(y_l[:, bass.ds(i * 2, 2), :], y_f[:, bass.ds(i * 2, 2), :],
                                y_h[:, bass.ds(i * 2, 2), :].bitcast(F32), ALU.subtract).then_inc(op_lo, 1)
                nxt_in(c0, 2, i, 3)
            st.n = n + 24
            made[0] += 4
            unflip(1)
            update("conv_out", 1.0, C["conv_out"] + 3)

            norm("mlp0", C["conv_out"] + 3)
            mlp("mlp0")

            norm("kv", C["kv_raw"] - 1)
            for w in range(2):
                dve.wait_ge(chunk_used, C["kv_raw"] + w + 1)
                b = bank[:, TURN + w, :]
                pe = col("pe_k" if w == 0 else "pe_v", 0, 16)
                for half in range(2):
                    for e in range(2):
                        rows = slice(64 * half, 64 * half + 64)
                        src = b[64 * e:64 * e + 64, :].rearrange("p (a n l) -> p l a n", a=2, l=16)
                        dst = y_flat[rows, 960 * w:960 * w + 960].rearrange("p (l g n) -> p l g n", l=16, g=4)
                        for t in range(2):
                            ins = V.tensor_tensor(dst[:, :, 2 * t + e, :], src[:, :, t, half:half + NCMP],
                                                  pe[rows, :].rearrange("p (l n) -> p l n", n=1).to_broadcast([64, 16, NCMP]),
                                                  ALU.add)
                        ins.then_inc(blk_ready, 1)
                nxt(C["kv_raw"] + w)
            for w in range(2):
                dve.wait_ge(chunk_used, C["k_att"] + w + 1)
                V.tensor_copy((n_ks, n_kw)[w], bank[:, (6, 0)[w], :].rearrange("p (a b) -> p a b", a=2)).then_inc(kv_done, 1)
                nxt(C["k_att"] + w)
            for w in range(2):
                dve.wait_ge(chunk_used, C["v_att"] + w + 1)
                V.tensor_copy((n_vs, n_vw)[w], bank[:, (1, 2)[w], :].rearrange("p (a b) -> p a b", a=2)).then_inc(kv_done, 1)
                nxt(C["v_att"] + w)
            y_hf, y_lf = (t[:, :, :].rearrange("p a b -> p (a b)") for t in (y_h, y_l))
            lo(y_lf[:, 0:960], y_flat[:, 0:960], y_hf[:, 0:960])
            lo(y_lf[:, 960:1920], y_flat[:, 960:1920], y_hf[:, 960:1920])
            normed_set("mix1")
            for w in range(2):
                nxt(C["phi"] + 2 * w)
                nxt(C["phi"] + 2 * w + 1)
                dve.wait_ge(phi_sig, w + 1)
                V.tensor_tensor(cmp_hid[:, w, :, :], bank[:, SUMS, 0:120].rearrange("p (a b) -> p a b", a=2),
                                t_exp[:, 0:120].rearrange("p (a b) -> p a b", a=2), ALU.mult).then_inc(phi_hid, 1)
            dve.wait_ge(phi_mm, 1)
            V.tensor_copy(k_cmp[:, :, 0:NCMP], bank[:, 3, 0:32].rearrange("p (a b) -> p a b", a=2)[:, :, 0:NCMP]).then_inc(cmp_done, 1)
            V.tensor_copy(v_cmp[0:NCMP, :], bank[0:NCMP, 3, 64:320]).then_inc(cmp_done, 1)
            for j in range(4):
                dve.wait_ge(chunk_used, C["nsa_q"] + j + 1)
                V.tensor_scalar(n_q[:, 2 * j:2 * j + 2, :], bank[:, TURN + j % 3, :].rearrange("p (a b) -> p a b", a=2),
                                0.125, None, ALU.mult).then_inc(q_done, 1)
                nxt(C["nsa_q"] + j)
            dve.wait_ge(g_sig, 1)
            g0 = nsa_g[:, 0, 0:48:3]
            st.done(V.tensor_scalar(g0, g0, cst("has_any", 1), None, ALU.mult))
            for o in range(2):
                st.done(V.memset(n_pb[o][:, 256 + NVALID0:272], 0.0))
            nxt(C["nsa_gate"])

            for k in range(G_HEADS + 1):
                o = 24 * (k % 2)
                if k < G_HEADS:
                    head = NSA_ORDER[k]
                    bias = gate_or_bias[:, head, :]
                    pa, pb = n_pa[k % 2], n_pb[k % 2]
                    dve.wait_ge(n_scores, k + 1)
                    if k >= 2:
                        dve.wait_ge(n_pt, 2 * (k - 1))
                    a, b = bank[:, 4, :], bank[:, 5, :]
                    for m, (dst, src, bs) in enumerate((
                            (pa[:, 0:256], a[:, 0:256], bias), (pa[:, 256:512], a[:, 256:512], bias),
                            (pb[:, 0:128], b[:, 0:128], bias[:, 128:256]), (pb[:, 128:256], b[:, 128:256], bias[:, 128:256]),
                            (pb[:, 256:256 + NVALID0], b[:, 256:256 + NVALID0], bias[:, 159:256:16]),
                            (pb[:, 272:272 + NCMP], b[:, 272:272 + NCMP], bias[:, 31:256:16]))):
                        st.inc(V.tensor_tensor_reduce(dst, src, bs, 1.0, -3e38, ALU.add, ALU.max,
                                                      stat[:, o + m:o + m + 1]))
                    st.wait()
                    V.tensor_scalar(stat[:, o + 6:o + 12], stat[:, o:o + 6], -1.0, None, ALU.mult).then_inc(n_max, 1)
                if k >= 1:
                    dve.wait_ge(n_pt, 2 * k)
                    if k >= 3:
                        dve.wait_ge(n_pv, k - 2)
                    V.tensor_copy(n_t[(k - 1) % 2][:, 512:768], bank[:, 7, 0:256])
                    V.tensor_copy(n_t[(k - 1) % 2][0:NCMP, 768:1024], bank[0:NCMP, 7, 256:512]).then_inc(n_ptd, 1)
                if k < G_HEADS:
                    dve.wait_ge(n_exp, 6 * k + 6)
                    st.done(V.reciprocal(stat[:, o + 18:o + 24], stat[:, o + 12:o + 18]))
                    for m, (q, branch) in enumerate(((1, 1), (1, 2), (0, 1), (0, 2), (0, 0), (1, 0))):
                        gcol = nsa_g[:, q, 3 * head + branch:3 * head + branch + 1]
                        ap = (pa[:, 0:256], pa[:, 256:512], pb[:, 0:128], pb[:, 128:256],
                              pb[:, 256:256 + NVALID0], pb[:, 272:272 + NCMP])[m]
                        ins = V.tensor_scalar(ap, ap, stat[:, o + 18 + m:o + 19 + m], gcol, ALU.mult, ALU.mult)
                    ins.then_inc(n_prob, 1)
            dve.wait_ge(n_pv, G_HEADS)
            for j in range(4):
                V.tensor_copy(y_f[:, 2 * j:2 * j + 2, :],
                              bank[:, j, :].rearrange("p (a b) -> p a b", a=2)).then_inc(full_ready, 1)
            for j in range(4):
                lo(y_l[:, 2 * j:2 * j + 2, :], y_f[:, 2 * j:2 * j + 2, :], y_h[:, 2 * j:2 * j + 2, :])
            update("nsa_out", 1.0, C["nsa_out"] + 3)

            norm("mlp1", C["nsa_out"] + 3)
            mlp("mlp1")
            rsqrt("final", bank[:, SUMS, 0:S], r_out=r_sb[:, :])
            for t in range(KT):
                scaled("final", x_f[:, t, :], h[:, t, :], t, y_ready if t % 2 else None)

        @block.tensor
        def _(pe):
            mm = nc.tensor.matmul

            def product(out_, s, c, m, hi_, lo_, start, stop, **kw):
                mm(out_, w_hi[:, s, c:c + m], hi_, start=start, stop=False, **kw)
                mm(out_, w_hi[:, s, c:c + m], lo_, start=False, stop=False, **kw)
                return mm(out_, w_lo[:, s, c:c + m], hi_, start=False, stop=stop, **kw)

            def arrived(count):
                pe.wait_ge(lo_split, count)

            def pair(s, bk, hi_, lo_, pieces=None, kt=KT):
                for t in range(2):
                    for k in range(kt):
                        if pieces is not None and t == 0 and k % 2 == 0:
                            pe.wait_ge(op_lo, pieces + k // 2 + 1)
                        last = product(bank[:, bk, t * S:(t + 1) * S], s, k * 256 + t * P, P, hi_[:, k, :],
                                       lo_[:, k, :], k == 0, k == kt - 1)
                return last

            def tokens(s, bk, width, kts, hi_, lo_, base, first, last_):
                for t in range(2):
                    for n, k in enumerate(kts):
                        tok = slice(t * P, t * P + P)
                        c = base + n * width if isinstance(base, int) else base[n]
                        o = bk(t)
                        a, b = hi_[:, k, tok], lo_[:, k, tok]
                        wh, wl = w_hi[:, s, c:c + width], w_lo[:, s, c:c + width]
                        kw = dict(skip_group_check=True)
                        mm(o, a, wh, start=first and n == 0, stop=False, **kw)
                        mm(o, a, wl, start=False, stop=False, **kw)
                        ins = mm(o, b, wh, start=False, stop=last_ and n == len(kts) - 1, **kw)
                return ins

            def sum_squares(name, pieces, bk=SUMS):
                n, at = sum(b - a for a, b in pieces), 0
                for j, (a, b) in enumerate(pieces):
                    pe.wait_ge(sq_ready, SQ[name] + j + 1)
                    for t in range(a, b):
                        ins = mm(bank[:, bk, 0:S], ones[:, :], sq[:, t, :], start=at == 0, stop=at == n - 1)
                        at += 1
                ins.then_inc(ss_ready, 1)

            PAIRS = [(2 * j, 2 * j + 2) for j in range(4)]

            def clear_acc():
                for j in range(4):
                    mm(bank[:, ACC + j, :], zeros[:, 0:P], zeros[:, :], start=True, stop=True)

            def down(s, last=False):
                for o in range(KT):
                    for f in range(2):
                        ins = product(bank[:, ACC + o // 2, (o % 2) * S:(o % 2) * S + S], s, f * D + o * P, P,
                                      hid_h[:, f, :], hid_l[:, f, :], False, last, skip_group_check=True)
                    if last and o in (1, 3, 5):
                        ins.then_inc(acc_ready, 1)
                ins.then_inc(chunk_used, 1)

            def ffn(name, piece):
                c0, b = C[name], HID[name]
                if name == "ffn2":
                    pe.wait_ge(h_upd, UPD[name])
                clear_acc()
                for f in range(2):
                    arrived(c0 + f + 1)
                    pair((c0 + f) % RING, TURN + f, x_h, x_l, piece if f == 0 else None).then_inc(chunk_used, 1)
                c1 = c0 + 2
                with pe.Fori(0, FF // 2 - 1) as i:
                    for f in range(2):
                        arrived(i * 3 + (c1 + 2 * f + 1))
                        pe.wait_ge(hid_full, i * 2 + (b + f + 1))
                        pair((c1 + 2 * f) % RING, TURN + f, x_h, x_l).then_inc(chunk_used, 1)
                        if f == 0:
                            arrived(i * 3 + (c1 + 2))
                            pe.wait_ge(hid_lo, i * 2 + (b + 2))
                            down((c1 + 1) % RING)
                last = c0 + FF + FF // 2 - 1
                arrived(last + 1)
                pe.wait_ge(hid_lo, b + FF)
                down(last % RING, True)

            def mlp(name, piece):
                c0, b = C[name], HID[name]
                pe.wait_ge(h_upd, UPD[name])
                clear_acc()
                arrived(c0 + 1)
                pair(c0 % RING, TURN, x_h, x_l, piece).then_inc(chunk_used, 1)
                with pe.Fori(0, (MF - 1) // 3) as i:
                    for r in range(3):
                        c = c0 + 1 + 2 * r
                        arrived(i * 6 + (c + 1))
                        pe.wait_ge(hid_full, i * 3 + (b + r - 1))
                        pair(c % RING, TURN + (r + 1) % 3, x_h, x_l).then_inc(chunk_used, 1)
                        arrived(i * 6 + (c + 2))
                        pe.wait_ge(hid_lo, i * 3 + (b + r + 1))
                        down((c + 1) % RING)
                last = c0 + 2 * MF - 1
                arrived(last + 1)
                pe.wait_ge(hid_lo, b + MF)
                down(last % RING, True)

            def project(name, banks, hi_, lo_, piece, waits=None):
                for j, bk in enumerate(banks):
                    c = C[name] + j
                    arrived(c + 1)
                    if waits is not None and waits[j] is not None:
                        pe.wait_ge(drained, waits[j])
                    pair(c % RING, bk, hi_, lo_, piece if j == 0 else None).then_inc(chunk_used, 1)

            pe.wait_ge(setup, 5)
            sum_squares("ffn1", PAIRS)
            pe.wait_ge(con_in, 16)
            pe.wait_ge(relb_in, 16)
            mm(bank[0:16, 6, 0:384], relb[:, :], con[0:33, CN["bucket"]:CN["bucket"] + 384], start=True,
               stop=True).then_inc(bias_mm, 1)
            ffn("ffn1", PC["ffn1"])

            sum_squares("mix", PAIRS)
            project("latent", [TURN, TURN + 1, TURN + 2], x_h, x_l, PC["mix"])
            project("sb_q", [TURN, TURN + 1], x_h, x_l, None, [1, 2])
            project("sb_k", [TURN + 2, TURN], x_h, x_l, None, [3, 4])
            sum_squares("c_q", [(0, 2), (2, 3)])
            sum_squares("c_kv", [(3, 5)], 3)
            for j in range(2):
                arrived(C["sb_v"] + j + 1)
                tokens((C["sb_v"] + j) % RING, lambda t: bank[:, t, :], 512, range(4 * j, 4 * j + 4), x_h, x_l, 0,
                       j == 0, j == 1).then_inc(chunk_used, 1)
            project("gates", [TURN + (DRAIN["gates"] + j) % 3 for j in range(8)], x_h, x_l, None,
                    [DRAIN["gates"] + j - 2 for j in range(8)])
            pe.wait_ge(sv_done, 2)
            for j in range(2):
                arrived(C["q_up"] + j + 1)
                pe.wait_ge(op_lo, PC["c_q"] + 2)
                s = (C["q_up"] + j) % RING
                for hh in range(4):
                    o = bank[0:QK, 2 * j + hh // 2, (hh % 2) * S:(hh % 2) * S + S]
                    for k in range(3):
                        last = product(o, s, k * 384 + hh * QK, QK, y_h[:, k, :], y_l[:, k, :], k == 0, k == 2)
                last.then_inc(chunk_used, 1)
            arrived(C["kv_up"] + 1)
            pe.wait_ge(op_lo, PC["c_kv"] + 1)
            pe.wait_ge(drained, DRAIN["gates"] + 8)
            s = C["kv_up"] % RING
            for t in range(4):
                for k in range(2):
                    product(bank[:, 4 + t // 2, (t % 2) * S:(t % 2) * S + S], s, k * D + t * P, P, y_h[:, 3 + k, :],
                            y_l[:, 3 + k, :], k == 0, k == 1)
            tokens(s, lambda t: bank[:, 6 + t, :], 512, (3, 4), y_h, y_l, [512, D + 512], True,
                   True).then_inc(chunk_used, 1)

            pe.wait_ge(qk_raw, 10)
            for hd in range(16):
                p = hd // 2
                pe.wait_ge(sq_ready, SQ["head"] + p + 1)
                src = (sq if p < 4 else x_f)[0:QK, 2 * (p % 4) + hd % 2, :]
                pick = con[0:QK, CN["pick"] + 15 - hd:CN["pick"] + 31 - hd]
                ins = mm(bank[0:16, 0, 0:S], pick, src, start=hd == 0, stop=hd == 15)
            ins.then_inc(ss_ready, 1)
            pe.wait_ge(r_head, 1)

            def rotate(p):
                pe.wait_ge(normed, p + 1)
                mm(bank[64:96, p, :], con[64:96, CN["rot"]:CN["rot"] + 32],
                   heads[64:96, 2 * p:2 * p + 2, :].rearrange("p a b -> p (a b)"), start=True,
                   stop=True).then_inc(rot_ready, 1)

            for p in range(8):
                for e in range(2):
                    hd = 2 * p + e
                    row = con[0:16, CN["ident"] + hd:CN["ident"] + hd + 1].to_broadcast([16, QK])
                    ins = mm(bank[0:QK, p, e * S:e * S + S], row, r_sb[0:16, :], start=True, stop=True)
                ins.then_inc(bc_ready, 1)
                if p >= 1:
                    rotate(p - 1)
            rotate(7)

            pe.wait_ge(roped, 8)
            for hd in range(HEADS + 1):
                if hd < HEADS:
                    if hd >= 1:
                        pe.wait_ge(m_max, hd)
                    q, k = heads[0:QK, hd, :], heads[0:QK, 8 + hd, :]
                    mm(bank[:, 0, 0:128], q[:, 0:128], k[:, 0:128], start=True, stop=True)
                    mm(bank[:, 0, 128:384], q[:, 128:256], k, start=True, stop=True).then_inc(m_scores, 1)
                    if hd >= 1:
                        pe.wait_ge(s_min, hd)
                    r = slice(64 * (hd % 2), 64 * (hd % 2) + 64)
                    q, k = sb_q[r, hd // 2, :], sb_k[r, hd // 2, :]
                    mm(bank[:, 1, 0:256], k[:, 0:128], q, start=True, stop=True)
                    mm(bank[:, 1, 256:384], k[:, 128:256], q[:, 128:256], start=True, stop=True).then_inc(s_z, 1)
                if hd >= 1:
                    g = hd - 1
                    r = slice(64 * (g % 2), 64 * (g % 2) + 64)
                    q, k = sb_q[r, g // 2, :], sb_k[r, g // 2, :]
                    if g >= 1:
                        pe.wait_ge(s_x, g)
                        pe.wait_ge(m_ptc, g)
                    pe.wait_ge(s_l, g + 1)
                    e = bank[:, 3, :]
                    kw = dict(skip_group_check=True)
                    mm(e[:, 0:256], k[:, 0:128], q, start=True, stop=False, **kw)
                    mm(e[:, 256:384], k[:, 128:256], q[:, 128:256], start=False, stop=False, **kw)
                    mm(e[:, 0:384], cst("tri", P), s_lm, start=False, stop=False, **kw)
                    mm(e[:, 128:256], ones[:, :], s_lm[:, 256:384], start=False, stop=True, **kw).then_inc(s_e, 1)
                    pe.wait_ge(m_prob, g + 1)
                    mp, b2 = m_p[g % 2], bank[:, 2, :]
                    for blk in range(3):
                        ins = nc.tensor.transpose(b2[:, blk * P:blk * P + P], mp[:, blk * P:blk * P + P], ident)
                    ins.then_inc(m_pt, 1)
                    cols = slice(g * 64, g * 64 + 64)
                    oc = (g // 2 % 2) * S
                    pe.wait_ge(m_ptc, g + 1)
                    om, mt = bank[r, 4 + g // 4, oc:oc + S], m_t[g % 2]
                    mm(om, mv[:, 0, cols], mt[:, 0:256], start=True, stop=False).then_inc(m_pv, 1)
                    mm(om[:, 128:256], mv[:, 1, cols], mt[:, 256:384], start=False, stop=True).then_inc(m_pv, 1)
                    pe.wait_ge(s_a, g + 1)
                    os, sp_ = bank[r, 6 + g // 4, oc:oc + S], s_p[g % 2]
                    mm(os, sv[:, 0, cols], sp_[:, 0:256], start=True, stop=False)
                    mm(os[:, 128:256], sv[:, 1, cols], sp_[:, 256:384], start=False, stop=True).then_inc(s_pv, 1)

            for half in range(2):
                for w in range(2):
                    c = C["branch"] + 2 * half + w
                    arrived(c + 1)
                    pe.wait_ge(op_lo, PC["o_mla"] + 4)
                    for o in range(4):
                        dst = bank[:, 4 - 4 * half + 2 * w + o // 2, (o % 2) * S:(o % 2) * S + S]
                        for k in range(4):
                            last = product(dst, c % RING, k * 512 + o * P, P, y_h[:, 4 * w + k, :],
                                           y_l[:, 4 * w + k, :], k == 0, k == 3)
                    last.then_inc(chunk_used, 1)
            pe.wait_ge(merged_done, 4)
            project("w_out", range(4), x_h, x_l, PC["merged"])

            sum_squares("ffn2", PAIRS)
            ffn("ffn2", PC["ffn2"])

            sum_squares("ple", PAIRS)
            project("ple_gate", range(4), x_h, x_l, PC["ple"])
            arrived(C["ple_proj"] + 1)
            pe.wait_ge(op_lo, PC["p"] + 1)
            for o in range(KT):
                for k in range(2):
                    last = product(bank[:, 4 + o // 2, (o % 2) * S:(o % 2) * S + S], C["ple_proj"] % RING,
                                   k * D + o * P, P, y_h[:, k, :], y_l[:, k, :], k == 0, k == 1)
            last.then_inc(chunk_used, 1)

            def flip(half):
                for m in range(4):
                    t = 2 * (4 * half + m)
                    mm(bank[:, m, :], cst("flip", P), gate_or_bias[:, t:t + 2, :].rearrange("p a b -> p (a b)"),
                       start=True, stop=True).then_inc(flipped, 1)

            pe.wait_ge(h_upd, UPD["mix0"])
            sum_squares("mix0", PAIRS)
            pe.wait_ge(bias_in, 16)
            flip(0)
            for p in range(4):
                pe.wait_ge(op_lo, PC["mix0"] + p + 1)
            with pe.Fori(0, 4) as i:
                for j in range(3):
                    c = C["conv_in"] + j
                    arrived(i * 3 + (c + 1))
                    pe.wait_ge(drained, i * 3 + (DRAIN["conv"] + j - 2))
                    pair(c % RING, TURN + j, x_h, x_l).then_inc(chunk_used, 1)
            pe.wait_ge(unflipped, 4)
            flip(1)
            pe.wait_ge(unflipped, 8)
            project("conv_out", range(4), y_h, y_l, PC["conv"])
            sum_squares("mlp0", PAIRS)
            mlp("mlp0", PC["mlp0"])

            sum_squares("kv", PAIRS)
            project("kv_raw", [TURN, TURN + 1], x_h, x_l, PC["kv"])
            project("k_att", [6, 0], x_h, x_l, None)
            for w in range(2):
                c = C["v_att"] + w
                arrived(c + 1)
                tokens(c % RING, lambda t: bank[:, 1 + w, t * 256:t * 256 + 256], 256, range(KT), x_h, x_l, 0, True,
                       True).then_inc(chunk_used, 1)
            y_hf, y_lf = (t[:, :, :].rearrange("p a b -> p (a b)") for t in (y_h, y_l))
            for w in range(2):
                for half in range(2):
                    c = C["phi"] + 2 * w + half
                    arrived(c + 1)
                    pe.wait_ge(op_lo, PC["blk_k"] + w + 1)
                    if w == 1:
                        pe.wait_ge(phi_hid, 1)
                    for ht in range(2):
                        for l in range(8):
                            a = 960 * w + (8 * half + l) * 60
                            last = product(bank[:, SUMS, ht * 60:ht * 60 + 60], c % RING, l * 256 + ht * P, P,
                                           y_hf[:, a:a + 60], y_lf[:, a:a + 60], half == 0 and ht == 0 and l == 0,
                                           half == 1 and l == 7, skip_group_check=True)
                    last.then_inc(chunk_used, 1)
            pe.wait_ge(phi_hid, 2)
            kw = dict(skip_group_check=True)
            for g in range(4):
                e = g % 2
                for k in range(2):
                    mm(bank[64 * e:64 * e + 64, 3, (g // 2) * 16:(g // 2) * 16 + NCMP],
                       col("phi_k2", k * 64, 64), cmp_hid[:, 0, k, g * NCMP:(g + 1) * NCMP],
                       start=k == 0, stop=k == 1, **kw)
            for g in range(4):
                for k in range(2):
                    ins = mm(bank[0:NCMP, 3, 64 + g * 64:128 + g * 64], cmp_hid[:, 1, k, g * NCMP:(g + 1) * NCMP],
                             col("phi_v2", k * 64, 64), start=k == 0, stop=k == 1, **kw)
            ins.then_inc(phi_mm, 1)
            for j in range(4):
                c = C["nsa_q"] + j
                arrived(c + 1)
                if j == 3:
                    pe.wait_ge(q_done, 1)
                pair(c % RING, TURN + j % 3, x_h, x_l, PC["mix1"] if j == 0 else None).then_inc(chunk_used, 1)
            arrived(C["nsa_gate"] + 1)
            tokens(C["nsa_gate"] % RING, lambda t: bank[:, SUMS, t * 48:t * 48 + 48], 48, range(KT), x_h, x_l, 0,
                   True, True).then_inc(chunk_used, 1)

            pe.wait_ge(q_done, 4)
            pe.wait_ge(kv_done, 4)
            pe.wait_ge(cmp_done, 2)
            pe.wait_ge(g_sig, 1)
            for kk in range(G_HEADS + 1):
                if kk < G_HEADS:
                    if kk >= 1:
                        pe.wait_ge(n_max, kk)
                    t, e = kk // 2, kk % 2
                    r, j = slice(64 * e, 64 * e + 64), t // 4
                    q0, q1 = n_q[r, t, 0:128], n_q[r, t, 128:256]
                    a, b = bank[:, 4, :], bank[:, 5, :]
                    mm(a[:, 0:256], q1, n_ks[r, j, :], start=True, stop=True)
                    mm(a[:, 256:512], q1, n_kw[r, j, :], start=True, stop=True)
                    mm(b[:, 0:128], q0, n_ks[r, j, 0:128], start=True, stop=True)
                    mm(b[:, 128:256], q0, n_kw[r, j, 0:128], start=True, stop=True)
                    mm(b[:, 256:256 + NVALID0], q0, k_cmp[r, j, 0:NVALID0], start=True, stop=True)
                    mm(b[:, 272:272 + NCMP], q1, k_cmp[r, j, 0:NCMP], start=True, stop=True).then_inc(n_scores, 1)
                if kk >= 1:
                    g = kk - 1
                    pa, pb, nt = n_pa[g % 2], n_pb[g % 2], n_t[g % 2]
                    pe.wait_ge(n_prob, g + 1)
                    if g >= 1:
                        pe.wait_ge(n_ptc, g)
                        pe.wait_ge(n_ptd, g)
                    T = nc.tensor.transpose
                    b6, b7 = bank[:, 6, :], bank[:, 7, :]
                    T(b6[:, 0:128], pb[:, 0:128], ident)
                    T(b6[:, 128:256], pa[:, 0:128], ident)
                    T(b6[:, 256:384], pb[:, 128:256], ident)
                    T(b6[:, 384:512], pa[:, 256:384], ident).then_inc(n_pt, 1)
                    T(b7[:, 0:128], pa[:, 128:256], ident)
                    T(b7[:, 128:256], pa[:, 384:512], ident)
                    T(b7[0:NCMP, 256:384], pb[:, 256:256 + NCMP], ident)
                    T(b7[0:NCMP, 384:512], pb[:, 272:272 + NCMP], ident).then_inc(n_pt, 1)
                    t, e = g // 2, g % 2
                    grp = 2 * (t // 4) + e
                    cols = slice(64 * grp, 64 * grp + 64)
                    r, oc = slice(64 * e, 64 * e + 64), (t % 2) * S
                    o = bank[r, t // 2, oc:oc + S]
                    pe.wait_ge(n_ptc, g + 1)
                    mm(o, n_vs[:, 0, cols], nt[:, 0:256], start=True, stop=False)
                    mm(o, n_vw[:, 0, cols], nt[:, 256:512], start=False, stop=False)
                    pe.wait_ge(n_ptd, g + 1)
                    mm(o, v_cmp[0:NCMP, cols], nt[0:NCMP, 768:1024], start=False, stop=False)
                    mm(o[:, 128:256], n_vs[:, 1, cols], nt[:, 512:640], start=False, stop=False)
                    mm(o[:, 128:256], n_vw[:, 1, cols], nt[:, 640:768], start=False, stop=True).then_inc(n_pv, 1)
            pe.wait_ge(full_ready, FULL["o_nsa"] + 4)
            project("nsa_out", range(4), y_h, y_l, PC["o_nsa"])
            sum_squares("mlp1", PAIRS)
            mlp("mlp1", PC["mlp1"])
            sum_squares("final", PAIRS)


FULL, _at = {}, 0
for _name, _n in (("ffn1", 4), ("mix", 4), ("c_q", 2), ("c_kv", 1), ("o_mla", 4), ("ffn2", 4), ("ple", 4),
                  ("mix0", 4), ("mlp0", 4), ("kv", 4), ("mix1", 4), ("o_nsa", 4), ("mlp1", 4)):
    FULL[_name] = _at
    _at += _n
NSA_ORDER = [(2 * (t // 4) + e) * 4 + t % 4 for t in range(8) for e in range(2)]


def make_constants():
    c = np.zeros((P, N_CONST), np.float32)

    def put(name, a, row=0):
        c[row:row + a.shape[0], CN[name]:CN[name] + a.shape[1]] = a

    i, j = np.arange(P)[:, None], np.arange(P)[None, :]
    put("ident", np.eye(P, dtype=np.float32))
    put("flip", (i + j == P - 1).astype(np.float32))
    put("tri", (i >= j).astype(np.float32))
    strict = np.where(i < j, 0.0, NEG).astype(np.float32)
    put("sb_neg", np.concatenate([strict, np.zeros((P, P), np.float32), strict], 1))
    put("mla_neg", np.concatenate([np.zeros((P, P)), np.where(j <= i, 0.0, NEG)], 1).astype(np.float32))
    rot = np.zeros((32, 32), np.float32)
    for m in range(16):
        rot[m + 16, m] = -1.0
        rot[m, m + 16] = 1.0
    put("rot", rot, 64)
    d = 255 - np.arange(384)
    large = 16 + np.floor(np.log(np.maximum(d, 1) / 16.0) / np.log(8.0) * 16 + 1e-9).astype(int)
    bucket = np.where(d < 16, d, np.minimum(large, 31))
    onehot = np.zeros((33, 384), np.float32)
    for n in range(384):
        onehot[32 if d[n] < 0 else bucket[n], n] = 1.0
    put("bucket", onehot)
    pick = np.zeros((P, 31), np.float32)
    pick[:, 15] = 1.0
    put("pick", pick)
    inv = np.float32(10000.0) ** (-np.arange(0, ROPE, 2, dtype=np.float32) / np.float32(ROPE))
    put("inv_freq", np.concatenate([inv, inv])[:, None].astype(np.float32), 64)
    put("has_any", (np.arange(P) >= 31).astype(np.float32)[:, None])
    return c


def pack_weights(w):
    chunks = []

    def add(a):
        a = a.reshape(P, -1)
        n = -(-a.shape[1] // CH) * CH
        a = np.concatenate([a, np.zeros((P, n - a.shape[1]), np.float32)], 1)
        chunks.extend(a[:, k:k + CH] for k in range(0, n, CH))

    def rows(a, kt=None):
        return a.reshape(-1, P, a.shape[1]).transpose(1, 0, 2)

    def pairs(a):
        for n in range(0, a.shape[1], 256):
            add(rows(a[:, n:n + 256]))

    def ffn(w_in, w_out):
        n = FF * P
        up = lambda f: add(rows(np.concatenate([w_in[:, f * P:f * P + P], w_in[:, n + f * P:n + f * P + P]], 1)))
        down = lambda i: add(rows(w_out[256 * i:256 * i + 256]))
        up(0)
        up(1)
        for i in range(1, FF // 2):
            up(2 * i)
            down(i - 1)
            up(2 * i + 1)
        down(FF // 2 - 1)

    def mlp(w1, w2):
        for j in range(MF + 1):
            if j < MF:
                add(rows(w1[:, 256 * j:256 * j + 256]))
            if j >= 1:
                add(rows(w2[256 * (j - 1):256 * j]))

    ffn(w["ffn1_w_in"][0], w["ffn1_w_out"][0])
    w_in = w["w_in"][0]
    pairs(np.concatenate([w_in[:, 0:672], np.zeros((D, 96), np.float32)], 1))
    pairs(w_in[:, 672:672 + 1024])
    for j in range(2):
        add(rows(w_in[512 * j:512 * j + 512, 1696:2208]))
    pairs(w_in[:, 2208:])
    for j in range(2):
        add(rows(w["w_q_up"][0][:, 384 * j:384 * j + 384]))
    kv = w["w_kv_up"][0].reshape(256, 8, 2, 64)
    add(rows(kv.transpose(0, 2, 1, 3).reshape(256, 1024)))
    for half in range(2):
        for name in ("w_branch_mla", "w_branch_sb"):
            add(rows(w[name][0][:, 512 * half:512 * half + 512]))
    pairs(w["w_out"][0])
    ffn(w["ffn2_w_in"][0], w["ffn2_w_out"][0])
    pairs(w["w_ple_gate"][0])
    add(rows(w["w_ple_proj"][0]))
    a_in = w["a_w_in_2"][0]
    tile = lambda k, t: a_in[:, k * D + t * P:k * D + t * P + P]
    for i in range(4):
        for a, b in ((tile(1, 2 * i), tile(2, 2 * i)), (tile(1, 2 * i + 1), tile(2, 2 * i + 1)),
                     (tile(0, 2 * i), tile(0, 2 * i + 1))):
            add(rows(np.concatenate([a, b], 1)))
    pairs(w["a_w_out_2"][0])
    mlp(w["mlp_w1_2"][0], w["mlp_w2_2"][0])
    for k in (0, 1, 2, 4, 3, 5):
        add(rows(w["w_kv_2"][:, 256 * k:256 * k + 256]))
    for name in ("phi_k_w1_2", "phi_v_w1_2"):
        add(w[name].reshape(2, 16, 64, 256).transpose(0, 2, 1, 3).reshape(P, 16 * 256))
    qg = w["b_w_qg_2"][0]
    pairs(qg[:, :D].reshape(D, 16, 64)[:, NSA_ORDER].reshape(D, D))
    add(rows(qg[:, D:]))
    pairs(w["b_w_o_2"][0].reshape(16, 64, D)[NSA_ORDER].reshape(D, D))
    mlp(w["mlp_w1_2"][1], w["mlp_w2_2"][1])
    out = np.stack(chunks)
    assert out.shape == (N_CHUNKS, P, CH), out.shape
    return out


def pack_small(w):
    s = np.zeros((P, N_SMALL), np.float32)
    s_cols = lambda v: v.reshape(-1, P).T

    def put(name, a):
        s[:a.shape[0], SM[name]:SM[name] + a.shape[1]] = a

    for name, v in (("ffn1", w["ffn1_norm"][0]), ("mix", w["mix_norm"][0]), ("c_q", w["q_latent_norm"][0]),
                    ("c_kv", w["kv_latent_norm"][0]), ("ffn2", w["ffn2_norm"][0]), ("ple", w["ple_norm"][0]),
                    ("mix0", w["norm_mix_2"][0]), ("mlp0", w["norm_mlp_2"][0]), ("kv", w["kv_norm_2"]),
                    ("mix1", w["norm_mix_2"][1]), ("mlp1", w["norm_mlp_2"][1]), ("final", w["final_norm_2"])):
        put(name, s_cols(v))
    put("conv_w", np.concatenate([s_cols(w["a_conv_w_2"][0][k]) for k in range(3)], 1))
    put("q_head", w["q_head_norm"][0][:, None])
    put("k_head", w["k_head_norm"][0][:, None])
    for name in ("k", "v"):
        put("pe_" + name, w[f"cmp_pe_{name}_2"].reshape(2, 16, 64).transpose(0, 2, 1).reshape(P, 16))
        put(f"phi_{name}2", w[f"phi_{name}_w2_2"].reshape(2, P, 64).transpose(1, 0, 2).reshape(P, P))
    return s


def kernel(**inputs):
    import concourse.bacc as _bacc
    from concourse.bass_utils import run_bass_kernel_spmd as _run

    w = {k: np.asarray(v) for k, v in inputs.items()}
    tok = lambda a: np.ascontiguousarray(a.T.reshape(-1, P, S).transpose(1, 0, 2))
    arrays = {
        "x_t": tok(w["x"][0]),
        "p_t": tok(w["p"][0, 0]),
        "positions": np.ascontiguousarray(w["positions"][0]),
        "weights": pack_weights(w),
        "small": pack_small(w),
        "consts": make_constants(),
        "rel_bias": np.ascontiguousarray(w["rel_bias_2"]),
    }
    nc = _bacc.Bacc("TRN2", target_bir_lowering=False, num_devices=1)
    aps = {k: nc.dram_tensor(k, a.shape, mybir.dt.from_np(a.dtype), kind="ExternalInput").ap()
           for k, a in arrays.items()}
    bias_rows = nc.dram_tensor("bias_rows", (16, 384), F32)
    out = nc.dram_tensor("out_t", (P, KT, S), F32, kind="ExternalOutput").ap()
    program(nc, bias_rows=bias_rows, out=out, **aps)
    r = _run(nc, [arrays], core_ids=[0])
    y = r.results[0]["out_t"]
    return y.transpose(2, 1, 0).reshape(1, S, D)
```

```python
from contextlib import ExitStack

import numpy as np

import concourse.bass as bass
from concourse import mybir

F32 = mybir.dt.float32
F32R = mybir.dt.float32r
BF16 = mybir.dt.bfloat16
I32 = mybir.dt.int32
ALU = mybir.AluOpType
ACT = mybir.ActivationFunctionType
AX = mybir.AxisListType

P = 128
S = 256
D = 1024
KT = D // P
FF = 2816 // P
MF = 4096 // P // 2
MLP_TURNS = (MF - 2) // 3
EPS = 1e-6
NEG = -1e30
RING = 3
CH = 2048
HEADS, NOPE, ROPE = 8, 64, 32
QK = NOPE + ROPE
NCMP = S // 16 - 1
NVALID0 = 7
G_HEADS = 16
LINE = 384
SKEW = LINE + 1
UPDATES = 4

_sizes = [("ffn1", FF + FF // 2), ("latent", 3), ("sb_q", 2), ("sb_k", 2), ("sb_v", 2), ("q_up", 2),
          ("kv_up", 1), ("gates", 8), ("branch", 4), ("w_out", 4), ("ffn2", FF + FF // 2),
          ("ple_proj", 1), ("ple_gate", 4), ("conv_in", 12), ("conv_out", 4), ("mlp0", 2 * MF),
          ("kv_raw", 2), ("k_att", 2), ("v_att", 2), ("nsa_q", 4), ("nsa_gate", 1), ("phi", 4),
          ("nsa_out", 4), ("mlp1", 2 * MF)]
C, _at = {}, 0
for _name, _n in _sizes:
    C[_name] = _at
    _at += _n
N_CHUNKS = _at
assert N_CHUNKS % RING == 0

_pieces = [("ffn1", 4), ("mix", 4), ("c_q", 2), ("c_kv", 1), ("o", 4), ("merged", 4), ("ffn2", 4), ("p", 1),
           ("ple", 4), ("mix0", 4), ("conv", 4), ("mlp0", 4), ("kv", 4), ("mix1", 4), ("blk_k", 1),
           ("blk_v", 1), ("o_nsa", 4), ("mlp1", 4)]
PC, _at = {}, 0
for _name, _n in _pieces:
    PC[_name] = _at
    _at += _n

_small = [("ffn1", 8), ("mix", 8), ("c_q", 3), ("c_kv", 2), ("ffn2", 8), ("ple", 8), ("mix0", 8),
          ("mlp0", 8), ("kv", 8), ("mix1", 8), ("mlp1", 8), ("final", 8), ("conv_w", 24),
          ("q_head", 1), ("k_head", 1), ("pe_k", 16), ("pe_v", 16), ("phi_k2", 128), ("phi_v2", 128)]
SM, _at = {}, 0
for _name, _n in _small:
    SM[_name] = _at
    _at += _n
N_SMALL = _at

_const = [("ident", 128), ("tri", 128), ("sb_neg", 384), ("mla_neg", 256), ("rot", 32), ("bucket", 384),
          ("pick", 31), ("inv_freq", 1), ("has_any", 1)]
CN, _at = {}, 0
for _name, _n in _const:
    CN[_name] = _at
    _at += _n
N_CONST = _at

ACC, TURN, SUMS = 0, 4, 7
HID = {"ffn1": 0, "ffn2": FF, "mlp0": 2 * FF, "mlp1": 2 * FF + MF}
ENDS = {"ffn1": 0, "ffn2": 3, "mlp0": 6, "mlp1": 9}
UPD = {"ffn1": 0, "mix": 4, "ffn2": 8, "ple": 12, "mix0": 16, "mlp0": 20, "kv": 24, "mlp1": 28, "final": 32}
NORMS = ["ffn1", "mix", "c_q", "c_kv", "head", "ffn2", "ple", "mix0", "mlp0", "kv", "mlp1", "final"]
NO = {n: i for i, n in enumerate(NORMS)}
SQ, _at = {}, 0
for _n, _c in (("ffn1", 4), ("mix", 4), ("c_q", 1), ("c_kv", 1), ("head", 8), ("ffn2", 4), ("ple", 4),
               ("mix0", 4), ("mlp0", 4), ("kv", 4), ("mlp1", 4), ("final", 4)):
    SQ[_n] = _at
    _at += _c
DRAIN = {"latent": 0, "sb": 3, "gates": 7, "conv": 15}


class Steps:

    def __init__(self, eng, sem):
        self.eng, self.sem, self.n = eng, sem, 0

    def inc(self, ins):
        ins.then_inc(self.sem, 1)
        self.n = self.n + 1

    def wait(self):
        self.eng.wait_ge(self.sem, self.n)

    def done(self, ins):
        self.inc(ins)
        self.wait()


def program(nc, x_t, p_t, positions, weights, small, consts, rel_bias, bias_rows, bias_skew, out):
    with ExitStack() as ctx:
        def sb(name, shape, dt=F32):
            return ctx.enter_context(nc.sbuf_tensor(name, shape, dt))

        def sem(name):
            return ctx.enter_context(nc.semaphore(name))

        bank = ctx.enter_context(nc.psum_tensor("bank", [P, 8, 512], F32))

        raw = sb("raw", [P, RING, CH])
        w_hi = sb("w_hi", [P, RING, CH], F32R)
        w_lo = sb("w_lo", [P, RING, CH], F32R)
        h = sb("h", [P, KT, S])
        x_f, x_h, x_l = sb("x_f", [P, KT, S]), sb("x_h", [P, KT, S], F32R), sb("x_l", [P, KT, S], F32R)
        y_f, y_h, y_l = sb("y_f", [P, KT, S]), sb("y_h", [P, KT, S], F32R), sb("y_l", [P, KT, S], F32R)
        sq = sb("sq", [P, KT, S])
        hid_f = sb("hid_f", [P, 2, S])
        t_exp, t_a, t_b, r_sb = sb("t_exp", [P, S]), sb("t_a", [P, S]), sb("t_b", [P, S]), sb("r_sb", [P, S])
        t_ab = sb("t_ab", [P, 2, S])
        r_lat = sb("r_lat", [P, 2, S])
        r_tok = sb("r_tok", [P, 2, 2])
        t_m = sb("t_m", [P, S])
        heads = sb("heads", [P, 16, S])
        gate_or_bias = sb("gate_or_bias", [P, 16, S])
        sv = sb("sv", [P, 2, 512])
        mv = sb("mv", [P, 2, 512])
        par = sb("par", [P, N_SMALL])
        con = sb("con", [P, N_CONST])
        ones = sb("ones", [P, P])
        zeros = sb("zeros", [P, 512], BF16)
        relb = sb("relb", [33, 16])
        bias_1d = sb("bias_1d", [16, 384])
        pos_i, rope_tab = sb("pos_i", [P, S], I32), sb("rope_tab", [P, 2, S])
        v_pad = sb("v_pad", [P, 2, S + 2])
        stat = sb("stat", [P, 64])

        raw_landed = [sem(f"raw_landed{i}") for i in range(RING)]
        hi_split, lo_split, chunk_used = sem("hi_split"), sem("lo_split"), sem("chunk_used")
        x_in, small_in, con_in, relb_in, pos_in, p_in = (
            sem("x_in"), sem("small_in"), sem("con_in"), sem("relb_in"), sem("pos_in"), sem("p_in"))
        setup = sem("setup")
        sq_ready, ss_ready, ms_ready, r0_ready = sem("sq_ready"), sem("ss_ready"), sem("ms_ready"), sem("r0_ready")
        op_hi, op_lo = sem("op_hi"), sem("op_lo")
        ffn_sig, hid_full, hid_hi, hid_lo = sem("ffn_sig"), sem("hid_full"), sem("hid_hi"), sem("hid_lo")
        acc_ready, h_upd, drained = sem("acc_ready"), sem("h_upd"), sem("drained")
        dve_step, act_step = sem("dve_step"), sem("act_step")
        ab_ready, sum_ready, r_ready, rt_mm, conv_full = (
            sem("ab_ready"), sem("sum_ready"), sem("r_ready"), sem("rt_mm"), sem("conv_full"))
        rope_ang, rope_sin = sem("rope_ang"), sem("rope_sin")
        sv_done, qk_raw, ss_head = sem("sv_done"), sem("qk_raw"), sem("ss_head")
        r_head, bc_ready, normed, rot_ready, rope_cos, roped = (
            sem("r_head"), sem("bc_ready"), sem("normed"), sem("rot_ready"), sem("rope_cos"), sem("roped"))
        m_scores, m_max, m_exp, m_prob, m_pt, m_ptc, m_pv = (
            sem("m_scores"), sem("m_max"), sem("m_exp"), sem("m_prob"), sem("m_pt"), sem("m_ptc"), sem("m_pv"))
        s_z, s_abs, s_min, s_ln, s_l, s_e, s_x, s_a, s_pv = (
            sem("s_z"), sem("s_abs"), sem("s_min"), sem("s_ln"), sem("s_l"), sem("s_e"), sem("s_x"), sem("s_a"),
            sem("s_pv"))
        merged_done = sem("merged_done")
        ple_sig = sem("ple_sig")
        bias_ready, bias_out, bias_in = sem("bias_ready"), sem("bias_out"), sem("bias_in")
        bias_mm = sem("bias_mm")
        gates_done, ple_raw, g_raw = sem("gates_done"), sem("ple_raw"), sem("g_raw")
        kv_done, blk_ready = sem("kv_done"), sem("blk_ready")
        phi_t = sem("phi_t")
        phi_sig, phi_hid, phi_mm, cmp_done = sem("phi_sig"), sem("phi_hid"), sem("phi_mm"), sem("cmp_done")
        q_done, g_sig = sem("q_done"), sem("g_sig")
        c_scores, c_sub, c_exp, c_prob, c_pt, c_ptc = (
            sem("c_scores"), sem("c_sub"), sem("c_exp"), sem("c_prob"), sem("c_pt"), sem("c_ptc"))
        n_scores, n_max, n_exp, n_prob, n_pt, n_ptc, n_ptd, n_pv = (
            sem("n_scores"), sem("n_max"), sem("n_exp"), sem("n_prob"), sem("n_pt"), sem("n_ptc"), sem("n_ptd"),
            sem("n_pv"))
        y_ready, stored = sem("y_ready"), sem("stored")

        def col(name, i=0, n=1):
            return par[:, SM[name] + i:SM[name] + i + n]

        def cst(name, n, i=0):
            return con[:, CN[name] + i:CN[name] + i + n]

        ident = cst("ident", P)
        flat = lambda t: t[:, :, :].rearrange("p a b -> p (a b)")
        x_flat, sq_flat, y_flat = flat(x_f), flat(sq), flat(y_f)
        x_hf, x_lf = flat(x_h), flat(x_l)
        two = lambda ap: ap.rearrange("p (a b) -> p a b", a=2)
        r_two = r_sb[:, :].rearrange("p (a b) -> p a b", a=1).to_broadcast([P, 2, S])

        hidden = {"ffn1": (y_h[:, 0:4, :], y_l[:, 0:4, :]), "ffn2": (x_h[:, 2:6, :], x_l[:, 2:6, :]),
                  "mlp0": (y_h[:, 0:6, :], y_l[:, 0:6, :]), "mlp1": (y_h[:, 0:6, :], y_l[:, 0:6, :])}

        m_p = [x_flat[:, 384 * i:384 * i + 384] for i in range(2)]
        m_t = [x_flat[:, 768 + 384 * i:1152 + 384 * i] for i in range(2)]
        s_t1 = x_flat[:, 1536:1920]
        s_t2, s_m, s_lm = (sq_flat[:, 384 * i:384 * i + 384] for i in range(3))
        s_p = [sq_flat[:, 1152 + 384 * i:1536 + 384 * i] for i in range(2)]
        v_cmp = mv[:, 0, 0:64]
        c_stat = mv[:, 1, 160:288].rearrange("p (a q h) -> p a q h", a=4, q=2)
        k_cmp = mv[:, 1, 0:64].rearrange("p (j e n) -> p j e n", j=2, e=2)
        nsa_g = mv[:, 1, 64:160].rearrange("p (a b) -> p a b", a=2)
        cmp_hid = sv[:, 0, 0:240].rearrange("p (w k n) -> p w k n", w=2, k=2)
        phi_h = sv[0:60, 1, :].rearrange("p (w n) -> p w n", w=2)
        n_pa = [x_flat[:, 512 * i:512 * i + 512] for i in range(3)]
        n_pb = [x_flat[:, 1536 + 256 * i:1792 + 256 * i] for i in range(2)] + [t_ab[:, 0, :]]
        n_t = [sq_flat[:, 768 * i:768 * i + 768] for i in range(2)]
        c_p = y_flat[:, 0:1024].rearrange("p (q t g n) -> p q t g n", q=2, t=4, g=4)
        c_t = y_flat[:, 1024:2048]
        c_n = (NVALID0, NCMP)
        sb_q, sb_k = y_f[:, 0:4, :], y_f[:, 4:8, :]
        gate = gate_or_bias
        lat_raw = heads[:, 0:5, :]
        n_q, n_ks, n_kw, n_vs, n_vw = heads[:, 0:8, :], heads[:, 8:10, :], heads[:, 10:12, :], heads[:, 12:14, :], heads[:, 14:16, :]
        k_rope = t_b

        def n_parts(k):
            pa, pb = n_pa[k % 3], n_pb[k % 3]
            return pa[:, 0:256], pa[:, 256:512], pb[:, 0:128], pb[:, 128:256]

        bcb = lambda p: p % 6

        block = ctx.enter_context(nc.Block())

        @block.sync
        def _(sp):
            sp.dma_start(h[:, :, :], x_t).then_inc(x_in, 16)
            sp.dma_start(par[:, :], small).then_inc(small_in, 16)
            for c in range(RING):
                sp.dma_start(raw[:, c, :], weights[c]).then_inc(raw_landed[c], 16)
            sp.dma_start(con[:, :], consts).then_inc(con_in, 16)
            sp.dma_start(relb[0:32, :], rel_bias).then_inc(relb_in, 16)
            sp.dma_start(pos_i[64:96, :], positions.partition_broadcast(32)).then_inc(pos_in, 16)
            with sp.Fori(1, N_CHUNKS // RING) as i:
                for j in range(RING):
                    sp.wait_ge(lo_split, RING * i + (j - RING + 1))
                    sp.dma_start(raw[:, j, :], weights[i * RING + j]).then_inc(raw_landed[j], 16)
            for j in range(UPDATES):
                sp.wait_ge(y_ready, j + 1)
                sp.dma_start(out[:, 2 * j:2 * j + 2, :], x_f[:, 2 * j:2 * j + 2, :]).then_inc(stored, 16)
            sp.wait_ge(stored, 16 * UPDATES)

        @block.gpsimd
        def _(pool):
            for n, (t, value) in enumerate(((ones[:, :], 1.0), (zeros[:, :], 0.0), (v_pad[:, :, :], 0.0),
                                            (relb[32:33, :], NEG))):
                if n >= 1:
                    pool.wait_ge(setup, n)
                nc.gpsimd.memset(t, value).then_inc(setup, 1)
            pool.wait_ge(setup, 4)
            for p in range(8):
                pool.wait_ge(normed, p + 1)
                pool.wait_ge(rope_sin, 2)
                if p >= 1:
                    pool.wait_ge(roped, p)
                y = heads[64:96, 2 * p:2 * p + 2, :]
                cos = rope_tab[64:96, 0:1, :].to_broadcast([32, 2, S])
                nc.gpsimd.tensor_tensor(v_pad[64:96, :, 0:S], y, cos, ALU.mult).then_inc(rope_cos, 1)
            pool.wait_ge(roped, 8)
            nc.gpsimd.memset(v_pad[:, :, 0:2], 0.0).then_inc(setup, 1)
            pool.wait_ge(bias_ready, 1)
            pool.dma_start(bias_rows.ap(), bias_1d[:, :]).then_inc(bias_out, 16)
            pool.wait_ge(bias_out, 16)
            pool.dma_start(bass.AP(tensor=bias_skew, offset=0, ap=[[P * SKEW, G_HEADS], [SKEW, P], [1, LINE]]),
                           bass.AP(tensor=bias_rows, offset=0, ap=[[LINE, G_HEADS], [0, P], [1, LINE]])
                           ).then_inc(bias_out, 16)
            pool.wait_ge(bias_out, 32)
            pool.wait_ge(m_pv, 2 * HEADS)
            pool.dma_start(heads[:, 0:2, :], p_t).then_inc(p_in, 16)
            pool.wait_ge(merged_done, UPDATES)
            toeplitz = bass.AP(tensor=bias_skew, offset=P - 1, ap=[[LINE, P], [P * SKEW, G_HEADS], [1, S]])
            pool.dma_start(gate_or_bias[:, :, :], toeplitz).then_inc(bias_in, 16)
            pool.wait_ge(bias_in, 16)
            pool.wait_ge(p_in, 16)
            pool.wait_ge(op_lo, PC["blk_v"] + 1)
            nc.gpsimd.memset(y_flat[:, 0:1024], 0.0).then_inc(setup, 1)

        @block.scalar
        def _(act):
            st = Steps(act, act_step)

            def split(c, s, turn):
                act.wait_ge(raw_landed[s], 16 * turn)
                nc.scalar.activation(w_hi[:, s, :], raw[:, s, :], ACT.Copy).then_inc(hi_split, 1)

            def nxt(c):
                if c + RING < N_CHUNKS:
                    act.wait_ge(chunk_used, c + 1)
                    split(c + RING, c % RING, (c + RING) // RING + 1)

            def nxt_in(c0, j, i, step):
                c = c0 + j
                if isinstance(i, int):
                    nxt(c + i * step)
                    return
                act.wait_ge(chunk_used, i * step + (c + 1))
                split(None, c % RING, i * (step // RING) + (c // RING + 2))

            def hi(dst, src, full_sem=None, full_value=None, free=None):
                if full_sem is not None:
                    act.wait_ge(full_sem, full_value)
                if free is not None:
                    act.wait_ge(chunk_used, free)
                nc.scalar.activation(dst, src, ACT.Copy).then_inc(op_hi, 1)

            def gained_hi(dst, src, name, a, b):
                for t in range(a, b):
                    ins = nc.scalar.activation(dst[:, t - a, :], src[:, t - a, :], ACT.Copy, scale=col(name, t))
                ins.then_inc(op_hi, 1)

            def rsqrt(name, rows=slice(0, P)):
                nc.scalar.preload_act_table_set("natural_log_exp_and_others")
                act.wait_ge(ms_ready, NO[name] + 1)
                st.done(nc.scalar.activation(t_a[rows, :], t_m[rows, :], ACT.Ln))
                nc.scalar.activation(t_exp[rows, :], t_a[rows, :], ACT.Exp, scale=-0.5).then_inc(r0_ready, 1)

            def operand(name, dst, free=None, chunks=()):
                for j in range(4):
                    if name == "ffn1":
                        act.wait_ge(x_in, 16)
                        act.wait_ge(small_in, 16)
                    else:
                        act.wait_ge(h_upd, UPD[name] - UPDATES + j + 1)
                    if j == 0 and free is not None:
                        act.wait_ge(chunk_used, free)
                    gained_hi(dst[:, 2 * j:2 * j + 2, :], h[:, 2 * j:2 * j + 2, :], name, 2 * j, 2 * j + 2)
                    if j < len(chunks):
                        nxt(chunks[j])

            def squares(name):
                for j in range(4):
                    if name == "final":
                        act.wait_ge(h_upd, UPD[name] - UPDATES + j + 1)
                    nc.scalar.activation(sq[:, 2 * j:2 * j + 2, :], h[:, 2 * j:2 * j + 2, :],
                                         ACT.Square).then_inc(sq_ready, 1)

            def norm(name, dst, free=None, chunks=(), last_chunk=None):
                operand(name, dst, free, chunks)
                squares(name)
                if last_chunk is not None:
                    nxt(last_chunk)
                rsqrt(name)

            def ffn(name):
                c0, b = C[name], HID[name]
                hid_h = hidden[name][0]

                def hid(slot, f, value, used=None):
                    act.wait_ge(hid_full, value)
                    if used is not None:
                        act.wait_ge(chunk_used, used)
                    nc.scalar.activation(hid_h[:, slot + f, :], hid_f[:, f, :], ACT.Copy).then_inc(hid_hi, 1)

                e0 = 0 if name == "ffn1" else FF

                def sigmoid(count):
                    act.wait_ge(ab_ready, count)
                    nc.scalar.activation(t_exp[:, :], t_ab[:, 0, :], ACT.Sigmoid).then_inc(ffn_sig, 1)

                for f in range(2):
                    sigmoid(e0 + f + 1)
                    hid(0, f, b + f + 1)
                    nxt(c0 + f)
                with act.Fori(0, (FF // 2 - 1) // 2) as i:
                    for r in range(2):
                        c1, n = c0 + 2 + 3 * r, 2 * r + 2
                        sigmoid(i * 4 + (e0 + n + 1))
                        nxt_in(c1, 0, i, 6)
                        hid(2 - 2 * r, 0, i * 4 + (b + n + 1), i * 6 + c1)
                        sigmoid(i * 4 + (e0 + n + 2))
                        hid(2 - 2 * r, 1, i * 4 + (b + n + 2))
                        nxt_in(c1, 1, i, 6)
                        nxt_in(c1, 2, i, 6)

            def mlp(name):
                c0, b = C[name], HID[name]
                hid_h = hidden[name][0]

                def hid(slot, value, used=None):
                    act.wait_ge(hid_full, value)
                    if used is not None:
                        act.wait_ge(chunk_used, used)
                    nc.scalar.activation(hid_h[:, 2 * slot:2 * slot + 2, :], hid_f[:, :, :],
                                         ACT.Copy).then_inc(hid_hi, 1)

                for j in range(2):
                    hid(j, b + j + 1)
                    nxt(c0 + j)

                def step(r, i):
                    nxt_in(c0 + 2, 2 * r, i, 6)
                    hid((r + 2) % 3, i * 3 + (b + r + 3), i * 6 + (c0 + 2 * r + 2))
                    nxt_in(c0 + 2, 2 * r + 1, i, 6)

                with act.Fori(0, MLP_TURNS) as i:
                    for r in range(3):
                        step(r, i)
                for j in range(3 * MLP_TURNS, MF - 2):
                    step(j % 3, j // 3)
                nxt(c0 + 2 * MF - 2)

            def products_of_gates(j):
                nxt(C["gates"] + j)

            split(0, 0, 1)
            operand("ffn1", x_h)
            for c in range(1, RING):
                split(c, c, 1)
            squares("ffn1")
            rsqrt("ffn1")
            ffn("ffn1")

            norm("mix", x_h, C["latent"] - 1, (), C["latent"] - 1)
            for j in range(3):
                nxt(C["latent"] + j)
            act.wait_ge(drained, DRAIN["latent"] + 3)
            gained_hi(y_h[:, 0:2, :], lat_raw[:, 0:2, :], "c_q", 0, 2)
            gained_hi(y_h[:, 2:3, :], lat_raw[:, 2:3, :], "c_q", 2, 3)
            gained_hi(y_h[:, 3:5, :], lat_raw[:, 3:5, :], "c_kv", 0, 2)
            nc.scalar.activation(sq[:, 0:3, :], lat_raw[:, 0:3, :], ACT.Square).then_inc(sq_ready, 1)
            nc.scalar.activation(sq[:, 3:5, :], lat_raw[:, 3:5, :], ACT.Square).then_inc(sq_ready, 1)
            for j in range(4):
                nxt(C["sb_q"] + j)
            rsqrt("c_q")
            rsqrt("c_kv")
            act.wait_ge(rope_ang, 2)
            nc.scalar.activation(rope_tab[64:96, 0, :], rope_tab[64:96, 0, :], ACT.Sin).then_inc(rope_sin, 1)
            nc.scalar.activation(rope_tab[64:96, 1, :], rope_tab[64:96, 1, :], ACT.Sin).then_inc(rope_sin, 1)
            for j in range(2):
                nxt(C["sb_v"] + j)
            for j in range(3):
                nxt(C["q_up"] + j)
            act.wait_ge(qk_raw, 9)
            for p in range(8):
                dst = sq if p < 4 else x_f
                nc.scalar.activation(dst[0:QK, 2 * (p % 4):2 * (p % 4) + 2, :], heads[0:QK, 2 * p:2 * p + 2, :],
                                     ACT.Square).then_inc(sq_ready, 1)
            for j in range(2):
                products_of_gates(j)
            rsqrt("head", slice(0, 16))
            for j in range(2, 4):
                products_of_gates(j)

            def m_front(hd):
                act.wait_ge(m_max, hd + 1)
                for q in range(2):
                    c = slice(0, 128) if q == 0 else slice(128, 384)
                    o = 4 * (hd % 2) + q
                    nc.scalar.activation(m_p[hd % 2][:, c], m_p[hd % 2][:, c], ACT.Exp, scale=float(QK) ** -0.5,
                                         bias=stat[:, 8 + o:9 + o], accum_out=stat[:, 16 + o:17 + o]).then_inc(m_exp, 1)

            for hd in range(HEADS + 1):
                if hd < HEADS:
                    act.wait_ge(s_z, hd + 1)
                    if hd >= 1:
                        act.wait_ge(s_l, hd)
                    nc.scalar.activation(s_t1, bank[:, 1, 0:384], ACT.Abs).then_inc(s_abs, 1)
                    act.wait_ge(s_abs, hd + 1)
                    st.done(nc.scalar.activation(s_t1, s_t1, ACT.Exp, scale=-1.0))
                    nc.scalar.activation(s_t2, s_t1, ACT.Ln, bias=1.0).then_inc(s_ln, 1)
                    m_front(hd)
                if hd >= 1:
                    act.wait_ge(s_x, hd)
                    nc.scalar.activation(s_p[(hd - 1) % 2], s_p[(hd - 1) % 2], ACT.Exp).then_inc(s_a, 1)
                if hd % 2 == 1:
                    products_of_gates(4 + hd // 2)
                if hd >= 2 and hd % 2 == 0:
                    t = hd // 2 - 1
                    act.wait_ge(m_pv, 2 * hd)
                    hi(y_h[:, t:8:4, :], two(bank[:, 4 + t % 2, :]), s_pv, hd)
            act.wait_ge(drained, DRAIN["gates"] + 8)
            for j in range(4):
                nc.scalar.activation(gate[:, 4 * j:4 * j + 4, :], gate[:, 4 * j:4 * j + 4, :],
                                     ACT.Sigmoid).then_inc(gates_done, 1)
            for j in range(4):
                if j == 2:
                    nxt(C["branch"])
                    nxt(C["branch"] + 1)
                hi(x_h[:, 2 * j:2 * j + 2, :], x_f[:, 2 * j:2 * j + 2, :], merged_done, j + 1)
            nxt(C["branch"] + 2)
            nxt(C["branch"] + 3)

            w = C["w_out"]
            norm("ffn2", y_h, C["branch"] + 4, (w, w + 1, w + 2), w + 3)
            hi(x_h[:, 0:2, :], heads[:, 0:2, :], p_in, 16)
            ffn("ffn2")

            norm("ple", y_h, C["ple_proj"] - 1, (), C["ple_proj"] - 1)
            nxt(C["ple_proj"])
            c = C["ple_gate"]
            for j in range(4):
                act.wait_ge(ple_raw, j + 1)
                g = y_f[:, 2 * j:2 * j + 2, :]
                nc.scalar.activation(g, g, ACT.Sigmoid).then_inc(ple_sig, 1)
                if j < 3:
                    nxt(c + j)
                act.wait_ge(h_upd, UPD["mix0"] - UPDATES + j + 1)
                gained_hi(x_h[:, 2 * j:2 * j + 2, :], h[:, 2 * j:2 * j + 2, :], "mix0", 2 * j, 2 * j + 2)

            squares("mix0")
            nxt(c + 3)
            rsqrt("mix0")
            with act.Fori(0, 4) as i:
                c0 = C["conv_in"]
                nxt_in(c0, 0, i, 3)
                nxt_in(c0, 1, i, 3)
                act.wait_ge(conv_full, i + 1)
                nc.scalar.activation(y_h[:, bass.ds(i * 2, 2), :], y_f[:, bass.ds(i * 2, 2), :], ACT.Copy).then_inc(op_hi, 1)
                nxt_in(c0, 2, i, 3)

            w = C["conv_out"]
            norm("mlp0", x_h, w, (w, w + 1, w + 2), w + 3)
            mlp("mlp0")

            c = C["kv_raw"]
            norm("kv", x_h, c - 1, (), c - 1)
            nxt(c)
            for j in range(4):
                gained_hi(y_h[:, 2 * j:2 * j + 2, :], h[:, 2 * j:2 * j + 2, :], "mix1", 2 * j, 2 * j + 2)
            for j in range(1, 6):
                nxt(c + j)
            hi(x_hf[:, 0:960], y_flat[:, 0:960], blk_ready, 4, C["nsa_q"])
            hi(x_hf[:, 960:1920], y_flat[:, 960:1920], blk_ready, 8)
            for j in range(4):
                nxt(C["nsa_q"] + j)
            act.wait_ge(g_raw, 1)
            nc.scalar.activation(nsa_g[:, :, :], nsa_g[:, :, :], ACT.Sigmoid).then_inc(g_sig, 1)
            nxt(C["nsa_gate"])
            for w in range(2):
                nxt(C["phi"] + w)
            for w in range(2):
                act.wait_ge(chunk_used, C["phi"] + 2 * w + 2)
                if w == 1:
                    act.wait_ge(phi_hid, 1)
                nc.scalar.activation(t_exp[0:60, :], bank[0:60, (7, 3)[w], 0:256], ACT.Sigmoid).then_inc(phi_sig, 1)
            nc.scalar.preload_act_table_set("natural_log_exp_and_others")

            for k in range(G_HEADS + 2):
                if k < G_HEADS:
                    act.wait_ge(n_max, k + 1)
                    o = 16 * (k % 3)
                    for m, ap in enumerate(n_parts(k)):
                        nc.scalar.activation(ap, ap, ACT.Exp, bias=stat[:, o + 4 + m:o + 5 + m],
                                             accum_out=stat[:, o + 8 + m:o + 9 + m]).then_inc(n_exp, 1)
                if k >= 2:
                    act.wait_ge(n_pt, 2 * k - 3)
                    if k >= 4:
                        act.wait_ge(n_pv, k - 3)
                    nc.scalar.activation(n_t[k % 2][:, 0:512], bank[:, 6, :], ACT.Copy).then_inc(n_ptc, 1)
                if k == 0:
                    for q in range(2):
                        c = c_p[:, q, :, :, 0:c_n[q]]
                        act.wait_ge(c_sub, q + 1)
                        nc.scalar.activation(c, c, ACT.Exp).then_inc(c_exp, 1)
                if k == 2:
                    act.wait_ge(c_pt, 1)
                    nc.scalar.activation(c_t[:, 512:1024], bank[:, 1, :], ACT.Copy).then_inc(c_ptc, 1)
                if k in (4, 5):
                    nxt(C["phi"] + k - 2)
                if k % 4 == 3 and k >= 7:
                    m = k // 4 - 1
                    hi(y_h[:, 2 * m:2 * m + 2, :], two(bank[:, m % 2, :]), n_pv, 4 * m + 4)
            hi(y_h[:, 6:8, :], two(bank[:, 1, :]), n_pv, G_HEADS)

            w = C["nsa_out"]
            norm("mlp1", x_h, w, (w, w + 1, w + 2), w + 3)
            mlp("mlp1")
            squares("final")
            rsqrt("final")

        @block.vector
        def _(dve):
            st = Steps(dve, dve_step)
            V = nc.vector

            def split(s, count):
                dve.wait_ge(hi_split, count)
                V.tensor_tensor(w_lo[:, s, :], raw[:, s, :], w_hi[:, s, :].bitcast(F32), ALU.subtract).then_inc(lo_split, 1)

            def nxt(c):
                if c + RING < N_CHUNKS:
                    split(c % RING, c + RING + 1)

            def nxt_in(c0, j, i, step):
                if isinstance(i, int):
                    nxt(c0 + j + i * step)
                    return
                split((c0 + j) % RING, i * step + (c0 + j + RING + 1))

            made = [0]

            def lo(dst, src, hi_part):
                made[0] += 1
                dve.wait_ge(op_hi, made[0])
                V.tensor_tensor(dst, src, hi_part.bitcast(F32), ALU.subtract).then_inc(op_lo, 1)

            def rsqrt(name, ss, rows=slice(0, P), width=D, r_out=None, last=None):
                dve.wait_ge(ss_ready, NO[name] + 1)
                V.tensor_scalar(t_m[rows, :], ss, 1.0 / width, EPS, ALU.mult, ALU.add).then_inc(ms_ready, 1)
                dve.wait_ge(r0_ready, NO[name] + 1)
                st.done(V.tensor_tensor(t_a[rows, :], t_exp[rows, :], t_exp[rows, :], ALU.mult))
                st.done(V.scalar_tensor_tensor(out=t_a[rows, :], in0=t_a[rows, :], scalar=-0.5, in1=t_m[rows, :],
                                               op0=ALU.mult, op1=ALU.mult))
                ins = V.scalar_tensor_tensor(out=r_out, in0=t_a[rows, :], scalar=1.5, in1=t_exp[rows, :],
                                             op0=ALU.add, op1=ALU.mult)
                if last is None:
                    st.done(ins)
                else:
                    ins.then_inc(last, 1)

            def gained_lo(dst, src, hi_part, name, a, b):
                made[0] += 1
                dve.wait_ge(op_hi, made[0])
                for t in range(a, b):
                    ins = V.scalar_tensor_tensor(out=dst[:, t - a, :], in0=src[:, t - a, :], scalar=col(name, t),
                                                 in1=hi_part[:, t - a, :].bitcast(F32), op0=ALU.mult,
                                                 op1=ALU.subtract)
                ins.then_inc(op_lo, 1)

            def operand_piece(name, d_h, d_l, j):
                assert made[0] == PC[name] + j
                a = slice(2 * j, 2 * j + 2)
                gained_lo(d_l[:, a, :], h[:, a, :], d_h[:, a, :], name, 2 * j, 2 * j + 2)

            def sum_tiles(name):
                dve.wait_ge(sq_ready, SQ[name] + 2)
                st.done(V.tensor_tensor(sq[:, 0:2, :], sq[:, 0:2, :], sq[:, 2:4, :], ALU.add))
                dve.wait_ge(sq_ready, SQ[name] + 3)
                st.done(V.tensor_tensor(sq[:, 0:2, :], sq[:, 0:2, :], sq[:, 4:6, :], ALU.add))
                dve.wait_ge(sq_ready, SQ[name] + 4)
                st.done(V.tensor_tensor(sq[:, 0:2, :], sq[:, 0:2, :], sq[:, 6:8, :], ALU.add))
                V.tensor_tensor(sq[:, 0, :], sq[:, 0, :], sq[:, 1, :], ALU.add).then_inc(sum_ready, 1)

            def update_piece(scale, j):
                hj = h[:, 2 * j:2 * j + 2, :]
                V.scalar_tensor_tensor(out=hj, in0=two(bank[:, ACC + j, :]), scalar=scale, in1=hj, op0=ALU.mult,
                                       op1=ALU.add).then_inc(h_upd, 1)

            def finish(stage, scale, following, d_h, d_l):
                last_chunk = C[stage] + (FF + FF // 2 if stage in ("ffn1", "ffn2") else 2 * MF) - 1
                for j in range(5):
                    if j < 4:
                        if j < 3:
                            dve.wait_ge(acc_ready, ENDS[stage] + j + 1)
                        else:
                            dve.wait_ge(chunk_used, last_chunk + 1)
                        update_piece(scale, j)
                    if j >= 1 and d_h is not None:
                        operand_piece(following, d_h, d_l, j - 1)
                sum_tiles(following)
                nxt(last_chunk)

            def project_out(stage, following, d_h, d_l):
                c = C[stage]
                for j in range(4):
                    dve.wait_ge(chunk_used, c + j + 1)
                    update_piece(1.0, j)
                    if j < 3:
                        nxt(c + j)
                    operand_piece(following, d_h, d_l, j)
                sum_tiles(following)
                nxt(c + 3)

            def factor(name, bk=SUMS):
                rsqrt(name, bank[:, bk, 0:S], r_out=r_sb[:, :])

            def ffn(name):
                c0, b = C[name], HID[name]
                hid_h, hid_l = hidden[name]

                def swiglu(f, count, used):
                    dve.wait_ge(chunk_used, used)
                    V.tensor_tensor(t_ab[:, :, :], two(bank[:, TURN + f, :]), r_two, ALU.mult).then_inc(ab_ready, 1)
                    dve.wait_ge(ab_ready, ab + (count - e0))
                    st.done(V.tensor_tensor(t_a[:, :], t_ab[:, 0, :], t_ab[:, 1, :], ALU.mult))
                    dve.wait_ge(ffn_sig, count)
                    V.tensor_tensor(hid_f[:, f, :], t_a[:, :], t_exp[:, :], ALU.mult).then_inc(hid_full, 1)

                def hid(slot, f, count):
                    dve.wait_ge(hid_hi, count)
                    V.tensor_tensor(hid_l[:, slot + f, :], hid_f[:, f, :], hid_h[:, slot + f, :].bitcast(F32),
                                    ALU.subtract).then_inc(hid_lo, 1)

                e0 = ab = b
                for f in range(2):
                    swiglu(f, e0 + f + 1, c0 + f + 1)
                    hid(0, f, b + f + 1)
                    nxt(c0 + f)
                turns, start = (FF // 2 - 1) // 2, st.n
                with dve.Fori(0, turns) as i:
                    st.n = i * 4 + start
                    for r in range(2):
                        c1, n = c0 + 2 + 3 * r, 2 * r + 2
                        swiglu(0, i * 4 + (e0 + n + 1), i * 6 + (c1 + 1))
                        nxt_in(c1, 0, i, 6)
                        hid(2 - 2 * r, 0, i * 4 + (b + n + 1))
                        swiglu(1, i * 4 + (e0 + n + 2), i * 6 + (c1 + 2))
                        hid(2 - 2 * r, 1, i * 4 + (b + n + 2))
                        nxt_in(c1, 1, i, 6)
                        nxt_in(c1, 2, i, 6)
                st.n = start + 4 * turns

            def mlp(name):
                c0, b = C[name], HID[name]
                hid_h, hid_l = hidden[name]

                def act_fn(bk, used, count):
                    dve.wait_ge(chunk_used, used)
                    V.scalar_tensor_tensor(out=t_ab[:, :, :], in0=two(bank[:, TURN + bk, :]), scalar=0.0,
                                           in1=r_two, op0=ALU.max, op1=ALU.mult).then_inc(ab_ready, 1)
                    dve.wait_ge(ab_ready, count)
                    V.tensor_tensor(hid_f[:, :, :], t_ab[:, :, :], t_ab[:, :, :], ALU.mult).then_inc(hid_full, 1)

                def hid(slot, count):
                    dve.wait_ge(hid_hi, count)
                    V.tensor_tensor(hid_l[:, 2 * slot:2 * slot + 2, :], hid_f[:, :, :],
                                    hid_h[:, 2 * slot:2 * slot + 2, :].bitcast(F32), ALU.subtract).then_inc(hid_lo, 1)

                for j in range(2):
                    act_fn(j, c0 + j + 1, b + j + 1)
                    hid(j, b + j + 1)
                    nxt(c0 + j)

                def step(r, i):
                    act_fn((r + 2) % 3, i * 6 + (c0 + 2 * r + 3), i * 3 + (b + r + 3))
                    nxt_in(c0 + 2, 2 * r, i, 6)
                    hid((r + 2) % 3, i * 3 + (b + r + 3))
                    nxt_in(c0 + 2, 2 * r + 1, i, 6)

                with dve.Fori(0, MLP_TURNS) as i:
                    for r in range(3):
                        step(r, i)
                for j in range(3 * MLP_TURNS, MF - 2):
                    step(j % 3, j // 3)
                nxt(c0 + 2 * MF - 2)

            def angles():
                R = slice(64, 96)
                two_pi = 2.0 * np.pi
                c1 = float(np.float32(6.28125))
                rest = two_pi - 6.28125
                c2 = float((np.array([rest], np.float32).view(np.uint32) & np.uint32(0xFFFFF000)).view(np.float32)[0])
                c3 = float(np.float32(rest - c2))
                dve.wait_ge(pos_in, 16)
                dve.wait_ge(con_in, 16)
                st.done(V.tensor_copy(t_a[R, :], pos_i[R, :]))
                st.done(V.tensor_scalar(t_a[R, :], t_a[R, :], con[R, CN["inv_freq"]:CN["inv_freq"] + 1], None, ALU.mult))
                for which, turn in ((1, 0.0), (0, 0.25)):
                    tab = rope_tab[R, which, :]
                    st.done(V.tensor_scalar(t_b[R, :], t_a[R, :], float(1.0 / two_pi), turn, ALU.mult, ALU.add))
                    st.done(V.tensor_scalar(t_b[R, :], t_b[R, :], 12582912.0, None, ALU.add))
                    st.done(V.tensor_scalar(t_b[R, :], t_b[R, :], 12582912.0, None, ALU.subtract))
                    st.done(V.scalar_tensor_tensor(out=tab, in0=t_b[R, :], scalar=-c1, in1=t_a[R, :],
                                                   op0=ALU.mult, op1=ALU.add))
                    st.done(V.scalar_tensor_tensor(out=tab, in0=t_b[R, :], scalar=-c2, in1=tab,
                                                   op0=ALU.mult, op1=ALU.add))
                    st.done(V.scalar_tensor_tensor(out=tab, in0=t_b[R, :], scalar=-c3, in1=tab,
                                                   op0=ALU.mult, op1=ALU.add))
                    if which == 0:
                        st.done(V.tensor_scalar(tab, tab, float(np.pi / 2), None, ALU.add))
                    pi = float(np.nextafter(np.float32(np.pi), np.float32(0)))
                    V.tensor_scalar(tab, tab, pi, -pi, ALU.min, ALU.max).then_inc(rope_ang, 1)

            dve.wait_ge(small_in, 16)
            dve.wait_ge(x_in, 16)
            split(0, 1)
            for j in range(4):
                operand_piece("ffn1", x_h, x_l, j)
            for c in range(1, RING):
                split(c, c + 1)
            sum_tiles("ffn1")
            factor("ffn1")
            ffn("ffn1")
            finish("ffn1", 0.5, "mix", x_h, x_l)

            factor("mix")
            dve.wait_ge(bias_mm, 1)
            V.tensor_copy(bias_1d[:, :], bank[0:16, 6, 0:384]).then_inc(bias_ready, 1)
            for j in range(3):
                dve.wait_ge(chunk_used, C["latent"] + j + 1)
                b = two(bank[:, TURN + j, :])
                if j < 2:
                    V.tensor_tensor(lat_raw[:, 2 * j:2 * j + 2, :], b, r_two, ALU.mult).then_inc(drained, 1)
                else:
                    V.tensor_tensor(lat_raw[:, 4, :], b[:, 0, :], r_sb[:, :], ALU.mult)
                    V.tensor_tensor(k_rope[0:ROPE, :], b[0:ROPE, 1, :], r_sb[0:ROPE, :], ALU.mult).then_inc(drained, 1)
                nxt(C["latent"] + j)
            angles()
            gained_lo(y_l[:, 0:2, :], lat_raw[:, 0:2, :], y_h[:, 0:2, :], "c_q", 0, 2)
            gained_lo(y_l[:, 2:3, :], lat_raw[:, 2:3, :], y_h[:, 2:3, :], "c_q", 2, 3)
            gained_lo(y_l[:, 3:5, :], lat_raw[:, 3:5, :], y_h[:, 3:5, :], "c_kv", 0, 2)
            dve.wait_ge(sq_ready, SQ["c_q"] + 1)
            st.done(V.tensor_tensor(sq[:, 0, :], sq[:, 0, :], sq[:, 1, :], ALU.add))
            V.tensor_tensor(sq[:, 0, :], sq[:, 0, :], sq[:, 2, :], ALU.add).then_inc(sum_ready, 1)
            dve.wait_ge(sq_ready, SQ["c_kv"] + 1)
            V.tensor_tensor(sq[:, 3, :], sq[:, 3, :], sq[:, 4, :], ALU.add).then_inc(sum_ready, 1)
            for j in range(4):
                c = C["sb_q"] + j
                dve.wait_ge(chunk_used, c + 1)
                b = two(bank[:, TURN + (DRAIN["sb"] + j) % 3, :])
                V.scalar_tensor_tensor(out=y_f[:, 2 * j:2 * j + 2, :], in0=b, scalar=0.125 if j < 2 else 1.0,
                                       in1=r_two, op0=ALU.mult, op1=ALU.mult).then_inc(drained, 1)
                nxt(c)
            rsqrt("c_q", bank[:, SUMS, 0:S], width=384, r_out=r_lat[:, 0, :])
            rsqrt("c_kv", bank[:, 3, 0:S], width=256, r_out=r_lat[:, 1, :], last=r_ready)
            dve.wait_ge(rt_mm, 1)
            st.done(V.tensor_copy(r_tok[:, 0, :], bank[:, SUMS, 0:256:128]))
            st.done(V.tensor_copy(r_tok[:, 1, :], bank[:, SUMS, 256:512:128]))
            dve.wait_ge(chunk_used, C["sb_v"] + 2)
            for t in range(2):
                V.tensor_scalar(sv[:, t, :], bank[:, t, :], r_tok[:, 0, t:t + 1], None, ALU.mult).then_inc(sv_done, 1)
            for j in range(2):
                nxt(C["sb_v"] + j)
            lat_two = [r_lat[:, i, :].rearrange("p (a b) -> p a b", a=1).to_broadcast([P, 2, S]) for i in range(2)]
            for j in range(2):
                dve.wait_ge(chunk_used, C["q_up"] + j + 1)
                for t in range(2):
                    hd = 4 * j + 2 * t
                    V.tensor_tensor(heads[0:QK, hd:hd + 2, :], two(bank[0:QK, 2 * j + t, :]), lat_two[0][0:QK],
                                    ALU.mult).then_inc(qk_raw, 1)
                nxt(C["q_up"] + j)
            dve.wait_ge(chunk_used, C["kv_up"] + 1)
            V.tensor_copy(heads[64:96, 8:16, :], k_rope[0:ROPE, :].rearrange("p (a b) -> p a b", a=1).to_broadcast([ROPE, 8, S])).then_inc(qk_raw, 1)
            for t in range(2):
                b = two(bank[:, 4 + t, :])
                for e in range(2):
                    k = heads[0:NOPE, 8 + 4 * t + e:8 + 4 * t + e + 3:2, :]
                    rows = slice(64 * e, 64 * e + 64)
                    V.tensor_tensor(k, b[rows], lat_two[1][rows], ALU.mult).then_inc(qk_raw, 1)
            for t in range(2):
                V.tensor_scalar(mv[:, t, :], bank[:, 6 + t, :], r_tok[:, 1, t:t + 1], None, ALU.mult).then_inc(qk_raw, 1)
            nxt(C["kv_up"])

            def gates_in(j):
                dve.wait_ge(chunk_used, C["gates"] + j + 1)
                V.tensor_tensor(gate[:, 2 * j:2 * j + 2, :], two(bank[:, 6 + j % 2, :]), r_two,
                                ALU.mult).then_inc(drained, 1)
                nxt(C["gates"] + j)

            for j in range(2):
                gates_in(j)
            rsqrt("head", bank[0:16, 0, 0:S], slice(0, 16), QK, t_b[0:16, :], r_head)
            gates_in(2)

            def rope(p):
                y = heads[64:96, 2 * p:2 * p + 2, :]
                dve.wait_ge(rot_ready, p + 1)
                if p >= 1:
                    dve.wait_ge(roped, p)
                b = bank[64:96, bcb(p), :].rearrange("p (a b) -> p a b", a=2)
                sin = rope_tab[64:96, 1:2, :].to_broadcast([32, 2, S])
                st.done(V.tensor_tensor(hid_f[64:96, :, :], b, sin, ALU.mult))
                dve.wait_ge(rope_cos, p + 1)
                V.tensor_tensor(y, hid_f[64:96, :, :], v_pad[64:96, :, 0:S], ALU.add).then_inc(roped, 1)

            dve.wait_ge(rope_sin, 2)
            for p in range(8):
                dve.wait_ge(bc_ready, p + 1)
                b = bank[0:QK, bcb(p), :].rearrange("p (a b) -> p a b", a=2)
                y = heads[0:QK, 2 * p:2 * p + 2, :]
                V.scalar_tensor_tensor(out=y, in0=y, scalar=col("q_head" if p < 4 else "k_head")[0:QK], in1=b,
                                       op0=ALU.mult, op1=ALU.mult).then_inc(normed, 1)
                if p >= 1:
                    rope(p - 1)
            rope(7)
            gates_in(3)

            for hd in range(HEADS + 1):
                o = 4 * (hd % 2)
                if hd < HEADS:
                    dve.wait_ge(s_z, hd + 1)
                    dve.wait_ge(s_abs, hd + 1)
                    V.tensor_scalar(s_m, bank[:, 1, 0:384], -1.0, 0.0, ALU.mult, ALU.min).then_inc(s_min, 1)
                    dve.wait_ge(m_scores, hd + 1)
                    mp = m_p[hd % 2]
                    if hd >= 2:
                        dve.wait_ge(m_pt, hd - 1)
                    for q in range(2):
                        c = slice(0, 128) if q == 0 else slice(128, 384)
                        neg = cst("mla_neg", 128, 128) if q == 0 else cst("mla_neg", 256)
                        st.inc(V.tensor_tensor_reduce(mp[:, c], bank[:, 0, c], neg, 1.0, -3e38, ALU.add, ALU.max,
                                                      stat[:, o + q:o + q + 1]))
                    st.wait()
                    V.tensor_scalar(stat[:, 8 + o:10 + o], stat[:, o:o + 2], -float(QK) ** -0.5, None,
                                    ALU.mult).then_inc(m_max, 1)
                if hd >= 1:
                    dve.wait_ge(s_e, hd)
                    if hd >= 3:
                        dve.wait_ge(s_pv, hd - 2)
                    V.tensor_tensor(s_p[(hd - 1) % 2], bank[:, 3, 0:384], cst("sb_neg", 384), ALU.add).then_inc(s_x, 1)
                    dve.wait_ge(m_pt, hd)
                    if hd >= 3:
                        dve.wait_ge(m_pv, 2 * (hd - 2))
                    V.tensor_copy(m_t[(hd - 1) % 2], bank[:, 2, 0:384]).then_inc(m_ptc, 1)
                if hd < HEADS:
                    dve.wait_ge(s_ln, hd + 1)
                    dve.wait_ge(s_min, hd + 1)
                    if hd >= 1:
                        dve.wait_ge(s_e, hd)
                    st.done(V.tensor_tensor(s_lm, s_m, s_t2, ALU.subtract))
                    lm = s_lm.rearrange("p (a b) -> p a b", a=3)[:, 0:3:2, :]
                    one = con[:, CN["tri"]:CN["tri"] + P].rearrange("p (a b) -> p a b", a=1).to_broadcast([P, 2, P])
                    st.done(V.tensor_tensor(s_m.rearrange("p (a b) -> p a b", a=3)[:, 0:3:2, :], lm, one, ALU.mult))
                    V.tensor_tensor(lm, lm, s_m.rearrange("p (a b) -> p a b", a=3)[:, 0:3:2, :],
                                    ALU.subtract).then_inc(s_l, 1)
                    dve.wait_ge(m_exp, 2 * hd + 2)
                    st.done(V.reciprocal(stat[:, 24 + o:26 + o], stat[:, 16 + o:18 + o]))
                    V.tensor_scalar(mp[:, 0:128], mp[:, 0:128], stat[:, 24 + o:25 + o], None, ALU.mult)
                    V.tensor_scalar(mp[:, 128:384], mp[:, 128:384], stat[:, 25 + o:26 + o], None,
                                    ALU.mult).then_inc(m_prob, 1)
                if hd % 2 == 1:
                    gates_in(4 + hd // 2)
                if hd >= 2 and hd % 2 == 0:
                    t = hd // 2 - 1
                    lo(y_l[:, t:8:4, :], two(bank[:, 4 + t % 2, :]), y_h[:, t:8:4, :])
            for half in range(2):
                for t in range(2):
                    m = 4 * half + t
                    j = 2 * half + t
                    dve.wait_ge(chunk_used, C["branch"] + 2 * half + 1)
                    dve.wait_ge(gates_done, 4)
                    if j >= 1:
                        dve.wait_ge(merged_done, j)
                    st.done(V.tensor_tensor(hid_f[:, :, :], two(bank[:, m, :]), gate[:, 2 * j:2 * j + 2, :], ALU.mult))
                    dve.wait_ge(chunk_used, C["branch"] + 2 * half + 2)
                    st.done(V.tensor_tensor(sq[:, 0:2, :], two(bank[:, m + 2, :]), gate[:, 8 + 2 * j:10 + 2 * j, :], ALU.mult))
                    V.tensor_tensor(x_f[:, 2 * j:2 * j + 2, :], hid_f[:, :, :], sq[:, 0:2, :],
                                    ALU.add).then_inc(merged_done, 1)
                for j in range(2 * half, 2 * half + 2):
                    lo(x_l[:, 2 * j:2 * j + 2, :], x_f[:, 2 * j:2 * j + 2, :], x_h[:, 2 * j:2 * j + 2, :])
                for j in range(2 * half, 2 * half + 2):
                    nxt(C["branch"] + j)

            project_out("w_out", "ffn2", y_h, y_l)
            factor("ffn2")
            lo(x_l[:, 0:2, :], heads[:, 0:2, :], x_h[:, 0:2, :])
            ffn("ffn2")
            finish("ffn2", 0.5, "ple", y_h, y_l)

            factor("ple", 3)
            nxt(C["ple_proj"])
            c = C["ple_gate"]
            for j in range(4):
                y, hj = y_f[:, 2 * j:2 * j + 2, :], h[:, 2 * j:2 * j + 2, :]
                dve.wait_ge(chunk_used, c + j + 1)
                V.tensor_tensor(y, two(bank[:, ACC + j, :]), r_two, ALU.mult).then_inc(ple_raw, 1)
                if j >= 1:
                    operand_piece("mix0", x_h, x_l, j - 1)
                dve.wait_ge(ple_sig, j + 1)
                st.done(V.tensor_tensor(y, two(bank[:, 4 + j, :]), y, ALU.mult))
                V.tensor_tensor(hj, hj, y, ALU.add).then_inc(h_upd, 1)
                if j < 3:
                    nxt(c + j)
            operand_piece("mix0", x_h, x_l, 3)
            sum_tiles("mix0")
            nxt(c + 3)

            factor("mix0")
            n = st.n
            dve.wait_ge(setup, 5)
            with dve.Fori(0, 4) as i:
                c0 = C["conv_in"]
                st.n = i * 8 + n
                for j in range(2):
                    dve.wait_ge(chunk_used, i * 3 + (c0 + j + 1))
                    V.tensor_tensor(t_ab[:, :, :], two(bank[:, TURN + j, :]), r_two, ALU.mult).then_inc(drained, 1)
                    dve.wait_ge(drained, i * 3 + (DRAIN["conv"] + j + 1))
                    st.done(V.tensor_tensor(v_pad[:, j, 2:S + 2], t_ab[:, 0, :], t_ab[:, 1, :], ALU.mult))
                    nxt_in(c0, j, i, 3)
                    for k in range(3):
                        tap = 2 - k
                        w = par[:, bass.ds(i * 2 + (SM["conv_w"] + 8 * tap + j), 1)]
                        src = v_pad[:, j, tap:tap + S]
                        if k == 0:
                            st.done(V.tensor_scalar(hid_f[:, j, :], src, w, None, ALU.mult))
                        else:
                            st.done(V.scalar_tensor_tensor(out=hid_f[:, j, :], in0=src, scalar=w,
                                                           in1=hid_f[:, j, :], op0=ALU.mult, op1=ALU.add))
                dve.wait_ge(chunk_used, i * 3 + (c0 + 3))
                V.tensor_tensor(t_ab[:, :, :], two(bank[:, TURN + 2, :]), r_two, ALU.mult).then_inc(drained, 1)
                dve.wait_ge(drained, i * 3 + (DRAIN["conv"] + 3))
                V.tensor_tensor(y_f[:, bass.ds(i * 2, 2), :], t_ab[:, :, :], hid_f[:, :, :],
                                ALU.mult).then_inc(conv_full, 1)
                dve.wait_ge(op_hi, i + (PC["conv"] + 1))
                V.tensor_tensor(y_l[:, bass.ds(i * 2, 2), :], y_f[:, bass.ds(i * 2, 2), :],
                                y_h[:, bass.ds(i * 2, 2), :].bitcast(F32), ALU.subtract).then_inc(op_lo, 1)
                nxt_in(c0, 2, i, 3)
            st.n = n + 32
            made[0] += 4

            project_out("conv_out", "mlp0", x_h, x_l)
            factor("mlp0")
            mlp("mlp0")
            finish("mlp0", 1.0, "kv", x_h, x_l)

            rsqrt("kv", bank[:, SUMS, 0:S], r_out=r_sb[:, :], last=r_ready)
            dve.wait_ge(r_ready, 2)
            for w in range(2):
                dve.wait_ge(chunk_used, C["kv_raw"] + w + 1)
                if w == 1:
                    dve.wait_ge(blk_ready, 4)
                V.tensor_tensor(t_ab[:, :, :], two(bank[:, TURN + w, :]), r_two, ALU.mult).then_inc(kv_done, 1)
                dve.wait_ge(kv_done, w + 1)
                pe = col("pe_k" if w == 0 else "pe_v", 0, 16)
                for half in range(2):
                    for e in range(2):
                        rows = slice(64 * half, 64 * half + 64)
                        src = t_ab[64 * e:64 * e + 64, :, :].rearrange("p a (n l) -> p l a n", l=16)
                        dst = y_flat[rows, 960 * w:960 * w + 960].rearrange("p (l g n) -> p l g n", l=16, g=4)
                        for t in range(2):
                            ins = V.tensor_tensor(dst[:, :, 2 * t + e, :], src[:, :, t, half:half + NCMP],
                                                  pe[rows, :].rearrange("p (l n) -> p l n", n=1).to_broadcast([64, 16, NCMP]),
                                                  ALU.add)
                        ins.then_inc(blk_ready, 1)
                nxt(C["kv_raw"] + w)
                for j in range(2 * w, 2 * w + 2):
                    operand_piece("mix1", y_h, y_l, j)
            for w in range(2):
                dve.wait_ge(chunk_used, C["k_att"] + w + 1)
                V.tensor_tensor((n_ks, n_kw)[w], two(bank[:, (6, 0)[w], :]), r_two, ALU.mult).then_inc(kv_done, 1)
                nxt(C["k_att"] + w)
            dve.wait_ge(rt_mm, 2)
            st.done(V.tensor_copy(r_tok[:, 0, :], bank[:, SUMS, 0:256:128]))
            for w in range(2):
                dve.wait_ge(chunk_used, C["v_att"] + w + 1)
                for t in range(2):
                    V.tensor_scalar((n_vs, n_vw)[w][:, t, :], bank[:, (1, 2)[w], t * 256:t * 256 + 256],
                                    r_tok[:, 0, t:t + 1], None, ALU.mult).then_inc(kv_done, 1)
                nxt(C["v_att"] + w)
            lo(x_lf[:, 0:960], y_flat[:, 0:960], x_hf[:, 0:960])
            lo(x_lf[:, 960:1920], y_flat[:, 960:1920], x_hf[:, 960:1920])
            for j in range(4):
                dve.wait_ge(chunk_used, C["nsa_q"] + j + 1)
                V.scalar_tensor_tensor(out=n_q[:, 2 * j:2 * j + 2, :], in0=two(bank[:, TURN + j % 3, :]), scalar=0.125,
                                       in1=r_two, op0=ALU.mult, op1=ALU.mult).then_inc(q_done, 1)
                nxt(C["nsa_q"] + j)
            dve.wait_ge(chunk_used, C["nsa_gate"] + 1)
            for t in range(2):
                ins = V.tensor_scalar(nsa_g[:, t, :], bank[:, SUMS, t * 48:t * 48 + 48], r_tok[:, 0, t:t + 1], None,
                                      ALU.mult)
            ins.then_inc(g_raw, 1)
            nxt(C["nsa_gate"])
            dve.wait_ge(g_sig, 1)
            g0 = nsa_g[:, 0, 0:48:3]
            st.done(V.tensor_scalar(g0, g0, cst("has_any", 1), None, ALU.mult))
            V.memset(mv[:, 1, 0:64], 0.0)
            for w in range(2):
                nxt(C["phi"] + w)
            for w in range(2):
                dve.wait_ge(phi_sig, w + 1)
                V.tensor_tensor(phi_h[:, w, :], bank[0:60, (7, 3)[w], 0:256], t_exp[0:60, :],
                                ALU.mult).then_inc(phi_hid, 1)
            dve.wait_ge(phi_t, 1)
            V.tensor_copy(sv[:, 0, 0:240], bank[:, 0, 0:240]).then_inc(phi_hid, 1)
            dve.wait_ge(phi_mm, 1)
            for e in range(2):
                rows = slice(64 * e, 64 * e + 64)
                src = bank[rows, 1, 0:32].rearrange("p (a b) -> p a b", a=2)
                ins = V.tensor_copy(k_cmp[rows, :, e, 0:NCMP], src[:, :, 0:NCMP])
            ins.then_inc(cmp_done, 1)
            for g in range(4):
                rows = slice(32 * g, 32 * g + NCMP)
                ins = V.tensor_copy(v_cmp[rows, :], bank[rows, 1, 64:128])
            ins.then_inc(cmp_done, 1)

            dve.wait_ge(bias_in, 16)
            c_max, c_sum, c_rec, c_fac = (c_stat[:, m, :, :] for m in range(4))
            by_head = lambda ap: ap.rearrange("p (t g) -> p t g", t=4)
            for k in range(G_HEADS + 2):
                if k < G_HEADS:
                    o = 16 * (k % 3)
                    bias = gate_or_bias[:, NSA_ORDER[k], :]
                    dve.wait_ge(n_scores, k + 1)
                    if k >= 3:
                        dve.wait_ge(n_pt, 2 * (k - 2))
                    a, b = bank[:, 4 - 2 * (k % 2), :], bank[:, 5 - 2 * (k % 2), :]
                    for m, (dst, src) in enumerate(zip(n_parts(k), (a[:, 0:256], a[:, 256:512], b[:, 0:128],
                                                                    b[:, 128:256]))):
                        st.inc(V.tensor_tensor_reduce(dst, src, bias if m < 2 else bias[:, 128:256], 1.0, -3e38,
                                                      ALU.add, ALU.max, stat[:, o + m:o + m + 1]))
                    st.wait()
                    V.tensor_scalar(stat[:, o + 4:o + 8], stat[:, o:o + 4], -1.0, None, ALU.mult).then_inc(n_max, 1)
                if 1 <= k <= G_HEADS:
                    g, o = k - 1, 16 * ((k - 1) % 3)
                    dve.wait_ge(n_exp, 4 * k)
                    st.done(V.reciprocal(stat[:, o + 12:o + 16], stat[:, o + 8:o + 12]))
                    for m, ap in enumerate(n_parts(g)):
                        at = 3 * NSA_ORDER[g] + 1 + m % 2
                        ins = V.tensor_scalar(ap, ap, stat[:, o + 12 + m:o + 13 + m],
                                              nsa_g[:, 1 - m // 2, at:at + 1], ALU.mult, ALU.mult)
                    ins.then_inc(n_prob, 1)
                if k == 0:
                    dve.wait_ge(c_scores, 1)
                    dve.wait_ge(setup, 6)
                    for q in range(2):
                        c = c_p[:, q, :, :, 0:c_n[q]]
                        first = (159, 31)[q]
                        bs = gate_or_bias[:, :, first:256:16].rearrange("p (g t) n -> p t g n", g=4)
                        src = bank[:, q, :].rearrange("p (t g n) -> p t g n", t=4, g=4)[:, :, :, 0:c_n[q]]
                        st.done(V.tensor_tensor(c, src, bs, ALU.add))
                        st.done(V.tensor_reduce(by_head(c_max[:, q, :]), c, AX.X, ALU.max))
                        mx = c_max[:, q, :].rearrange("p (t g n) -> p t g n", t=4, n=1).to_broadcast([P, 4, 4, c_n[q]])
                        V.tensor_tensor(c, c, mx, ALU.subtract).then_inc(c_sub, 1)
                if k >= 2:
                    dve.wait_ge(n_pt, 2 * k - 2)
                    if k >= 4:
                        dve.wait_ge(n_pv, k - 3)
                    V.tensor_copy(n_t[k % 2][:, 512:768], bank[:, 7, 0:256]).then_inc(n_ptd, 1)
                if k == 2:
                    dve.wait_ge(c_pt, 1)
                    V.tensor_copy(c_t[:, 0:512], bank[:, 0, :]).then_inc(c_ptc, 1)
                if k in (4, 5):
                    nxt(C["phi"] + k - 2)
                if k == 1:
                    dve.wait_ge(c_exp, 2)
                    for q in range(2):
                        c = c_p[:, q, :, :, 0:c_n[q]]
                        st.done(V.tensor_reduce(by_head(c_sum[:, q, :]), c, AX.X, ALU.add))
                    st.done(V.reciprocal(c_rec, c_sum))
                    for q in range(2):
                        g0 = nsa_g[:, q, 0:48:3].rearrange("p (g t) -> p t g", g=4)
                        st.done(V.tensor_tensor(by_head(c_fac[:, q, :]), by_head(c_rec[:, q, :]), g0, ALU.mult))
                        c = c_p[:, q, :, :, 0:c_n[q]]
                        fac = c_fac[:, q, :].rearrange("p (t g n) -> p t g n", t=4, n=1).to_broadcast([P, 4, 4, c_n[q]])
                        V.tensor_tensor(c, c, fac, ALU.mult).then_inc(c_prob, 1)
                if k % 4 == 3 and k >= 7:
                    m = k // 4 - 1
                    lo(y_l[:, 2 * m:2 * m + 2, :], two(bank[:, m % 2, :]), y_h[:, 2 * m:2 * m + 2, :])
            lo(y_l[:, 6:8, :], two(bank[:, 1, :]), y_h[:, 6:8, :])
            project_out("nsa_out", "mlp1", x_h, x_l)
            factor("mlp1")
            mlp("mlp1")
            finish("mlp1", 1.0, "final", None, None)
            factor("final")
            for t in range(KT):
                ins = V.scalar_tensor_tensor(out=x_f[:, t, :], in0=h[:, t, :], scalar=col("final", t),
                                             in1=r_sb[:, :], op0=ALU.mult, op1=ALU.mult)
                if t % 2 == 1:
                    ins.then_inc(y_ready, 1)

        @block.tensor
        def _(pe):
            mm = nc.tensor.matmul

            def product(out_, s, c, m, hi_, lo_, start, stop, **kw):
                mm(out_, w_hi[:, s, c:c + m], hi_, start=start, stop=False, **kw)
                mm(out_, w_hi[:, s, c:c + m], lo_, start=False, stop=False, **kw)
                return mm(out_, w_lo[:, s, c:c + m], hi_, start=False, stop=stop, **kw)

            def arrived(count):
                pe.wait_ge(lo_split, count)

            def pair(s, bk, hi_, lo_, pieces=None):
                if pieces is None:
                    for t in range(2):
                        for k in range(KT):
                            last = product(bank[:, bk, t * S:(t + 1) * S], s, k * 256 + t * P, P, hi_[:, k, :],
                                           lo_[:, k, :], k == 0, k == KT - 1)
                    return last
                for p in range(KT // 2):
                    pe.wait_ge(op_lo, pieces + p + 1)
                    for t in range(2):
                        for k in range(2 * p, 2 * p + 2):
                            last = product(bank[:, bk, t * S:(t + 1) * S], s, k * 256 + t * P, P, hi_[:, k, :],
                                           lo_[:, k, :], k == 0 and t == 0, k == KT - 1, skip_group_check=True)
                return last

            def tokens(s, bk, width, kts, hi_, lo_, base, first, last_):
                for t in range(2):
                    for n, k in enumerate(kts):
                        tok = slice(t * P, t * P + P)
                        c = base + n * width if isinstance(base, int) else base[n]
                        o = bk(t)
                        a, b = hi_[:, k, tok], lo_[:, k, tok]
                        wh, wl = w_hi[:, s, c:c + width], w_lo[:, s, c:c + width]
                        kw = dict(skip_group_check=True)
                        mm(o, a, wh, start=first and n == 0, stop=False, **kw)
                        mm(o, a, wl, start=False, stop=False, **kw)
                        ins = mm(o, b, wh, start=False, stop=last_ and n == len(kts) - 1, **kw)
                return ins

            def sum_squares(count, bk=SUMS, tile=0):
                pe.wait_ge(sum_ready, count)
                mm(bank[:, bk, 0:S], ones[:, :], sq[:, tile, :], start=True, stop=True).then_inc(ss_ready, 1)

            def transposed_factors(c, *srcs):
                pe.wait_ge(r_ready, c)
                for n, src in enumerate(srcs):
                    for t in range(2):
                        ins = nc.tensor.transpose(bank[:, SUMS, 256 * n + P * t:256 * n + P * t + P],
                                                  src[:, P * t:P * t + P], ident)
                ins.then_inc(rt_mm, 1)

            def clear_acc():
                for j in range(4):
                    mm(bank[:, ACC + j, :], zeros[:, 0:P], zeros[:, :], start=True, stop=True)

            def down(s, hid, slot, last=False):
                for o in range(KT):
                    for f in range(2):
                        ins = product(bank[:, ACC + o // 2, (o % 2) * S:(o % 2) * S + S], s, f * D + o * P, P,
                                      hid[0][:, slot + f, :], hid[1][:, slot + f, :], False, last,
                                      skip_group_check=True)
                    if last and o in (1, 3, 5):
                        ins.then_inc(acc_ready, 1)
                ins.then_inc(chunk_used, 1)

            def ffn(name, piece, x_h, x_l, norm_no):
                c0, b = C[name], HID[name]
                if name == "ffn1":
                    pe.wait_ge(setup, 4)
                for f in range(2):
                    arrived(c0 + f + 1)
                    pair((c0 + f) % RING, TURN + f, x_h, x_l, piece if f == 0 else None).then_inc(chunk_used, 1)
                    if f == 0:
                        clear_acc()
                        sum_squares(norm_no)
                with pe.Fori(0, (FF // 2 - 1) // 2) as i:
                    for r in range(2):
                        c1 = c0 + 2 + 3 * r
                        for f in range(2):
                            arrived(i * 6 + (c1 + f + 1))
                            pe.wait_ge(ab_ready, i * 4 + (b + 2 * r + f + 1))
                            pair((c1 + f) % RING, TURN + f, x_h, x_l).then_inc(chunk_used, 1)
                        arrived(i * 6 + (c1 + 3))
                        pe.wait_ge(hid_lo, i * 4 + (b + 2 * r + 2))
                        down((c1 + 2) % RING, hidden[name], 2 * r)
                last = c0 + FF + FF // 2 - 1
                arrived(last + 1)
                pe.wait_ge(hid_lo, b + FF)
                down(last % RING, hidden[name], 0, True)

            def mlp(name, piece, norm_no):
                c0, b = C[name], HID[name]
                for j in range(2):
                    arrived(c0 + j + 1)
                    pair((c0 + j) % RING, TURN + j, x_h, x_l, piece if j == 0 else None).then_inc(chunk_used, 1)
                    if j == 0:
                        clear_acc()
                        sum_squares(norm_no)

                def step(r, i):
                    c = c0 + 2 + 2 * r
                    arrived(i * 6 + (c + 1))
                    pe.wait_ge(ab_ready, i * 3 + (b + r))
                    pair(c % RING, TURN + (r + 2) % 3, x_h, x_l).then_inc(chunk_used, 1)
                    arrived(i * 6 + (c + 2))
                    pe.wait_ge(hid_lo, i * 3 + (b + r + 1))
                    down((c + 1) % RING, hidden[name], 2 * r)

                with pe.Fori(0, MLP_TURNS) as i:
                    for r in range(3):
                        step(r, i)
                for j in range(3 * MLP_TURNS, MF - 2):
                    step(j % 3, j // 3)
                for j in range(MF - 2, MF):
                    c = c0 + MF + j
                    arrived(c + 1)
                    pe.wait_ge(hid_lo, b + j + 1)
                    down(c % RING, hidden[name], 2 * (j % 3), j == MF - 1)

            def project(name, banks, hi_, lo_, piece, waits=None):
                for j, bk in enumerate(banks):
                    c = C[name] + j
                    arrived(c + 1)
                    if waits is not None and waits[j] is not None:
                        pe.wait_ge(drained, waits[j])
                    pair(c % RING, bk, hi_, lo_, piece if j == 0 else None).then_inc(chunk_used, 1)

            ffn("ffn1", PC["ffn1"], x_h, x_l, 1)
            pe.wait_ge(con_in, 16)
            pe.wait_ge(relb_in, 16)
            mm(bank[0:16, 6, 0:384], relb[:, :], con[0:33, CN["bucket"]:CN["bucket"] + 384], start=True,
               stop=True).then_inc(bias_mm, 1)

            project("latent", [TURN], x_h, x_l, PC["mix"])
            sum_squares(2)
            for j in range(1, 3):
                c = C["latent"] + j
                arrived(c + 1)
                if j == 2:
                    pe.wait_ge(bias_ready, 1)
                pair(c % RING, TURN + j, x_h, x_l).then_inc(chunk_used, 1)
            project("sb_q", [TURN, TURN + 1], x_h, x_l, None, [1, 2])
            project("sb_k", [TURN + 2, TURN], x_h, x_l, None, [3, 4])
            sum_squares(3)
            sum_squares(4, 3, 3)
            for j in range(2):
                arrived(C["sb_v"] + j + 1)
                tokens((C["sb_v"] + j) % RING, lambda t: bank[:, t, :], 512, range(4 * j, 4 * j + 4), x_h, x_l, 0,
                       j == 0, j == 1).then_inc(chunk_used, 1)
            transposed_factors(1, r_sb, r_lat[:, 1, :])
            for j in range(2):
                arrived(C["q_up"] + j + 1)
                if j == 0:
                    pe.wait_ge(sv_done, 2)
                s = (C["q_up"] + j) % RING
                for hh in range(4):
                    o = bank[0:QK, 2 * j + hh // 2, (hh % 2) * S:(hh % 2) * S + S]
                    for k in range(3):
                        last = product(o, s, k * 384 + hh * QK, QK, y_h[:, k, :], y_l[:, k, :], k == 0, k == 2)
                last.then_inc(chunk_used, 1)
            arrived(C["kv_up"] + 1)
            s = C["kv_up"] % RING
            for t in range(4):
                for k in range(2):
                    product(bank[:, 4 + t // 2, (t % 2) * S:(t % 2) * S + S], s, k * D + t * P, P, y_h[:, 3 + k, :],
                            y_l[:, 3 + k, :], k == 0, k == 1)
            tokens(s, lambda t: bank[:, 6 + t, :], 512, (3, 4), y_h, y_l, [512, D + 512], True,
                   True).then_inc(chunk_used, 1)

            def gate_unit(u):
                j, t = u // 2, u % 2
                c = C["gates"] + j
                if t == 0:
                    arrived(c + 1)
                    if j >= 2:
                        pe.wait_ge(drained, DRAIN["gates"] + j - 1)
                for k in range(KT):
                    last = product(bank[:, 6 + j % 2, t * S:(t + 1) * S], c % RING, k * 256 + t * P, P, x_h[:, k, :],
                                   x_l[:, k, :], k == 0, k == KT - 1)
                if t == 1:
                    last.then_inc(chunk_used, 1)

            pe.wait_ge(qk_raw, 11)
            for u in range(4):
                gate_unit(u)

            for hd in range(16):
                p = hd // 2
                pe.wait_ge(sq_ready, SQ["head"] + p + 1)
                src = (sq if p < 4 else x_f)[0:QK, 2 * (p % 4) + hd % 2, :]
                pick = con[0:QK, CN["pick"] + 15 - hd:CN["pick"] + 31 - hd]
                ins = mm(bank[0:16, 0, 0:S], pick, src, start=hd == 0, stop=hd == 15)
            ins.then_inc(ss_ready, 1)
            gate_unit(4)
            gate_unit(5)
            pe.wait_ge(r_head, 1)

            def rotate(p):
                pe.wait_ge(normed, p + 1)
                mm(bank[64:96, bcb(p), :], con[64:96, CN["rot"]:CN["rot"] + 32],
                   heads[64:96, 2 * p:2 * p + 2, :].rearrange("p a b -> p (a b)"), start=True,
                   stop=True).then_inc(rot_ready, 1)

            for p in range(8):
                if p >= 6:
                    pe.wait_ge(roped, p - 5)
                for e in range(2):
                    hd = 2 * p + e
                    row = con[0:16, CN["ident"] + hd:CN["ident"] + hd + 1].to_broadcast([16, QK])
                    ins = mm(bank[0:QK, bcb(p), e * S:e * S + S], row, t_b[0:16, :], start=True, stop=True)
                ins.then_inc(bc_ready, 1)
                if p >= 1:
                    rotate(p - 1)
            rotate(7)
            gate_unit(6)
            gate_unit(7)

            pe.wait_ge(roped, 8)
            for hd in range(HEADS + 1):
                if hd < HEADS:
                    if hd >= 1:
                        pe.wait_ge(m_max, hd)
                    q, k = heads[0:QK, hd, :], heads[0:QK, 8 + hd, :]
                    mm(bank[:, 0, 0:128], q[:, 0:128], k[:, 0:128], start=True, stop=True)
                    mm(bank[:, 0, 128:384], q[:, 128:256], k, start=True, stop=True).then_inc(m_scores, 1)
                    if hd >= 1:
                        pe.wait_ge(s_min, hd)
                    r = slice(64 * (hd % 2), 64 * (hd % 2) + 64)
                    q, k = sb_q[r, hd // 2, :], sb_k[r, hd // 2, :]
                    mm(bank[:, 1, 0:256], k[:, 0:128], q, start=True, stop=True)
                    mm(bank[:, 1, 256:384], k[:, 128:256], q[:, 128:256], start=True, stop=True).then_inc(s_z, 1)
                    gate_unit(8 + hd)
                if hd >= 1:
                    g = hd - 1
                    r = slice(64 * (g % 2), 64 * (g % 2) + 64)
                    q, k = sb_q[r, g // 2, :], sb_k[r, g // 2, :]
                    if g >= 1:
                        pe.wait_ge(s_x, g)
                        pe.wait_ge(m_ptc, g)
                    pe.wait_ge(s_l, g + 1)
                    e = bank[:, 3, :]
                    kw = dict(skip_group_check=True)
                    mm(e[:, 0:256], k[:, 0:128], q, start=True, stop=False, **kw)
                    mm(e[:, 256:384], k[:, 128:256], q[:, 128:256], start=False, stop=False, **kw)
                    mm(e[:, 0:384], cst("tri", P), s_lm, start=False, stop=False, **kw)
                    mm(e[:, 128:256], ones[:, :], s_lm[:, 256:384], start=False, stop=True, **kw).then_inc(s_e, 1)
                    pe.wait_ge(m_prob, g + 1)
                    mp, b2 = m_p[g % 2], bank[:, 2, :]
                    for blk in range(3):
                        ins = nc.tensor.transpose(b2[:, blk * P:blk * P + P], mp[:, blk * P:blk * P + P], ident)
                    ins.then_inc(m_pt, 1)
                    cols = slice(g * 64, g * 64 + 64)
                    ob = 4 + g // 2 % 2
                    pe.wait_ge(m_ptc, g + 1)
                    if g >= 4 and g % 2 == 0:
                        pe.wait_ge(op_lo, PC["o"] + g // 2 - 1)
                    om, mt = bank[r, ob, 0:S], m_t[g % 2]
                    mm(om, mv[:, 0, cols], mt[:, 0:256], start=True, stop=False).then_inc(m_pv, 1)
                    mm(om[:, 128:256], mv[:, 1, cols], mt[:, 256:384], start=False, stop=True).then_inc(m_pv, 1)
                    pe.wait_ge(s_a, g + 1)
                    os, sp_ = bank[r, ob, S:2 * S], s_p[g % 2]
                    mm(os, sv[:, 0, cols], sp_[:, 0:256], start=True, stop=False)
                    mm(os[:, 128:256], sv[:, 1, cols], sp_[:, 256:384], start=False, stop=True).then_inc(s_pv, 1)

            for half in range(2):
                for w in range(2):
                    c = C["branch"] + 2 * half + w
                    arrived(c + 1)
                    pe.wait_ge(op_lo, PC["o"] + 4)
                    for o in range(4):
                        dst = bank[:, 4 * half + 2 * w + o // 2, (o % 2) * S:(o % 2) * S + S]
                        for k in range(4):
                            last = product(dst, c % RING, k * 512 + o * P, P, y_h[:, 4 * w + k, :],
                                           y_l[:, 4 * w + k, :], k == 0, k == 3)
                    last.then_inc(chunk_used, 1)
            project("w_out", range(4), x_h, x_l, PC["merged"])

            ffn("ffn2", PC["ffn2"], y_h, y_l, 5)

            arrived(C["ple_proj"] + 1)
            for o in range(KT):
                for k in range(2):
                    last = product(bank[:, 4 + o // 2, (o % 2) * S:(o % 2) * S + S], C["ple_proj"] % RING,
                                   k * D + o * P, P, x_h[:, k, :], x_l[:, k, :], k == 0, k == 1)
            last.then_inc(chunk_used, 1)
            project("ple_gate", [0], y_h, y_l, PC["ple"])
            sum_squares(6, 3)
            for j in range(1, 4):
                c = C["ple_gate"] + j
                arrived(c + 1)
                if j == 3:
                    pe.wait_ge(ms_ready, NO["ple"] + 1)
                pair(c % RING, j, y_h, y_l).then_inc(chunk_used, 1)

            c = C["conv_in"]
            for j in range(3):
                arrived(c + j + 1)
                pair((c + j) % RING, TURN + j, x_h, x_l, PC["mix0"] if j == 0 else None).then_inc(chunk_used, 1)
                if j == 0:
                    sum_squares(7)
            with pe.Fori(1, 4) as i:
                for j in range(3):
                    arrived(i * 3 + (c + j + 1))
                    pe.wait_ge(drained, i * 3 + (DRAIN["conv"] + j - 2))
                    pair((c + j) % RING, TURN + j, x_h, x_l).then_inc(chunk_used, 1)
            project("conv_out", range(4), y_h, y_l, PC["conv"])
            mlp("mlp0", PC["mlp0"], 8)

            project("kv_raw", [TURN], x_h, x_l, PC["kv"])
            sum_squares(9)
            c = C["kv_raw"] + 1
            arrived(c + 1)
            pair(c % RING, TURN + 1, x_h, x_l).then_inc(chunk_used, 1)
            project("k_att", [6, 0], x_h, x_l, None)
            transposed_factors(2, r_sb)
            for w in range(2):
                c = C["v_att"] + w
                arrived(c + 1)
                tokens(c % RING, lambda t: bank[:, 1 + w, t * 256:t * 256 + 256], 256, range(KT), x_h, x_l, 0, True,
                       True).then_inc(chunk_used, 1)
            for j in range(4):
                c = C["nsa_q"] + j
                arrived(c + 1)
                if j == 0:
                    pe.wait_ge(blk_ready, 8)
                if j == 2:
                    pe.wait_ge(kv_done, 3)
                if j == 3:
                    pe.wait_ge(q_done, 1)
                pair(c % RING, TURN + j % 3, y_h, y_l, PC["mix1"] if j == 0 else None).then_inc(chunk_used, 1)
            arrived(C["nsa_gate"] + 1)
            tokens(C["nsa_gate"] % RING, lambda t: bank[:, SUMS, t * 48:t * 48 + 48], 48, range(KT), y_h, y_l, 0,
                   True, True).then_inc(chunk_used, 1)
            pe.wait_ge(op_lo, PC["blk_v"] + 1)
            pe.wait_ge(g_raw, 1)
            for w in range(2):
                for half in range(2):
                    c = C["phi"] + 2 * w + half
                    arrived(c + 1)
                    for l in range(8):
                        a, o = 960 * w + (8 * half + l) * 60, bank[0:120, (7, 3)[w], 0:256]
                        wh, wl = (t[:, c % RING, l * 256:l * 256 + 256] for t in (w_hi, w_lo))
                        mm(o, x_hf[:, a:a + 120], wh, start=half == 0 and l == 0, stop=False)
                        mm(o, x_hf[:, a:a + 120], wl, start=False, stop=False)
                        last = mm(o, x_lf[:, a:a + 120], wh, start=False, stop=half == 1 and l == 7)
                    last.then_inc(chunk_used, 1)
            pe.wait_ge(kv_done, 8)
            pe.wait_ge(q_done, 4)
            T = nc.tensor.transpose

            def n_score(k):
                if k >= 2:
                    pe.wait_ge(n_max, k - 1)
                t, e = k // 2, k % 2
                r, j = slice(64 * e, 64 * e + 64), t // 4
                keys = heads[r, 8 + j:12:2, :]
                mm(bank[:, 4 - 2 * e, :], n_q[r, t, 128:256], keys, start=True, stop=True)
                mm(bank[:, 5 - 2 * e, 0:256], n_q[r, t, 0:128], keys[:, :, 0:128], start=True,
                   stop=True).then_inc(n_scores, 1)

            for w in range(2):
                pe.wait_ge(phi_hid, w + 1)
                for k in range(2):
                    at = 120 * w + 60 * k
                    ins = T(bank[:, 0, at:at + 60], phi_h[:, w, P * k:P * k + P], con[0:60, CN["ident"]:CN["ident"] + 60])
            ins.then_inc(phi_t, 1)
            pe.wait_ge(phi_hid, 3)
            kw = dict(skip_group_check=True)
            for g in range(4):
                e = g % 2
                for k in range(2):
                    mm(bank[64 * e:64 * e + 64, 1, (g // 2) * 16:(g // 2) * 16 + NCMP],
                       col("phi_k2", k * 64, 64), cmp_hid[:, 0, k, g * NCMP:(g + 1) * NCMP],
                       start=k == 0, stop=k == 1, **kw)
            for g in range(4):
                for k in range(2):
                    ins = mm(bank[32 * g:32 * g + NCMP, 1, 64:128], cmp_hid[:, 1, k, g * NCMP:(g + 1) * NCMP],
                             col("phi_v2", k * 64, 64), start=k == 0, stop=k == 1, **kw)
            ins.then_inc(phi_mm, 1)

            b6, b7 = bank[:, 6, :], bank[:, 7, :]
            for k in range(G_HEADS + 3):
                if k < G_HEADS:
                    n_score(k)
                if k == 0:
                    pe.wait_ge(cmp_done, 2)
                    for t in range(KT):
                        at = (t % 4) * 128 + (t // 4) * 64
                        for q in range(2):
                            o = bank[:, q, at:at + 64].rearrange("p (e n) -> p e n", e=2)[:, :, 0:c_n[q]]
                            ins = mm(o, n_q[:, t, P * q:P * q + P], k_cmp[:, t // 4, :, 0:c_n[q]], start=True,
                                     stop=True)
                    ins.then_inc(c_scores, 1)
                if 2 <= k <= G_HEADS + 1:
                    (s1, w1, s0, w0) = n_parts(k - 2)
                    pe.wait_ge(n_prob, k - 1)
                    if k >= 3:
                        pe.wait_ge(n_ptc, k - 2)
                        pe.wait_ge(n_ptd, k - 2)
                    T(b6[:, 0:128], s0, ident)
                    T(b6[:, 128:256], s1[:, 0:128], ident)
                    T(b6[:, 256:384], w0, ident)
                    T(b6[:, 384:512], w1[:, 0:128], ident).then_inc(n_pt, 1)
                    T(b7[:, 0:128], s1[:, 128:256], ident)
                    T(b7[:, 128:256], w1[:, 128:256], ident).then_inc(n_pt, 1)
                if k == 2:
                    for q in range(2):
                        pe.wait_ge(c_prob, q + 1)
                        for t in range(4):
                            at = (t % 2) * S + q * P
                            ins = T(bank[:, t // 2, at:at + P],
                                    y_flat[:, 512 * q + 128 * t:512 * q + 128 * t + 128], ident)
                    ins.then_inc(c_pt, 1)
                if k == 3:
                    pe.wait_ge(c_ptc, 2)
                if k >= 3:
                    g = k - 3
                    nt = n_t[g % 2]
                    t, e = g // 2, g % 2
                    grp = 2 * (t // 4) + e
                    cols, own = slice(64 * grp, 64 * grp + 64), slice(32 * grp, 32 * grp + NCMP)
                    o = bank[64 * e:64 * e + 64, t // 2 % 2, (t % 2) * S:(t % 2) * S + S]
                    pe.wait_ge(n_ptc, g + 1)
                    if g >= 8 and g % 4 == 0:
                        pe.wait_ge(op_lo, PC["o_nsa"] + g // 4 - 1)
                    mm(o, n_vs[:, 0, cols], nt[:, 0:256], start=True, stop=False)
                    mm(o, n_vw[:, 0, cols], nt[:, 256:512], start=False, stop=False)
                    mm(o, v_cmp[own, :], c_t[own, (t % 4) * S:(t % 4) * S + S], start=False, stop=False)
                    pe.wait_ge(n_ptd, g + 1)
                    mm(o[:, 128:256], n_vs[:, 1, cols], nt[:, 512:640], start=False, stop=False)
                    mm(o[:, 128:256], n_vw[:, 1, cols], nt[:, 640:768], start=False, stop=True).then_inc(n_pv, 1)
            project("nsa_out", range(4), y_h, y_l, PC["o_nsa"])
            mlp("mlp1", PC["mlp1"], 10)
            sum_squares(11)


NSA_ORDER = [(2 * (t // 4) + e) * 4 + t % 4 for t in range(8) for e in range(2)]


def make_constants():
    c = np.zeros((P, N_CONST), np.float32)

    def put(name, a, row=0):
        c[row:row + a.shape[0], CN[name]:CN[name] + a.shape[1]] = a

    i, j = np.arange(P)[:, None], np.arange(P)[None, :]
    put("ident", np.eye(P, dtype=np.float32))
    put("tri", (i >= j).astype(np.float32))
    strict = np.where(i < j, 0.0, NEG).astype(np.float32)
    put("sb_neg", np.concatenate([strict, np.zeros((P, P), np.float32), strict], 1))
    put("mla_neg", np.concatenate([np.zeros((P, P)), np.where(j <= i, 0.0, NEG)], 1).astype(np.float32))
    rot = np.zeros((32, 32), np.float32)
    for m in range(16):
        rot[m + 16, m] = -1.0
        rot[m, m + 16] = 1.0
    put("rot", rot, 64)
    d = 255 - np.arange(384)
    large = 16 + np.floor(np.log(np.maximum(d, 1) / 16.0) / np.log(8.0) * 16 + 1e-9).astype(int)
    bucket = np.where(d < 16, d, np.minimum(large, 31))
    onehot = np.zeros((33, 384), np.float32)
    for n in range(384):
        onehot[32 if d[n] < 0 else bucket[n], n] = 1.0
    put("bucket", onehot)
    pick = np.zeros((P, 31), np.float32)
    pick[:, 15] = 1.0
    put("pick", pick)
    inv = np.float32(10000.0) ** (-np.arange(0, ROPE, 2, dtype=np.float32) / np.float32(ROPE))
    put("inv_freq", np.concatenate([inv, inv])[:, None].astype(np.float32), 64)
    put("has_any", (np.arange(P) >= 31).astype(np.float32)[:, None])
    return c


def pack_weights(w):
    chunks = []

    def add(a):
        a = a.reshape(P, -1)
        n = -(-a.shape[1] // CH) * CH
        a = np.concatenate([a, np.zeros((P, n - a.shape[1]), np.float32)], 1)
        chunks.extend(a[:, k:k + CH] for k in range(0, n, CH))

    def rows(a, kt=None):
        return a.reshape(-1, P, a.shape[1]).transpose(1, 0, 2)

    def pairs(a):
        for n in range(0, a.shape[1], 256):
            add(rows(a[:, n:n + 256]))

    def ffn(w_in, w_out):
        n = FF * P
        up = lambda f: add(rows(np.concatenate([w_in[:, f * P:f * P + P], w_in[:, n + f * P:n + f * P + P]], 1)))
        down = lambda i: add(rows(w_out[256 * i:256 * i + 256]))
        for i in range(FF // 2 + 1):
            if i < FF // 2:
                up(2 * i)
                up(2 * i + 1)
            if i >= 1:
                down(i - 1)

    def mlp(w1, w2):
        for j in range(MF + 2):
            if j < MF:
                add(rows(w1[:, 256 * j:256 * j + 256]))
            if j >= 2:
                add(rows(w2[256 * (j - 2):256 * (j - 1)]))

    ffn(w["ffn1_w_in"][0], w["ffn1_w_out"][0])
    w_in = w["w_in"][0]
    pairs(np.concatenate([w_in[:, 0:672], np.zeros((D, 96), np.float32)], 1))
    pairs(w_in[:, 672:672 + 1024])
    for j in range(2):
        add(rows(w_in[512 * j:512 * j + 512, 1696:2208]))
    for j in range(2):
        add(rows(w["w_q_up"][0][:, 384 * j:384 * j + 384]))
    kv = w["w_kv_up"][0].reshape(256, 8, 2, 64)
    add(rows(kv.transpose(0, 2, 1, 3).reshape(256, 1024)))
    pairs(w_in[:, 2208:])
    for half in range(2):
        for name in ("w_branch_mla", "w_branch_sb"):
            add(rows(w[name][0][:, 512 * half:512 * half + 512]))
    pairs(w["w_out"][0])
    ffn(w["ffn2_w_in"][0], w["ffn2_w_out"][0])
    add(rows(w["w_ple_proj"][0]))
    pairs(w["w_ple_gate"][0])
    a_in = w["a_w_in_2"][0]
    tile = lambda k, t: a_in[:, k * D + t * P:k * D + t * P + P]
    for i in range(4):
        for a, b in ((tile(1, 2 * i), tile(2, 2 * i)), (tile(1, 2 * i + 1), tile(2, 2 * i + 1)),
                     (tile(0, 2 * i), tile(0, 2 * i + 1))):
            add(rows(np.concatenate([a, b], 1)))
    pairs(w["a_w_out_2"][0])
    mlp(w["mlp_w1_2"][0], w["mlp_w2_2"][0])
    for k in (0, 1, 2, 4, 3, 5):
        add(rows(w["w_kv_2"][:, 256 * k:256 * k + 256]))
    qg = w["b_w_qg_2"][0]
    pairs(qg[:, :D].reshape(D, 16, 64)[:, NSA_ORDER].reshape(D, D))
    add(rows(qg[:, D:]))
    for name in ("phi_k_w1_2", "phi_v_w1_2"):
        add(w[name].reshape(2, 16, 64, 256).transpose(0, 2, 1, 3).reshape(P, 16 * 256))
    pairs(w["b_w_o_2"][0].reshape(16, 64, D)[NSA_ORDER].reshape(D, D))
    mlp(w["mlp_w1_2"][1], w["mlp_w2_2"][1])
    out = np.stack(chunks)
    assert out.shape == (N_CHUNKS, P, CH), out.shape
    return out


def pack_small(w):
    s = np.zeros((P, N_SMALL), np.float32)
    s_cols = lambda v: v.reshape(-1, P).T

    def put(name, a):
        s[:a.shape[0], SM[name]:SM[name] + a.shape[1]] = a

    for name, v in (("ffn1", w["ffn1_norm"][0]), ("mix", w["mix_norm"][0]), ("c_q", w["q_latent_norm"][0]),
                    ("c_kv", w["kv_latent_norm"][0]), ("ffn2", w["ffn2_norm"][0]), ("ple", w["ple_norm"][0]),
                    ("mix0", w["norm_mix_2"][0]), ("mlp0", w["norm_mlp_2"][0]), ("kv", w["kv_norm_2"]),
                    ("mix1", w["norm_mix_2"][1]), ("mlp1", w["norm_mlp_2"][1]), ("final", w["final_norm_2"])):
        put(name, s_cols(v))
    put("conv_w", np.concatenate([s_cols(w["a_conv_w_2"][0][k]) for k in range(3)], 1))
    put("q_head", w["q_head_norm"][0][:, None])
    put("k_head", w["k_head_norm"][0][:, None])
    for name in ("k", "v"):
        put("pe_" + name, w[f"cmp_pe_{name}_2"].reshape(2, 16, 64).transpose(0, 2, 1).reshape(P, 16))
        put(f"phi_{name}2", w[f"phi_{name}_w2_2"].reshape(2, P, 64).transpose(1, 0, 2).reshape(P, P))
    return s


def kernel(**inputs):
    import concourse.bacc as _bacc
    from concourse.bass_utils import run_bass_kernel_spmd as _run

    w = {k: np.asarray(v) for k, v in inputs.items()}
    tok = lambda a: np.ascontiguousarray(a.T.reshape(-1, P, S).transpose(1, 0, 2))
    arrays = {
        "x_t": tok(w["x"][0]),
        "p_t": tok(w["p"][0, 0]),
        "positions": np.ascontiguousarray(w["positions"][0]),
        "weights": pack_weights(w),
        "small": pack_small(w),
        "consts": make_constants(),
        "rel_bias": np.ascontiguousarray(w["rel_bias_2"]),
    }
    nc = _bacc.Bacc("TRN2", target_bir_lowering=False, num_devices=1)
    aps = {k: nc.dram_tensor(k, a.shape, mybir.dt.from_np(a.dtype), kind="ExternalInput").ap()
           for k, a in arrays.items()}
    bias_rows = nc.dram_tensor("bias_rows", (16, 384), F32)
    bias_skew = nc.dram_tensor("bias_skew", (G_HEADS, P * SKEW), F32)
    out = nc.dram_tensor("out_t", (P, KT, S), F32, kind="ExternalOutput").ap()
    program(nc, bias_rows=bias_rows, bias_skew=bias_skew, out=out, **aps)
    r = _run(nc, [arrays], core_ids=[0])
    y = r.results[0]["out_t"]
    return y.transpose(2, 1, 0).reshape(1, S, D)
```

```python
from contextlib import ExitStack

import numpy as np

import concourse.bass as bass
from concourse import mybir

F32 = mybir.dt.float32
F32R = mybir.dt.float32r
BF16 = mybir.dt.bfloat16
I32 = mybir.dt.int32
ALU = mybir.AluOpType
ACT = mybir.ActivationFunctionType
AX = mybir.AxisListType

P = 128
S = 256
D = 1024
KT = D // P
FF = 2816 // P
MF = 4096 // P // 2
FFN_TURNS = (FF // 2 - 1) // 2
MLP_TURNS = (MF - 2) // 3
EPS = 1e-6
NEG = -1e30
RING = 3
CH = 2048
HEADS, NOPE, ROPE = 8, 64, 32
QK = NOPE + ROPE
NCMP = S // 16 - 1
NVALID0 = 7
G_HEADS = 16
LINE = 384
SKEW = LINE + 1
UPDATES = 4

_sizes = [("ffn1", FF + FF // 2), ("latent", 3), ("sb_q", 2), ("sb_k", 2), ("sb_v", 2), ("q_up", 2),
          ("kv_up", 1), ("gates", 8), ("branch", 4), ("w_out", 4), ("ffn2", FF + FF // 2),
          ("ple_gate0", 1), ("ple_proj", 1), ("ple_gate", 3), ("conv_in", 12), ("conv_out", 4), ("mlp0", 2 * MF),
          ("kv_raw", 2), ("k_att", 2), ("v_att", 2), ("nsa_q", 4), ("nsa_gate", 1), ("phi", 4),
          ("nsa_out", 4), ("mlp1", 2 * MF)]
C, _at = {}, 0
for _name, _n in _sizes:
    C[_name] = _at
    _at += _n
N_CHUNKS = _at
assert N_CHUNKS % RING == 0
PLE_GATE = [C["ple_gate0"]] + [C["ple_gate"] + j for j in range(3)]

_pieces = [("ffn1", 4), ("mix", 4), ("c_q", 2), ("c_kv", 1), ("o", 4), ("merged", 4), ("ffn2", 4), ("p", 1),
           ("ple", 4), ("mix0", 4), ("conv", 4), ("mlp0", 4), ("kv", 4), ("mix1", 4), ("blk_k", 1),
           ("blk_v", 1), ("o_nsa", 4), ("mlp1", 4)]
PC, _at = {}, 0
for _name, _n in _pieces:
    PC[_name] = _at
    _at += _n

_small = [("ffn1", 8), ("mix", 8), ("c_q", 3), ("c_kv", 2), ("ffn2", 8), ("ple", 8), ("mix0", 8),
          ("mlp0", 8), ("kv", 8), ("mix1", 8), ("mlp1", 8), ("final", 8), ("conv_w", 24),
          ("q_head", 1), ("k_head", 1), ("pe_k", 16), ("pe_v", 16), ("phi_k2", 128), ("phi_v2", 128)]
SM, _at = {}, 0
for _name, _n in _small:
    SM[_name] = _at
    _at += _n
N_SMALL = _at

_const = [("ident", 128), ("tri", 128), ("sb_neg", 384), ("mla_neg", 256), ("rot", 32), ("bucket", 384),
          ("pick", 31), ("inv_freq", 1), ("has_any", 1)]
CN, _at = {}, 0
for _name, _n in _const:
    CN[_name] = _at
    _at += _n
N_CONST = _at

ACC, TURN, SUMS = 0, 4, 7
HID = {"ffn1": 0, "ffn2": FF, "mlp0": 2 * FF, "mlp1": 2 * FF + MF}
ENDS = {"ffn1": 0, "ffn2": 3, "mlp0": 6, "mlp1": 9}
UPD = {"ffn1": 0, "mix": 4, "ffn2": 8, "ple": 12, "mix0": 16, "mlp0": 20, "kv": 24, "mlp1": 28, "final": 32}
NORMS = ["ffn1", "mix", "c_q", "c_kv", "head", "ffn2", "ple", "mix0", "mlp0", "kv", "mlp1", "final"]
NO = {n: i for i, n in enumerate(NORMS)}
SQ, _at = {}, 0
for _n, _c in (("ffn1", 4), ("mix", 4), ("c_q", 1), ("c_kv", 1), ("head", 8), ("ffn2", 4), ("ple", 4),
               ("mix0", 4), ("mlp0", 4), ("kv", 4), ("mlp1", 4), ("final", 4)):
    SQ[_n] = _at
    _at += _c
DRAIN = {"latent": 0, "sb": 3, "gates": 7, "conv": 15}


class Steps:

    def __init__(self, eng, sem):
        self.eng, self.sem, self.n = eng, sem, 0

    def inc(self, ins):
        ins.then_inc(self.sem, 1)
        self.n = self.n + 1

    def wait(self):
        self.eng.wait_ge(self.sem, self.n)

    def done(self, ins):
        self.inc(ins)
        self.wait()


def program(nc, x_t, p_t, positions, weights, small, consts, rel_bias, bias_rows, bias_skew, out):
    with ExitStack() as ctx:
        def sb(name, shape, dt=F32):
            return ctx.enter_context(nc.sbuf_tensor(name, shape, dt))

        def sem(name):
            return ctx.enter_context(nc.semaphore(name))

        bank = ctx.enter_context(nc.psum_tensor("bank", [P, 8, 512], F32))

        raw = sb("raw", [P, RING, CH])
        w_hi = sb("w_hi", [P, RING, CH], F32R)
        w_lo = sb("w_lo", [P, RING, CH], F32R)
        h = sb("h", [P, KT, S])
        x_f, x_h, x_l = sb("x_f", [P, KT, S]), sb("x_h", [P, KT, S], F32R), sb("x_l", [P, KT, S], F32R)
        y_f, y_h, y_l = sb("y_f", [P, KT, S]), sb("y_h", [P, KT, S], F32R), sb("y_l", [P, KT, S], F32R)
        sq = sb("sq", [P, KT, S])
        hid_f = sb("hid_f", [P, 2, S])
        t_exp, t_a, t_b, r_sb = sb("t_exp", [P, S]), sb("t_a", [P, S]), sb("t_b", [P, S]), sb("r_sb", [P, S])
        t_ab = sb("t_ab", [P, 2, S])
        r_lat = sb("r_lat", [P, 2, S])
        r_tok = sb("r_tok", [P, 2, 2])
        t_m = sb("t_m", [P, S])
        heads = sb("heads", [P, 16, S])
        gate_or_bias = sb("gate_or_bias", [P, 16, S])
        sv = sb("sv", [P, 2, 512])
        mv = sb("mv", [P, 2, 512])
        par = sb("par", [P, N_SMALL])
        con = sb("con", [P, N_CONST])
        ones = sb("ones", [P, P])
        zeros = sb("zeros", [P, 512], BF16)
        relb = sb("relb", [33, 16])
        bias_1d = sb("bias_1d", [16, 384])
        pos_i, rope_tab = sb("pos_i", [P, S], I32), sb("rope_tab", [P, 2, S])
        v_pad = sb("v_pad", [P, 2, S + 2])
        stat = sb("stat", [P, 64])

        raw_landed = [sem(f"raw_landed{i}") for i in range(RING)]
        hi_split, lo_split, chunk_used = sem("hi_split"), sem("lo_split"), sem("chunk_used")
        first_hi, first_lo = sem("first_hi"), sem("first_lo")
        x_in, small_in, con_in, relb_in, pos_in, p_in = (
            sem("x_in"), sem("small_in"), sem("con_in"), sem("relb_in"), sem("pos_in"), sem("p_in"))
        setup = sem("setup")
        sq_ready, ss_ready, ms_ready, r0_ready = sem("sq_ready"), sem("ss_ready"), sem("ms_ready"), sem("r0_ready")
        op_hi, op_lo = sem("op_hi"), sem("op_lo")
        ffn_sig, hid_full, hid_hi, hid_lo = sem("ffn_sig"), sem("hid_full"), sem("hid_hi"), sem("hid_lo")
        acc_ready, h_upd, drained = sem("acc_ready"), sem("h_upd"), sem("drained")
        dve_step, act_step = sem("dve_step"), sem("act_step")
        ab_ready, sum_ready, r_ready, rt_mm, conv_full = (
            sem("ab_ready"), sem("sum_ready"), sem("r_ready"), sem("rt_mm"), sem("conv_full"))
        rope_ang, rope_sin = sem("rope_ang"), sem("rope_sin")
        sv_done, qk_raw = sem("sv_done"), sem("qk_raw")
        rq_mm, rq_done = sem("rq_mm"), sem("rq_done")
        r_head, bc_ready, normed, rot_ready, rope_cos, roped = (
            sem("r_head"), sem("bc_ready"), sem("normed"), sem("rot_ready"), sem("rope_cos"), sem("roped"))
        m_scores, m_max, m_exp, m_prob, m_pt, m_ptc, m_pv = (
            sem("m_scores"), sem("m_max"), sem("m_exp"), sem("m_prob"), sem("m_pt"), sem("m_ptc"), sem("m_pv"))
        s_z, s_abs, s_min, s_ln, s_l, s_e, s_x, s_a, s_pv = (
            sem("s_z"), sem("s_abs"), sem("s_min"), sem("s_ln"), sem("s_l"), sem("s_e"), sem("s_x"), sem("s_a"),
            sem("s_pv"))
        merged_done = sem("merged_done")
        ple_sig = sem("ple_sig")
        bias_ready, bias_out, bias_in = sem("bias_ready"), sem("bias_out"), sem("bias_in")
        bias_mm = sem("bias_mm")
        gates_done, ple_raw, g_raw = sem("gates_done"), sem("ple_raw"), sem("g_raw")
        kv_done, blk_ready = sem("kv_done"), sem("blk_ready")
        phi_t = sem("phi_t")
        phi_sig, phi_hid, phi_mm, cmp_done = sem("phi_sig"), sem("phi_hid"), sem("phi_mm"), sem("cmp_done")
        q_done, g_sig = sem("q_done"), sem("g_sig")
        c_scores, c_sub, c_exp, c_prob, c_pt, c_ptc = (
            sem("c_scores"), sem("c_sub"), sem("c_exp"), sem("c_prob"), sem("c_pt"), sem("c_ptc"))
        n_scores, n_max, n_exp, n_prob, n_pt, n_ptc, n_ptd, n_pv = (
            sem("n_scores"), sem("n_max"), sem("n_exp"), sem("n_prob"), sem("n_pt"), sem("n_ptc"), sem("n_ptd"),
            sem("n_pv"))
        y_ready, stored = sem("y_ready"), sem("stored")

        def col(name, i=0, n=1):
            return par[:, SM[name] + i:SM[name] + i + n]

        def cst(name, n, i=0):
            return con[:, CN[name] + i:CN[name] + i + n]

        ident = cst("ident", P)
        flat = lambda t: t[:, :, :].rearrange("p a b -> p (a b)")
        x_flat, sq_flat, y_flat = flat(x_f), flat(sq), flat(y_f)
        x_hf, x_lf = flat(x_h), flat(x_l)
        two = lambda ap: ap.rearrange("p (a b) -> p a b", a=2)
        r_two = r_sb[:, :].rearrange("p (a b) -> p a b", a=1).to_broadcast([P, 2, S])

        hidden = {"ffn1": (y_h[:, 0:4, :], y_l[:, 0:4, :]), "ffn2": (x_h[:, 2:6, :], x_l[:, 2:6, :]),
                  "mlp0": (y_h[:, 0:6, :], y_l[:, 0:6, :]), "mlp1": (y_h[:, 0:6, :], y_l[:, 0:6, :])}

        m_p = [x_flat[:, 384 * i:384 * i + 384] for i in range(2)]
        m_t = [x_flat[:, 768 + 384 * i:1152 + 384 * i] for i in range(2)]
        s_t1 = x_flat[:, 1536:1920]
        s_t2, s_m, s_lm = (sq_flat[:, 384 * i:384 * i + 384] for i in range(3))
        s_p = [sq_flat[:, 1152 + 384 * i:1536 + 384 * i] for i in range(2)]
        v_cmp = mv[:, 0, 0:64]
        c_stat = mv[:, 1, 160:288].rearrange("p (a q h) -> p a q h", a=4, q=2)
        k_cmp = mv[:, 1, 0:64].rearrange("p (j e n) -> p j e n", j=2, e=2)
        nsa_g = mv[:, 1, 64:160].rearrange("p (a b) -> p a b", a=2)
        cmp_hid = sv[:, 0, 0:240].rearrange("p (w k n) -> p w k n", w=2, k=2)
        phi_h = sv[0:60, 1, :].rearrange("p (w n) -> p w n", w=2)
        n_pa = [x_flat[:, 512 * i:512 * i + 512] for i in range(3)]
        n_pb = [x_flat[:, 1536 + 256 * i:1792 + 256 * i] for i in range(2)] + [t_ab[:, 0, :]]
        n_t = [sq_flat[:, 768 * i:768 * i + 768] for i in range(2)]
        c_p = y_flat[:, 0:1024].rearrange("p (q t g n) -> p q t g n", q=2, t=4, g=4)
        c_t = y_flat[:, 1024:2048]
        c_n = (NVALID0, NCMP)
        cos_part = (v_pad[64:96, :, 0:S], t_ab[64:96, :, :])
        z_bank = (1, 3)
        sb_q, sb_k = y_f[:, 0:4, :], y_f[:, 4:8, :]
        gate = gate_or_bias
        lat_raw = heads[:, 0:5, :]
        n_q, n_ks, n_kw, n_vs, n_vw = heads[:, 0:8, :], heads[:, 8:10, :], heads[:, 10:12, :], heads[:, 12:14, :], heads[:, 14:16, :]
        k_rope = t_b

        def n_parts(k):
            pa, pb = n_pa[k % 3], n_pb[k % 3]
            return pa[:, 0:256], pa[:, 256:512], pb[:, 0:128], pb[:, 128:256]

        pair_bank = (1, 2, 3, 4, 5, 0, 1, 2)
        q_scale, q_minus = (stat[:, 32 + 16 * i:48 + 16 * i].rearrange("p (t h) -> p t h", t=2) for i in range(2))

        block = ctx.enter_context(nc.Block())

        @block.sync
        def _(sp):
            sp.dma_start(h[:, :, :], x_t).then_inc(x_in, 16)
            sp.dma_start(par[:, :], small).then_inc(small_in, 16)
            for c in range(RING):
                sp.dma_start(raw[:, c, :], weights[c]).then_inc(raw_landed[c], 16)
            sp.dma_start(con[:, :], consts).then_inc(con_in, 16)
            sp.dma_start(relb[0:32, :], rel_bias).then_inc(relb_in, 16)
            sp.dma_start(pos_i[64:96, :], positions.partition_broadcast(32)).then_inc(pos_in, 16)
            with sp.Fori(1, N_CHUNKS // RING) as i:
                for j in range(RING):
                    sp.wait_ge(lo_split, RING * i + (j - RING + 1))
                    sp.dma_start(raw[:, j, :], weights[i * RING + j]).then_inc(raw_landed[j], 16)
            for j in range(UPDATES):
                sp.wait_ge(y_ready, j + 1)
                sp.dma_start(out[:, 2 * j:2 * j + 2, :], x_f[:, 2 * j:2 * j + 2, :]).then_inc(stored, 16)
            sp.wait_ge(stored, 16 * UPDATES)

        @block.gpsimd
        def _(pool):
            for n, (t, value) in enumerate(((ones[:, :], 1.0), (zeros[:, :], 0.0), (v_pad[:, :, :], 0.0),
                                            (relb[32:33, :], NEG))):
                if n >= 1:
                    pool.wait_ge(setup, n)
                nc.gpsimd.memset(t, value).then_inc(setup, 1)
            pool.wait_ge(setup, 4)
            for p in range(8):
                pool.wait_ge(normed, p + 1)
                pool.wait_ge(rope_sin, 2)
                if p >= 2:
                    pool.wait_ge(roped, p - 1)
                y = heads[64:96, 2 * p:2 * p + 2, :]
                cos = rope_tab[64:96, 0:1, :].to_broadcast([32, 2, S])
                nc.gpsimd.tensor_tensor(cos_part[p % 2], y, cos, ALU.mult).then_inc(rope_cos, 1)
            pool.wait_ge(roped, 8)
            nc.gpsimd.memset(v_pad[:, :, 0:2], 0.0).then_inc(setup, 1)
            pool.wait_ge(bias_ready, 1)
            pool.dma_start(bias_rows.ap(), bias_1d[:, :]).then_inc(bias_out, 16)
            pool.wait_ge(bias_out, 16)
            pool.dma_start(bass.AP(tensor=bias_skew, offset=0, ap=[[P * SKEW, G_HEADS], [SKEW, P], [1, LINE]]),
                           bass.AP(tensor=bias_rows, offset=0, ap=[[LINE, G_HEADS], [0, P], [1, LINE]])
                           ).then_inc(bias_out, 16)
            pool.wait_ge(bias_out, 32)
            pool.wait_ge(m_pv, 2 * HEADS)
            pool.dma_start(heads[:, 0:2, :], p_t).then_inc(p_in, 16)
            pool.wait_ge(merged_done, UPDATES)
            toeplitz = bass.AP(tensor=bias_skew, offset=P - 1, ap=[[LINE, P], [P * SKEW, G_HEADS], [1, S]])
            pool.dma_start(gate_or_bias[:, :, :], toeplitz).then_inc(bias_in, 16)
            pool.wait_ge(bias_in, 16)
            pool.wait_ge(p_in, 16)
            pool.wait_ge(op_lo, PC["blk_v"] + 1)
            nc.gpsimd.memset(y_flat[:, 0:1024], 0.0).then_inc(setup, 1)

        @block.scalar
        def _(act):
            st = Steps(act, act_step)

            def split(c, s, turn):
                act.wait_ge(raw_landed[s], 16 * turn)
                nc.scalar.activation(w_hi[:, s, :], raw[:, s, :], ACT.Copy).then_inc(hi_split, 1)

            def nxt(c):
                if c + RING < N_CHUNKS:
                    act.wait_ge(chunk_used, c + 1)
                    split(c + RING, c % RING, (c + RING) // RING + 1)

            def nxt_in(c0, j, i, step):
                c = c0 + j
                if isinstance(i, int):
                    nxt(c + i * step)
                    return
                act.wait_ge(chunk_used, i * step + (c + 1))
                split(None, c % RING, i * (step // RING) + (c // RING + 2))

            def hi(dst, src, full_sem=None, full_value=None, free=None):
                if full_sem is not None:
                    act.wait_ge(full_sem, full_value)
                if free is not None:
                    act.wait_ge(chunk_used, free)
                nc.scalar.activation(dst, src, ACT.Copy).then_inc(op_hi, 1)

            def gained_hi(dst, src, name, a, b):
                for t in range(a, b):
                    ins = nc.scalar.activation(dst[:, t - a, :], src[:, t - a, :], ACT.Copy, scale=col(name, t))
                ins.then_inc(op_hi, 1)

            def rsqrt(name, rows=slice(0, P), load=True):
                if load:
                    nc.scalar.preload_act_table_set("natural_log_exp_and_others")
                act.wait_ge(ms_ready, NO[name] + 1)
                st.done(nc.scalar.activation(t_a[rows, :], t_m[rows, :], ACT.Ln))
                nc.scalar.activation(t_exp[rows, :], t_a[rows, :], ACT.Exp, scale=-0.5).then_inc(r0_ready, 1)

            def operand(name, dst, free=None, chunks=()):
                for j in range(4):
                    if name == "ffn1":
                        act.wait_ge(x_in, 16)
                        act.wait_ge(small_in, 16)
                    else:
                        if j < len(chunks):
                            nxt(chunks[j])
                        act.wait_ge(h_upd, UPD[name] - UPDATES + j + 1)
                    if j == 0 and free is not None:
                        act.wait_ge(chunk_used, free)
                    gained_hi(dst[:, 2 * j:2 * j + 2, :], h[:, 2 * j:2 * j + 2, :], name, 2 * j, 2 * j + 2)
                    if name != "ffn1":
                        square(j)

            def square(j):
                nc.scalar.activation(sq[:, 2 * j:2 * j + 2, :], h[:, 2 * j:2 * j + 2, :],
                                     ACT.Square).then_inc(sq_ready, 1)

            def norm(name, dst, free=None, chunks=(), last_chunk=None):
                operand(name, dst, free, chunks)
                if last_chunk is not None:
                    nxt(last_chunk)
                rsqrt(name)

            def ffn(name):
                c0, b = C[name], HID[name]
                hid_h = hidden[name][0]

                def hid(slot, f, value, used=None):
                    act.wait_ge(hid_full, value)
                    if used is not None:
                        act.wait_ge(chunk_used, used)
                    nc.scalar.activation(hid_h[:, slot + f, :], hid_f[:, f, :], ACT.Copy).then_inc(hid_hi, 1)

                e0 = 0 if name == "ffn1" else FF

                def sigmoid(count):
                    act.wait_ge(ab_ready, count)
                    nc.scalar.activation(t_exp[:, :], t_ab[:, 0, :], ACT.Sigmoid).then_inc(ffn_sig, 1)

                for f in range(2):
                    sigmoid(e0 + f + 1)
                    hid(0, f, b + f + 1)
                    nxt(c0 + f)
                def turn(i):
                    for r in range(2):
                        c1, n = c0 + 2 + 3 * r, 2 * r + 2
                        sigmoid(i * 4 + (e0 + n + 1))
                        nxt_in(c1, 0, i, 6)
                        hid(2 - 2 * r, 0, i * 4 + (b + n + 1), i * 6 + c1)
                        sigmoid(i * 4 + (e0 + n + 2))
                        hid(2 - 2 * r, 1, i * 4 + (b + n + 2))
                        nxt_in(c1, 1, i, 6)
                        if not isinstance(i, int) or r == 0:
                            nxt_in(c1, 2, i, 6)

                with act.Fori(0, FFN_TURNS - 1) as i:
                    turn(i)
                turn(FFN_TURNS - 1)

            def mlp(name):
                c0, b = C[name], HID[name]
                hid_h = hidden[name][0]

                def hid(slot, value, used=None):
                    act.wait_ge(hid_full, value)
                    if used is not None:
                        act.wait_ge(chunk_used, used)
                    nc.scalar.activation(hid_h[:, 2 * slot:2 * slot + 2, :], hid_f[:, :, :],
                                         ACT.Copy).then_inc(hid_hi, 1)

                for j in range(2):
                    hid(j, b + j + 1)
                    nxt(c0 + j)

                def step(r, i):
                    nxt_in(c0 + 2, 2 * r, i, 6)
                    hid((r + 2) % 3, i * 3 + (b + r + 3), i * 6 + (c0 + 2 * r + 2))
                    nxt_in(c0 + 2, 2 * r + 1, i, 6)

                with act.Fori(0, MLP_TURNS) as i:
                    for r in range(3):
                        step(r, i)
                for j in range(3 * MLP_TURNS, MF - 2):
                    step(j % 3, j // 3)

            operand("ffn1", x_h)
            act.wait_ge(raw_landed[0], 16)
            for q in range(4):
                a = slice(512 * q, 512 * q + 512)
                nc.scalar.activation(w_hi[:, 0, a], raw[:, 0, a], ACT.Copy).then_inc(first_hi if q < 3 else hi_split, 1)
            for c in range(1, RING):
                split(c, c, 1)
            for j in range(4):
                square(j)
            rsqrt("ffn1")
            ffn("ffn1")

            norm("mix", x_h, C["latent"] - 1, (C["latent"] - 2,), C["latent"] - 1)
            for j in range(3):
                nxt(C["latent"] + j)
            act.wait_ge(drained, DRAIN["latent"] + 3)
            gained_hi(y_h[:, 0:2, :], lat_raw[:, 0:2, :], "c_q", 0, 2)
            gained_hi(y_h[:, 2:3, :], lat_raw[:, 2:3, :], "c_q", 2, 3)
            gained_hi(y_h[:, 3:5, :], lat_raw[:, 3:5, :], "c_kv", 0, 2)
            nc.scalar.activation(sq[:, 0:3, :], lat_raw[:, 0:3, :], ACT.Square).then_inc(sq_ready, 1)
            nc.scalar.activation(sq[:, 3:5, :], lat_raw[:, 3:5, :], ACT.Square).then_inc(sq_ready, 1)
            for j in range(4):
                nxt(C["sb_q"] + j)
            rsqrt("c_q")
            rsqrt("c_kv", load=False)
            act.wait_ge(rope_ang, 2)
            nc.scalar.activation(rope_tab[64:96, 0, :], rope_tab[64:96, 0, :], ACT.Sin).then_inc(rope_sin, 1)
            nc.scalar.activation(rope_tab[64:96, 1, :], rope_tab[64:96, 1, :], ACT.Sin).then_inc(rope_sin, 1)
            for j in range(2):
                nxt(C["sb_v"] + j)
            st.done(nc.scalar.activation(heads[64:96, 8:16, :],
                                         k_rope[0:ROPE, :].rearrange("p (a b) -> p a b", a=1).to_broadcast([ROPE, 8, S]),
                                         ACT.Copy))
            for j in range(2):
                nxt(C["q_up"] + j)

            def head_squares(p):
                dst = sq if p < 4 else x_f
                nc.scalar.activation(dst[0:QK, 2 * (p % 4):2 * (p % 4) + 2, :], heads[0:QK, 2 * p:2 * p + 2, :],
                                     ACT.Square).then_inc(sq_ready, 1)

            act.wait_ge(qk_raw, 4)
            for p in range(4):
                head_squares(p)
            nxt(C["kv_up"])
            act.wait_ge(qk_raw, 10)
            for p in range(4, 8):
                head_squares(p)
            for j in range(2):
                nxt(C["gates"] + j)
            rsqrt("head", slice(0, 16))
            def m_front(hd):
                act.wait_ge(m_max, hd + 1)
                for q in range(2):
                    c = slice(0, 128) if q == 0 else slice(128, 384)
                    o = 4 * (hd % 2) + q
                    nc.scalar.activation(m_p[hd % 2][:, c], m_p[hd % 2][:, c], ACT.Exp, scale=q_scale[:, q, hd:hd + 1],
                                         bias=stat[:, 8 + o:9 + o], accum_out=stat[:, 16 + o:17 + o]).then_inc(m_exp, 1)

            for hd in range(HEADS + 1):
                if hd < HEADS:
                    act.wait_ge(s_z, hd + 1)
                    if hd >= 1:
                        act.wait_ge(s_l, hd)
                    nc.scalar.activation(s_t1, bank[:, z_bank[hd % 2], 0:384], ACT.Abs).then_inc(s_abs, 1)
                    act.wait_ge(s_abs, hd + 1)
                    st.done(nc.scalar.activation(s_t1, s_t1, ACT.Exp, scale=-1.0))
                    nc.scalar.activation(s_t2, s_t1, ACT.Ln, bias=1.0).then_inc(s_ln, 1)
                    m_front(hd)
                if hd >= 1:
                    act.wait_ge(s_x, hd)
                    nc.scalar.activation(s_p[(hd - 1) % 2], s_p[(hd - 1) % 2], ACT.Exp).then_inc(s_a, 1)
                if hd == 0:
                    nxt(C["gates"] + 2)
                if hd % 2 == 1:
                    nxt(C["gates"] + 3 + hd // 2)
                if hd >= 2 and hd % 2 == 0:
                    t = hd // 2 - 1
                    act.wait_ge(m_pv, 2 * hd)
                    hi(y_h[:, t:8:4, :], two(bank[:, 4 + t % 2, :]), s_pv, hd)
            nxt(C["gates"] + 7)
            act.wait_ge(drained, DRAIN["gates"] + 8)
            for j in range(4):
                nc.scalar.activation(gate[:, 4 * j:4 * j + 4, :], gate[:, 4 * j:4 * j + 4, :],
                                     ACT.Sigmoid).then_inc(gates_done, 1)
            for half in range(2):
                nxt(C["branch"] + 2 * half)
                for j in range(2 * half, 2 * half + 2):
                    hi(x_h[:, 2 * j:2 * j + 2, :], x_f[:, 2 * j:2 * j + 2, :], merged_done, j + 1)
                nxt(C["branch"] + 2 * half + 1)

            w = C["w_out"]
            norm("ffn2", y_h, C["branch"] + 4, (w, w + 1, w + 2), w + 3)
            hi(x_h[:, 0:2, :], heads[:, 0:2, :], p_in, 16)
            ffn("ffn2")

            norm("ple", y_h, C["ple_gate0"] - 1, (C["ple_gate0"] - 2,), C["ple_gate0"] - 1)
            for j in range(4):
                act.wait_ge(ple_raw, j + 1)
                g = y_f[:, 2 * j:2 * j + 2, :]
                nc.scalar.activation(g, g, ACT.Sigmoid).then_inc(ple_sig, 1)
                if j < 3:
                    nxt(PLE_GATE[j])
                if j == 0:
                    nxt(C["ple_proj"])
                act.wait_ge(h_upd, UPD["mix0"] - UPDATES + j + 1)
                gained_hi(x_h[:, 2 * j:2 * j + 2, :], h[:, 2 * j:2 * j + 2, :], "mix0", 2 * j, 2 * j + 2)
                square(j)

            nxt(PLE_GATE[3])
            rsqrt("mix0")
            c0 = C["conv_in"]

            def conv_turn(i):
                nxt_in(c0, 0, i, 3)
                if not isinstance(i, int):
                    nxt_in(c0, 1, i, 3)
                act.wait_ge(conv_full, i + 1)
                nc.scalar.activation(y_h[:, bass.ds(i * 2, 2), :], y_f[:, bass.ds(i * 2, 2), :], ACT.Copy).then_inc(op_hi, 1)
                if isinstance(i, int):
                    nxt_in(c0, 1, i, 3)
                nxt_in(c0, 2, i, 3)

            with act.Fori(0, 3) as i:
                conv_turn(i)
            conv_turn(3)

            w = C["conv_out"]
            norm("mlp0", x_h, w, (w, w + 1, w + 2), w + 3)
            mlp("mlp0")

            c = C["kv_raw"]
            norm("kv", x_h, c - 1, (c - 2,), c - 1)
            nxt(c)
            for j in range(4):
                gained_hi(y_h[:, 2 * j:2 * j + 2, :], h[:, 2 * j:2 * j + 2, :], "mix1", 2 * j, 2 * j + 2)
            for j in range(1, 6):
                nxt(c + j)
            hi(x_hf[:, 0:960], y_flat[:, 0:960], blk_ready, 4, C["nsa_q"])
            hi(x_hf[:, 960:1920], y_flat[:, 960:1920], blk_ready, 8)
            for j in range(4):
                nxt(C["nsa_q"] + j)
            act.wait_ge(g_raw, 1)
            nc.scalar.activation(nsa_g[:, :, :], nsa_g[:, :, :], ACT.Sigmoid).then_inc(g_sig, 1)
            nxt(C["nsa_gate"])
            for w in range(2):
                nxt(C["phi"] + w)
            for w in range(2):
                act.wait_ge(chunk_used, C["phi"] + 2 * w + 2)
                if w == 1:
                    act.wait_ge(phi_hid, 1)
                nc.scalar.activation(t_exp[0:60, :], bank[0:60, (7, 3)[w], 0:256], ACT.Sigmoid).then_inc(phi_sig, 1)
            nc.scalar.preload_act_table_set("natural_log_exp_and_others")

            for k in range(G_HEADS + 2):
                if k == 3:
                    act.wait_ge(c_pt, 1)
                    nc.scalar.activation(c_t[:, 512:1024], bank[:, 1, :], ACT.Copy).then_inc(c_ptc, 1)
                if k >= 2:
                    act.wait_ge(n_pt, 2 * k - 3)
                    if k >= 4:
                        act.wait_ge(n_pv, k - 3)
                    nc.scalar.activation(n_t[k % 2][:, 0:512], bank[:, 6, :], ACT.Copy).then_inc(n_ptc, 1)
                if k < G_HEADS:
                    act.wait_ge(n_max, k + 1)
                    o = 16 * (k % 3)
                    for m, ap in enumerate(n_parts(k)):
                        nc.scalar.activation(ap, ap, ACT.Exp, bias=stat[:, o + 4 + m:o + 5 + m],
                                             accum_out=stat[:, o + 8 + m:o + 9 + m]).then_inc(n_exp, 1)
                if k in (1, 2):
                    nxt(C["phi"] + k + 1)
                if k == 1:
                    for q in range(2):
                        c = c_p[:, q, :, :, 0:c_n[q]]
                        act.wait_ge(c_sub, q + 1)
                        nc.scalar.activation(c, c, ACT.Exp).then_inc(c_exp, 1)
                if k % 4 == 3 and k >= 7:
                    m = k // 4 - 1
                    hi(y_h[:, 2 * m:2 * m + 2, :], two(bank[:, m % 2, :]), n_pv, 4 * m + 4)
            hi(y_h[:, 6:8, :], two(bank[:, 1, :]), n_pv, G_HEADS)

            w = C["nsa_out"]
            norm("mlp1", x_h, w, (w, w + 1, w + 2), w + 3)
            mlp("mlp1")
            for j in range(4):
                act.wait_ge(h_upd, UPD["final"] - UPDATES + j + 1)
                square(j)
            rsqrt("final")

        @block.vector
        def _(dve):
            st = Steps(dve, dve_step)
            V = nc.vector

            def split(s, count):
                dve.wait_ge(hi_split, count)
                V.tensor_tensor(w_lo[:, s, :], raw[:, s, :], w_hi[:, s, :].bitcast(F32), ALU.subtract).then_inc(lo_split, 1)

            def nxt(c):
                if c + RING < N_CHUNKS:
                    split(c % RING, c + RING + 1)

            def nxt_in(c0, j, i, step):
                if isinstance(i, int):
                    nxt(c0 + j + i * step)
                    return
                split((c0 + j) % RING, i * step + (c0 + j + RING + 1))

            made = [0]

            def lo(dst, src, hi_part):
                made[0] += 1
                dve.wait_ge(op_hi, made[0])
                V.tensor_tensor(dst, src, hi_part.bitcast(F32), ALU.subtract).then_inc(op_lo, 1)

            def rsqrt(name, ss, rows=slice(0, P), width=D, r_out=None, last=None):
                dve.wait_ge(ss_ready, NO[name] + 1)
                V.tensor_scalar(t_m[rows, :], ss, 1.0 / width, EPS, ALU.mult, ALU.add).then_inc(ms_ready, 1)
                dve.wait_ge(r0_ready, NO[name] + 1)
                st.done(V.tensor_tensor(t_a[rows, :], t_exp[rows, :], t_exp[rows, :], ALU.mult))
                st.done(V.scalar_tensor_tensor(out=t_a[rows, :], in0=t_a[rows, :], scalar=-0.5, in1=t_m[rows, :],
                                               op0=ALU.mult, op1=ALU.mult))
                ins = V.scalar_tensor_tensor(out=r_out, in0=t_a[rows, :], scalar=1.5, in1=t_exp[rows, :],
                                             op0=ALU.add, op1=ALU.mult)
                if last is None:
                    st.done(ins)
                else:
                    ins.then_inc(last, 1)

            def gained_lo(dst, src, hi_part, name, a, b):
                made[0] += 1
                dve.wait_ge(op_hi, made[0])
                for t in range(a, b):
                    ins = V.scalar_tensor_tensor(out=dst[:, t - a, :], in0=src[:, t - a, :], scalar=col(name, t),
                                                 in1=hi_part[:, t - a, :].bitcast(F32), op0=ALU.mult,
                                                 op1=ALU.subtract)
                ins.then_inc(op_lo, 1)

            def operand_piece(name, d_h, d_l, j):
                assert made[0] == PC[name] + j
                a = slice(2 * j, 2 * j + 2)
                gained_lo(d_l[:, a, :], h[:, a, :], d_h[:, a, :], name, 2 * j, 2 * j + 2)

            def sum_step(name, j):
                dve.wait_ge(sq_ready, SQ[name] + j + 1)
                st.done(V.tensor_tensor(sq[:, 0:2, :], sq[:, 0:2, :], sq[:, 2 * j:2 * j + 2, :], ALU.add))
                if j == 3:
                    V.tensor_tensor(sq[:, 0, :], sq[:, 0, :], sq[:, 1, :], ALU.add).then_inc(sum_ready, 1)

            def sum_tiles(name):
                for j in range(1, 4):
                    sum_step(name, j)

            def update_piece(scale, j):
                hj = h[:, 2 * j:2 * j + 2, :]
                V.scalar_tensor_tensor(out=hj, in0=two(bank[:, ACC + j, :]), scalar=scale, in1=hj, op0=ALU.mult,
                                       op1=ALU.add).then_inc(h_upd, 1)

            def finish(stage, scale, following, d_h, d_l):
                last_chunk = C[stage] + (FF + FF // 2 if stage in ("ffn1", "ffn2") else 2 * MF) - 1
                for j in range(5):
                    if j < 4:
                        if j < 3:
                            dve.wait_ge(acc_ready, ENDS[stage] + j + 1)
                        else:
                            dve.wait_ge(chunk_used, last_chunk + 1)
                        update_piece(scale, j)
                    if j == 0:
                        nxt(last_chunk - 1)
                    if j >= 1 and d_h is not None:
                        operand_piece(following, d_h, d_l, j - 1)
                    if 2 <= j < 4:
                        sum_step(following, j - 1)
                sum_step(following, 3)
                nxt(last_chunk)

            def project_out(stage, following, d_h, d_l):
                c = C[stage]
                for j in range(4):
                    dve.wait_ge(chunk_used, c + j + 1)
                    update_piece(1.0, j)
                    if j >= 1:
                        operand_piece(following, d_h, d_l, j - 1)
                    if j < 3:
                        nxt(c + j)
                operand_piece(following, d_h, d_l, 3)
                sum_tiles(following)
                nxt(c + 3)

            def factor(name, bk=SUMS):
                rsqrt(name, bank[:, bk, 0:S], r_out=r_sb[:, :])

            def ffn(name):
                c0, b = C[name], HID[name]
                hid_h, hid_l = hidden[name]

                def swiglu(f, count, used):
                    dve.wait_ge(chunk_used, used)
                    V.tensor_tensor(t_ab[:, :, :], two(bank[:, TURN + f, :]), r_two, ALU.mult).then_inc(ab_ready, 1)
                    dve.wait_ge(ab_ready, ab + (count - e0))
                    st.done(V.tensor_tensor(t_a[:, :], t_ab[:, 0, :], t_ab[:, 1, :], ALU.mult))
                    dve.wait_ge(ffn_sig, count)
                    V.tensor_tensor(hid_f[:, f, :], t_a[:, :], t_exp[:, :], ALU.mult).then_inc(hid_full, 1)

                def hid(slot, f, count):
                    dve.wait_ge(hid_hi, count)
                    V.tensor_tensor(hid_l[:, slot + f, :], hid_f[:, f, :], hid_h[:, slot + f, :].bitcast(F32),
                                    ALU.subtract).then_inc(hid_lo, 1)

                e0 = ab = b
                for f in range(2):
                    swiglu(f, e0 + f + 1, c0 + f + 1)
                    hid(0, f, b + f + 1)
                    nxt(c0 + f)
                start = st.n

                def turn(i):
                    st.n = i * 4 + start
                    for r in range(2):
                        c1, n = c0 + 2 + 3 * r, 2 * r + 2
                        swiglu(0, i * 4 + (e0 + n + 1), i * 6 + (c1 + 1))
                        nxt_in(c1, 0, i, 6)
                        hid(2 - 2 * r, 0, i * 4 + (b + n + 1))
                        swiglu(1, i * 4 + (e0 + n + 2), i * 6 + (c1 + 2))
                        hid(2 - 2 * r, 1, i * 4 + (b + n + 2))
                        nxt_in(c1, 1, i, 6)
                        if not isinstance(i, int) or r == 0:
                            nxt_in(c1, 2, i, 6)

                with dve.Fori(0, FFN_TURNS - 1) as i:
                    turn(i)
                turn(FFN_TURNS - 1)

            def mlp(name):
                c0, b = C[name], HID[name]
                hid_h, hid_l = hidden[name]

                def act_fn(bk, used, count):
                    dve.wait_ge(chunk_used, used)
                    V.scalar_tensor_tensor(out=t_ab[:, :, :], in0=two(bank[:, TURN + bk, :]), scalar=0.0,
                                           in1=r_two, op0=ALU.max, op1=ALU.mult).then_inc(ab_ready, 1)
                    dve.wait_ge(ab_ready, count)
                    V.tensor_tensor(hid_f[:, :, :], t_ab[:, :, :], t_ab[:, :, :], ALU.mult).then_inc(hid_full, 1)

                def hid(slot, count):
                    dve.wait_ge(hid_hi, count)
                    V.tensor_tensor(hid_l[:, 2 * slot:2 * slot + 2, :], hid_f[:, :, :],
                                    hid_h[:, 2 * slot:2 * slot + 2, :].bitcast(F32), ALU.subtract).then_inc(hid_lo, 1)

                for j in range(2):
                    act_fn(j, c0 + j + 1, b + j + 1)
                    hid(j, b + j + 1)
                    nxt(c0 + j)

                def step(r, i):
                    act_fn((r + 2) % 3, i * 6 + (c0 + 2 * r + 3), i * 3 + (b + r + 3))
                    nxt_in(c0 + 2, 2 * r, i, 6)
                    hid((r + 2) % 3, i * 3 + (b + r + 3))
                    nxt_in(c0 + 2, 2 * r + 1, i, 6)

                with dve.Fori(0, MLP_TURNS) as i:
                    for r in range(3):
                        step(r, i)
                for j in range(3 * MLP_TURNS, MF - 2):
                    step(j % 3, j // 3)

            def angles():
                R = slice(64, 96)
                two_pi = 2.0 * np.pi
                c1 = float(np.float32(6.28125))
                rest = two_pi - 6.28125
                c2 = float((np.array([rest], np.float32).view(np.uint32) & np.uint32(0xFFFFF000)).view(np.float32)[0])
                c3 = float(np.float32(rest - c2))
                dve.wait_ge(pos_in, 16)
                dve.wait_ge(con_in, 16)
                st.done(V.tensor_copy(t_a[R, :], pos_i[R, :]))
                st.done(V.tensor_scalar(t_a[R, :], t_a[R, :], con[R, CN["inv_freq"]:CN["inv_freq"] + 1], None, ALU.mult))
                for which, turn in ((1, 0.0), (0, 0.25)):
                    tab = rope_tab[R, which, :]
                    st.done(V.tensor_scalar(t_b[R, :], t_a[R, :], float(1.0 / two_pi), turn, ALU.mult, ALU.add))
                    st.done(V.tensor_scalar(t_b[R, :], t_b[R, :], 12582912.0, None, ALU.add))
                    st.done(V.tensor_scalar(t_b[R, :], t_b[R, :], 12582912.0, None, ALU.subtract))
                    st.done(V.scalar_tensor_tensor(out=tab, in0=t_b[R, :], scalar=-c1, in1=t_a[R, :],
                                                   op0=ALU.mult, op1=ALU.add))
                    st.done(V.scalar_tensor_tensor(out=tab, in0=t_b[R, :], scalar=-c2, in1=tab,
                                                   op0=ALU.mult, op1=ALU.add))
                    st.done(V.scalar_tensor_tensor(out=tab, in0=t_b[R, :], scalar=-c3, in1=tab,
                                                   op0=ALU.mult, op1=ALU.add))
                    if which == 0:
                        st.done(V.tensor_scalar(tab, tab, float(np.pi / 2), None, ALU.add))
                    pi = float(np.nextafter(np.float32(np.pi), np.float32(0)))
                    V.tensor_scalar(tab, tab, pi, -pi, ALU.min, ALU.max).then_inc(rope_ang, 1)

            dve.wait_ge(small_in, 16)
            dve.wait_ge(x_in, 16)
            for j in range(4):
                operand_piece("ffn1", x_h, x_l, j)
            for q in range(4):
                a = slice(512 * q, 512 * q + 512)
                if q < 3:
                    dve.wait_ge(first_hi, q + 1)
                else:
                    dve.wait_ge(hi_split, 1)
                V.tensor_tensor(w_lo[:, 0, a], raw[:, 0, a], w_hi[:, 0, a].bitcast(F32),
                                ALU.subtract).then_inc(first_lo if q < 3 else lo_split, 1)
            for c in range(1, RING):
                split(c, c + 1)
            sum_tiles("ffn1")
            factor("ffn1")
            ffn("ffn1")
            finish("ffn1", 0.5, "mix", x_h, x_l)

            factor("mix")
            dve.wait_ge(bias_mm, 1)
            V.tensor_copy(bias_1d[:, :], bank[0:16, 6, 0:384]).then_inc(bias_ready, 1)
            for j in range(3):
                dve.wait_ge(chunk_used, C["latent"] + j + 1)
                b = two(bank[:, TURN + j, :])
                if j < 2:
                    V.tensor_tensor(lat_raw[:, 2 * j:2 * j + 2, :], b, r_two, ALU.mult).then_inc(drained, 1)
                else:
                    V.tensor_tensor(lat_raw[:, 4, :], b[:, 0, :], r_sb[:, :], ALU.mult)
                    V.tensor_tensor(k_rope[0:ROPE, :], b[0:ROPE, 1, :], r_sb[0:ROPE, :], ALU.mult).then_inc(drained, 1)
                nxt(C["latent"] + j)
            angles()
            gained_lo(y_l[:, 0:2, :], lat_raw[:, 0:2, :], y_h[:, 0:2, :], "c_q", 0, 2)
            gained_lo(y_l[:, 2:3, :], lat_raw[:, 2:3, :], y_h[:, 2:3, :], "c_q", 2, 3)
            gained_lo(y_l[:, 3:5, :], lat_raw[:, 3:5, :], y_h[:, 3:5, :], "c_kv", 0, 2)
            dve.wait_ge(sq_ready, SQ["c_q"] + 1)
            st.done(V.tensor_tensor(sq[:, 0, :], sq[:, 0, :], sq[:, 1, :], ALU.add))
            V.tensor_tensor(sq[:, 0, :], sq[:, 0, :], sq[:, 2, :], ALU.add).then_inc(sum_ready, 1)
            dve.wait_ge(sq_ready, SQ["c_kv"] + 1)
            V.tensor_tensor(sq[:, 3, :], sq[:, 3, :], sq[:, 4, :], ALU.add).then_inc(sum_ready, 1)
            for j in range(4):
                c = C["sb_q"] + j
                dve.wait_ge(chunk_used, c + 1)
                b = two(bank[:, TURN + (DRAIN["sb"] + j) % 3, :])
                V.scalar_tensor_tensor(out=y_f[:, 2 * j:2 * j + 2, :], in0=b, scalar=0.125 if j < 2 else 1.0,
                                       in1=r_two, op0=ALU.mult, op1=ALU.mult).then_inc(drained, 1)
                nxt(c)
            rsqrt("c_q", bank[:, SUMS, 0:S], width=384, r_out=r_lat[:, 0, :])
            rsqrt("c_kv", bank[:, 3, 0:S], width=256, r_out=r_lat[:, 1, :], last=r_ready)
            dve.wait_ge(rt_mm, 1)
            st.done(V.tensor_copy(r_tok[:, 0, :], bank[:, SUMS, 0:256:128]))
            st.done(V.tensor_copy(r_tok[:, 1, :], bank[:, SUMS, 256:512:128]))
            dve.wait_ge(chunk_used, C["sb_v"] + 2)
            for t in range(2):
                V.tensor_scalar(sv[:, t, :], bank[:, t, :], r_tok[:, 0, t:t + 1], None, ALU.mult).then_inc(sv_done, 1)
            for j in range(2):
                nxt(C["sb_v"] + j)
            lat_two = [r_lat[:, i, :].rearrange("p (a b) -> p a b", a=1).to_broadcast([P, 2, S]) for i in range(2)]
            for j in range(2):
                dve.wait_ge(chunk_used, C["q_up"] + j + 1)
                for t in range(2):
                    hd = 4 * j + 2 * t
                    V.tensor_tensor(heads[0:QK, hd:hd + 2, :], two(bank[0:QK, 2 - 2 * j + t, :]), lat_two[0][0:QK],
                                    ALU.mult).then_inc(qk_raw, 1)
                nxt(C["q_up"] + j)
            dve.wait_ge(chunk_used, C["kv_up"] + 1)
            for t in range(2):
                V.tensor_scalar(mv[:, t, :], bank[:, 2 + t, :], r_tok[:, 1, t:t + 1], None, ALU.mult).then_inc(qk_raw, 1)
            for t in range(2):
                b = two(bank[:, 4 + t, :])
                for e in range(2):
                    k = heads[0:NOPE, 8 + 4 * t + e:8 + 4 * t + e + 3:2, :]
                    rows = slice(64 * e, 64 * e + 64)
                    V.tensor_tensor(k, b[rows], lat_two[1][rows], ALU.mult).then_inc(qk_raw, 1)
            nxt(C["kv_up"])

            def gates_in(j):
                dve.wait_ge(chunk_used, C["gates"] + j + 1)
                V.tensor_tensor(gate[:, 2 * j:2 * j + 2, :], two(bank[:, 6 + j % 2, :]), r_two,
                                ALU.mult).then_inc(drained, 1)
                nxt(C["gates"] + j)

            def rope(p):
                y = heads[64:96, 2 * p:2 * p + 2, :]
                dve.wait_ge(rot_ready, p + 1)
                if p >= 1:
                    dve.wait_ge(roped, p)
                b = two(bank[64:96, pair_bank[p], :])
                sin = rope_tab[64:96, 1:2, :].to_broadcast([32, 2, S])
                st.done(V.tensor_tensor(hid_f[64:96, :, :], b, sin, ALU.mult))
                dve.wait_ge(rope_cos, p + 1)
                V.tensor_tensor(y, hid_f[64:96, :, :], cos_part[p % 2], ALU.add).then_inc(roped, 1)

            gates_in(0)
            for p in range(4):
                dve.wait_ge(sq_ready, SQ["head"] + p + 1)
                y = heads[0:QK, 2 * p:2 * p + 2, :]
                V.tensor_scalar(y, y, col("q_head")[0:QK], None, ALU.mult).then_inc(normed, 1)
            gates_in(1)
            rsqrt("head", bank[0:16, 0, 0:S], slice(0, 16), QK, t_b[0:16, :], r_head)
            dve.wait_ge(rq_mm, 1)
            r_q = bank[:, 0, 0:32].rearrange("p (t h) -> p t h", t=2)[:, :, 0:8]
            V.tensor_scalar(q_scale, r_q, float(QK) ** -0.5, None, ALU.mult).then_inc(rq_done, 1)
            V.tensor_scalar(q_minus, r_q, -float(QK) ** -0.5, None, ALU.mult).then_inc(rq_done, 1)
            dve.wait_ge(rope_sin, 2)
            for p in range(4, 8):
                rope(p - 4)
                dve.wait_ge(bc_ready, p - 3)
                b = two(bank[0:QK, pair_bank[p], :])
                y = heads[0:QK, 2 * p:2 * p + 2, :]
                V.scalar_tensor_tensor(out=y, in0=y, scalar=col("k_head")[0:QK], in1=b,
                                       op0=ALU.mult, op1=ALU.mult).then_inc(normed, 1)
            for p in range(4, 8):
                rope(p)

            dve.wait_ge(rq_done, 2)
            for hd in range(HEADS + 1):
                o = 4 * (hd % 2)
                if hd < HEADS:
                    dve.wait_ge(s_z, hd + 1)
                    dve.wait_ge(s_abs, hd + 1)
                    V.tensor_scalar(s_m, bank[:, z_bank[hd % 2], 0:384], -1.0, 0.0, ALU.mult, ALU.min).then_inc(s_min, 1)
                    dve.wait_ge(m_scores, hd + 1)
                    mp = m_p[hd % 2]
                    if hd >= 2:
                        dve.wait_ge(m_pt, hd - 1)
                    for q in range(2):
                        c = slice(0, 128) if q == 0 else slice(128, 384)
                        neg = cst("mla_neg", 128, 128) if q == 0 else cst("mla_neg", 256)
                        st.inc(V.tensor_tensor_reduce(mp[:, c], bank[:, 0, c], neg, 1.0, -3e38, ALU.add, ALU.max,
                                                      stat[:, o + q:o + q + 1]))
                    st.wait()
                    V.tensor_tensor(stat[:, 8 + o:10 + o], stat[:, o:o + 2], q_minus[:, :, hd],
                                    ALU.mult).then_inc(m_max, 1)
                if hd >= 1:
                    dve.wait_ge(s_e, hd)
                    if hd >= 3:
                        dve.wait_ge(s_pv, hd - 2)
                    V.tensor_tensor(s_p[(hd - 1) % 2], bank[:, z_bank[(hd - 1) % 2], 0:384], cst("sb_neg", 384), ALU.add).then_inc(s_x, 1)
                    dve.wait_ge(m_pt, hd)
                    if hd >= 3:
                        dve.wait_ge(m_pv, 2 * (hd - 2))
                    V.tensor_copy(m_t[(hd - 1) % 2], bank[:, 2, 0:384]).then_inc(m_ptc, 1)
                if hd < HEADS:
                    dve.wait_ge(s_ln, hd + 1)
                    dve.wait_ge(s_min, hd + 1)
                    if hd >= 1:
                        dve.wait_ge(s_e, hd)
                    st.done(V.tensor_tensor(s_lm, s_m, s_t2, ALU.subtract))
                    lm = s_lm.rearrange("p (a b) -> p a b", a=3)[:, 0:3:2, :]
                    one = con[:, CN["tri"]:CN["tri"] + P].rearrange("p (a b) -> p a b", a=1).to_broadcast([P, 2, P])
                    st.done(V.tensor_tensor(s_m.rearrange("p (a b) -> p a b", a=3)[:, 0:3:2, :], lm, one, ALU.mult))
                    V.tensor_tensor(lm, lm, s_m.rearrange("p (a b) -> p a b", a=3)[:, 0:3:2, :],
                                    ALU.subtract).then_inc(s_l, 1)
                    dve.wait_ge(m_exp, 2 * hd + 2)
                    st.done(V.reciprocal(stat[:, 24 + o:26 + o], stat[:, 16 + o:18 + o]))
                    V.tensor_scalar(mp[:, 0:128], mp[:, 0:128], stat[:, 24 + o:25 + o], None, ALU.mult)
                    V.tensor_scalar(mp[:, 128:384], mp[:, 128:384], stat[:, 25 + o:26 + o], None,
                                    ALU.mult).then_inc(m_prob, 1)
                if hd == 0:
                    gates_in(2)
                if hd % 2 == 1:
                    gates_in(3 + hd // 2)
                if hd >= 2 and hd % 2 == 0:
                    t = hd // 2 - 1
                    lo(y_l[:, t:8:4, :], two(bank[:, 4 + t % 2, :]), y_h[:, t:8:4, :])
            gates_in(7)
            dve.wait_ge(gates_done, 4)
            mla = (hid_f, sq[:, 2:4, :])
            for half in range(2):
                c = C["branch"] + 2 * half
                if half == 1:
                    dve.wait_ge(merged_done, 2)
                dve.wait_ge(chunk_used, c + 1)
                for t in range(2):
                    j = 2 * half + t
                    st.inc(V.tensor_tensor(mla[t][:, :, :], two(bank[:, 4 * half + t, :]), gate[:, 2 * j:2 * j + 2, :],
                                           ALU.mult))
                nxt(c)
                dve.wait_ge(chunk_used, c + 2)
                for t in range(2):
                    j = 2 * half + t
                    sbr = sq[:, 4 * t:4 * t + 2, :]
                    st.done(V.tensor_tensor(sbr, two(bank[:, 4 * half + 2 + t, :]), gate[:, 8 + 2 * j:10 + 2 * j, :],
                                            ALU.mult))
                    V.tensor_tensor(x_f[:, 2 * j:2 * j + 2, :], mla[t][:, :, :], sbr, ALU.add).then_inc(merged_done, 1)
                for j in range(2 * half, 2 * half + 2):
                    lo(x_l[:, 2 * j:2 * j + 2, :], x_f[:, 2 * j:2 * j + 2, :], x_h[:, 2 * j:2 * j + 2, :])
                nxt(c + 1)

            project_out("w_out", "ffn2", y_h, y_l)
            factor("ffn2")
            lo(x_l[:, 0:2, :], heads[:, 0:2, :], x_h[:, 0:2, :])
            ffn("ffn2")
            finish("ffn2", 0.5, "ple", y_h, y_l)

            factor("ple", 3)
            for j in range(4):
                y, hj = y_f[:, 2 * j:2 * j + 2, :], h[:, 2 * j:2 * j + 2, :]
                dve.wait_ge(chunk_used, PLE_GATE[j] + 1)
                V.tensor_tensor(y, two(bank[:, ACC + j, :]), r_two, ALU.mult).then_inc(ple_raw, 1)
                if j >= 1:
                    operand_piece("mix0", x_h, x_l, j - 1)
                else:
                    nxt(PLE_GATE[0])
                    dve.wait_ge(chunk_used, C["ple_proj"] + 1)
                dve.wait_ge(ple_sig, j + 1)
                st.done(V.tensor_tensor(y, two(bank[:, 4 + j, :]), y, ALU.mult))
                V.tensor_tensor(hj, hj, y, ALU.add).then_inc(h_upd, 1)
                if j == 0:
                    nxt(C["ple_proj"])
                elif j < 3:
                    nxt(PLE_GATE[j])
            operand_piece("mix0", x_h, x_l, 3)
            sum_tiles("mix0")
            nxt(PLE_GATE[3])

            factor("mix0")
            st.done(V.tensor_tensor(t_m[:, :], r_sb[:, :], r_sb[:, :], ALU.mult))
            n = st.n
            dve.wait_ge(setup, 5)
            c0 = C["conv_in"]

            def conv_turn(i):
                st.n = i * 8 + n
                for j in range(2):
                    dve.wait_ge(chunk_used, i * 3 + (c0 + j + 1))
                    st.done(V.tensor_tensor(t_ab[:, j, :], bank[:, TURN + j, 0:S], t_m[:, :], ALU.mult))
                    V.tensor_tensor(v_pad[:, j, 2:S + 2], t_ab[:, j, :], bank[:, TURN + j, S:2 * S],
                                    ALU.mult).then_inc(drained, 1)
                    dve.wait_ge(drained, i * 3 + (DRAIN["conv"] + j + 1))
                    for k in range(3):
                        tap = 2 - k
                        w = par[:, bass.ds(i * 2 + (SM["conv_w"] + 8 * tap + j), 1)]
                        src = v_pad[:, j, tap:tap + S]
                        if k == 0:
                            st.done(V.tensor_scalar(hid_f[:, j, :], src, w, None, ALU.mult))
                        else:
                            st.done(V.scalar_tensor_tensor(out=hid_f[:, j, :], in0=src, scalar=w,
                                                           in1=hid_f[:, j, :], op0=ALU.mult, op1=ALU.add))
                    if j == 0 or not isinstance(i, int):
                        nxt_in(c0, j, i, 3)
                dve.wait_ge(chunk_used, i * 3 + (c0 + 3))
                V.tensor_tensor(t_ab[:, :, :], two(bank[:, TURN + 2, :]), r_two, ALU.mult).then_inc(drained, 1)
                dve.wait_ge(drained, i * 3 + (DRAIN["conv"] + 3))
                V.tensor_tensor(y_f[:, bass.ds(i * 2, 2), :], t_ab[:, :, :], hid_f[:, :, :],
                                ALU.mult).then_inc(conv_full, 1)
                dve.wait_ge(op_hi, i + (PC["conv"] + 1))
                V.tensor_tensor(y_l[:, bass.ds(i * 2, 2), :], y_f[:, bass.ds(i * 2, 2), :],
                                y_h[:, bass.ds(i * 2, 2), :].bitcast(F32), ALU.subtract).then_inc(op_lo, 1)
                if isinstance(i, int):
                    nxt_in(c0, 1, i, 3)
                nxt_in(c0, 2, i, 3)

            with dve.Fori(0, 3) as i:
                conv_turn(i)
            conv_turn(3)
            st.n = n + 32
            made[0] += 4

            project_out("conv_out", "mlp0", x_h, x_l)
            factor("mlp0")
            mlp("mlp0")
            finish("mlp0", 1.0, "kv", x_h, x_l)

            rsqrt("kv", bank[:, SUMS, 0:S], r_out=r_sb[:, :], last=r_ready)
            dve.wait_ge(r_ready, 2)
            for w in range(2):
                dve.wait_ge(chunk_used, C["kv_raw"] + w + 1)
                if w == 1:
                    dve.wait_ge(blk_ready, 4)
                V.tensor_tensor(t_ab[:, :, :], two(bank[:, TURN + w, :]), r_two, ALU.mult).then_inc(kv_done, 1)
                dve.wait_ge(kv_done, w + 1)
                pe = col("pe_k" if w == 0 else "pe_v", 0, 16)
                for half in range(2):
                    for e in range(2):
                        rows = slice(64 * half, 64 * half + 64)
                        src = t_ab[64 * e:64 * e + 64, :, :].rearrange("p a (n l) -> p l a n", l=16)
                        dst = y_flat[rows, 960 * w:960 * w + 960].rearrange("p (l g n) -> p l g n", l=16, g=4)
                        for t in range(2):
                            ins = V.tensor_tensor(dst[:, :, 2 * t + e, :], src[:, :, t, half:half + NCMP],
                                                  pe[rows, :].rearrange("p (l n) -> p l n", n=1).to_broadcast([64, 16, NCMP]),
                                                  ALU.add)
                        ins.then_inc(blk_ready, 1)
                nxt(C["kv_raw"] + w)
                for j in range(2 * w, 2 * w + 2):
                    operand_piece("mix1", y_h, y_l, j)
            for w in range(2):
                dve.wait_ge(chunk_used, C["k_att"] + w + 1)
                V.tensor_tensor((n_ks, n_kw)[w], two(bank[:, (6, 0)[w], :]), r_two, ALU.mult).then_inc(kv_done, 1)
                nxt(C["k_att"] + w)
            dve.wait_ge(rt_mm, 2)
            st.done(V.tensor_copy(r_tok[:, 0, :], bank[:, SUMS, 0:256:128]))
            for w in range(2):
                dve.wait_ge(chunk_used, C["v_att"] + w + 1)
                for t in range(2):
                    V.tensor_scalar((n_vs, n_vw)[w][:, t, :], bank[:, (1, 2)[w], t * 256:t * 256 + 256],
                                    r_tok[:, 0, t:t + 1], None, ALU.mult).then_inc(kv_done, 1)
                nxt(C["v_att"] + w)
            lo(x_lf[:, 0:960], y_flat[:, 0:960], x_hf[:, 0:960])
            lo(x_lf[:, 960:1920], y_flat[:, 960:1920], x_hf[:, 960:1920])
            for j in range(4):
                dve.wait_ge(chunk_used, C["nsa_q"] + j + 1)
                V.scalar_tensor_tensor(out=n_q[:, 2 * j:2 * j + 2, :], in0=two(bank[:, TURN + j % 3, :]), scalar=0.125,
                                       in1=r_two, op0=ALU.mult, op1=ALU.mult).then_inc(q_done, 1)
                nxt(C["nsa_q"] + j)
            dve.wait_ge(chunk_used, C["nsa_gate"] + 1)
            for t in range(2):
                ins = V.tensor_scalar(nsa_g[:, t, :], bank[:, SUMS, t * 48:t * 48 + 48], r_tok[:, 0, t:t + 1], None,
                                      ALU.mult)
            ins.then_inc(g_raw, 1)
            nxt(C["nsa_gate"])
            dve.wait_ge(g_sig, 1)
            g0 = nsa_g[:, 0, 0:48:3]
            st.done(V.tensor_scalar(g0, g0, cst("has_any", 1), None, ALU.mult))
            V.memset(mv[:, 1, 0:64], 0.0)
            for w in range(2):
                nxt(C["phi"] + w)
            for w in range(2):
                dve.wait_ge(phi_sig, w + 1)
                V.tensor_tensor(phi_h[:, w, :], bank[0:60, (7, 3)[w], 0:256], t_exp[0:60, :],
                                ALU.mult).then_inc(phi_hid, 1)
            dve.wait_ge(phi_t, 1)
            V.tensor_copy(sv[:, 0, 0:240], bank[:, 0, 0:240]).then_inc(phi_hid, 1)
            dve.wait_ge(phi_mm, 1)
            for e in range(2):
                rows = slice(64 * e, 64 * e + 64)
                src = bank[rows, 1, 0:32].rearrange("p (a b) -> p a b", a=2)
                ins = V.tensor_copy(k_cmp[rows, :, e, 0:NCMP], src[:, :, 0:NCMP])
            ins.then_inc(cmp_done, 1)
            for g in range(4):
                rows = slice(32 * g, 32 * g + NCMP)
                ins = V.tensor_copy(v_cmp[rows, :], bank[rows, 1, 64:128])
            ins.then_inc(cmp_done, 1)

            dve.wait_ge(bias_in, 16)
            c_max, c_sum, c_rec, c_fac = (c_stat[:, m, :, :] for m in range(4))
            by_head = lambda ap: ap.rearrange("p (t g) -> p t g", t=4)
            for k in range(G_HEADS + 2):
                if k < G_HEADS:
                    o = 16 * (k % 3)
                    bias = gate_or_bias[:, NSA_ORDER[k], :]
                    dve.wait_ge(n_scores, k + 1)
                    if k >= 3:
                        dve.wait_ge(n_pt, 2 * (k - 2))
                    a, b = bank[:, 4 - 2 * (k % 2), :], bank[:, 5 - 2 * (k % 2), :]
                    for m, (dst, src) in enumerate(zip(n_parts(k), (a[:, 0:256], a[:, 256:512], b[:, 0:128],
                                                                    b[:, 128:256]))):
                        st.inc(V.tensor_tensor_reduce(dst, src, bias if m < 2 else bias[:, 128:256], 1.0, -3e38,
                                                      ALU.add, ALU.max, stat[:, o + m:o + m + 1]))
                    st.wait()
                    V.tensor_scalar(stat[:, o + 4:o + 8], stat[:, o:o + 4], -1.0, None, ALU.mult).then_inc(n_max, 1)
                if k == 3:
                    dve.wait_ge(c_pt, 1)
                    V.tensor_copy(c_t[:, 0:512], bank[:, 0, :]).then_inc(c_ptc, 1)
                if k >= 2:
                    dve.wait_ge(n_pt, 2 * k - 2)
                    if k >= 4:
                        dve.wait_ge(n_pv, k - 3)
                    V.tensor_copy(n_t[k % 2][:, 512:768], bank[:, 7, 0:256]).then_inc(n_ptd, 1)
                if 1 <= k <= G_HEADS:
                    g, o = k - 1, 16 * ((k - 1) % 3)
                    dve.wait_ge(n_exp, 4 * k)
                    st.done(V.reciprocal(stat[:, o + 12:o + 16], stat[:, o + 8:o + 12]))
                    for m, ap in enumerate(n_parts(g)):
                        at = 3 * NSA_ORDER[g] + 1 + m % 2
                        ins = V.tensor_scalar(ap, ap, stat[:, o + 12 + m:o + 13 + m],
                                              nsa_g[:, 1 - m // 2, at:at + 1], ALU.mult, ALU.mult)
                    ins.then_inc(n_prob, 1)
                if k in (1, 2):
                    nxt(C["phi"] + k + 1)
                if k == 1:
                    dve.wait_ge(c_scores, 1)
                    dve.wait_ge(setup, 6)
                    for q in range(2):
                        c = c_p[:, q, :, :, 0:c_n[q]]
                        first = (159, 31)[q]
                        bs = gate_or_bias[:, :, first:256:16].rearrange("p (g t) n -> p t g n", g=4)
                        src = bank[:, q, :].rearrange("p (t g n) -> p t g n", t=4, g=4)[:, :, :, 0:c_n[q]]
                        st.done(V.tensor_tensor(c, src, bs, ALU.add))
                        st.done(V.tensor_reduce(by_head(c_max[:, q, :]), c, AX.X, ALU.max))
                        mx = c_max[:, q, :].rearrange("p (t g n) -> p t g n", t=4, n=1).to_broadcast([P, 4, 4, c_n[q]])
                        V.tensor_tensor(c, c, mx, ALU.subtract).then_inc(c_sub, 1)
                if k == 2:
                    dve.wait_ge(c_exp, 2)
                    for q in range(2):
                        c = c_p[:, q, :, :, 0:c_n[q]]
                        st.done(V.tensor_reduce(by_head(c_sum[:, q, :]), c, AX.X, ALU.add))
                    st.done(V.reciprocal(c_rec, c_sum))
                    for q in range(2):
                        g0 = nsa_g[:, q, 0:48:3].rearrange("p (g t) -> p t g", g=4)
                        st.done(V.tensor_tensor(by_head(c_fac[:, q, :]), by_head(c_rec[:, q, :]), g0, ALU.mult))
                        c = c_p[:, q, :, :, 0:c_n[q]]
                        fac = c_fac[:, q, :].rearrange("p (t g n) -> p t g n", t=4, n=1).to_broadcast([P, 4, 4, c_n[q]])
                        V.tensor_tensor(c, c, fac, ALU.mult).then_inc(c_prob, 1)
                if k % 4 == 3 and k >= 7:
                    m = k // 4 - 1
                    lo(y_l[:, 2 * m:2 * m + 2, :], two(bank[:, m % 2, :]), y_h[:, 2 * m:2 * m + 2, :])
            lo(y_l[:, 6:8, :], two(bank[:, 1, :]), y_h[:, 6:8, :])
            project_out("nsa_out", "mlp1", x_h, x_l)
            factor("mlp1")
            mlp("mlp1")
            finish("mlp1", 1.0, "final", None, None)
            factor("final")
            for t in range(KT):
                ins = V.scalar_tensor_tensor(out=x_f[:, t, :], in0=h[:, t, :], scalar=col("final", t),
                                             in1=r_sb[:, :], op0=ALU.mult, op1=ALU.mult)
                if t % 2 == 1:
                    ins.then_inc(y_ready, 1)

        @block.tensor
        def _(pe):
            mm = nc.tensor.matmul

            def product(out_, s, c, m, hi_, lo_, start, stop, **kw):
                mm(out_, w_hi[:, s, c:c + m], hi_, start=start, stop=False, **kw)
                mm(out_, w_hi[:, s, c:c + m], lo_, start=False, stop=False, **kw)
                return mm(out_, w_lo[:, s, c:c + m], hi_, start=False, stop=stop, **kw)

            def arrived(count):
                pe.wait_ge(lo_split, count)

            def pair(s, bk, hi_, lo_, pieces=None, first=False):
                if pieces is None:
                    for t in range(2):
                        for k in range(KT):
                            last = product(bank[:, bk, t * S:(t + 1) * S], s, k * 256 + t * P, P, hi_[:, k, :],
                                           lo_[:, k, :], k == 0, k == KT - 1)
                    return last
                for p in range(KT // 2):
                    pe.wait_ge(op_lo, pieces + p + 1)
                    if first:
                        if p < 3:
                            pe.wait_ge(first_lo, p + 1)
                        else:
                            arrived(1)
                    for t in range(2):
                        for k in range(2 * p, 2 * p + 2):
                            last = product(bank[:, bk, t * S:(t + 1) * S], s, k * 256 + t * P, P, hi_[:, k, :],
                                           lo_[:, k, :], k == 0 and t == 0, k == KT - 1, skip_group_check=True)
                return last

            def tokens(s, bk, width, kts, hi_, lo_, base, first, last_):
                for t in range(2):
                    for n, k in enumerate(kts):
                        tok = slice(t * P, t * P + P)
                        c = base + n * width if isinstance(base, int) else base[n]
                        o = bk(t)
                        a, b = hi_[:, k, tok], lo_[:, k, tok]
                        wh, wl = w_hi[:, s, c:c + width], w_lo[:, s, c:c + width]
                        kw = dict(skip_group_check=True)
                        mm(o, a, wh, start=first and n == 0, stop=False, **kw)
                        mm(o, a, wl, start=False, stop=False, **kw)
                        ins = mm(o, b, wh, start=False, stop=last_ and n == len(kts) - 1, **kw)
                return ins

            def sum_squares(count, bk=SUMS, tile=0):
                pe.wait_ge(sum_ready, count)
                mm(bank[:, bk, 0:S], ones[:, :], sq[:, tile, :], start=True, stop=True).then_inc(ss_ready, 1)

            def transposed_factors(c, *srcs):
                pe.wait_ge(r_ready, c)
                for n, src in enumerate(srcs):
                    for t in range(2):
                        ins = nc.tensor.transpose(bank[:, SUMS, 256 * n + P * t:256 * n + P * t + P],
                                                  src[:, P * t:P * t + P], ident)
                ins.then_inc(rt_mm, 1)

            def clear_acc():
                for j in range(4):
                    mm(bank[:, ACC + j, :], zeros[:, 0:P], zeros[:, :], start=True, stop=True)

            def down(s, hid, slot, last=False):
                for o in range(KT):
                    for f in range(2):
                        ins = product(bank[:, ACC + o // 2, (o % 2) * S:(o % 2) * S + S], s, f * D + o * P, P,
                                      hid[0][:, slot + f, :], hid[1][:, slot + f, :], False, last,
                                      skip_group_check=True)
                    if last and o in (1, 3, 5):
                        ins.then_inc(acc_ready, 1)
                ins.then_inc(chunk_used, 1)

            def ffn(name, piece, x_h, x_l, norm_no):
                c0, b = C[name], HID[name]
                if name == "ffn1":
                    pe.wait_ge(setup, 4)
                for f in range(2):
                    first = c0 + f == 0
                    if not first:
                        arrived(c0 + f + 1)
                    pair((c0 + f) % RING, TURN + f, x_h, x_l, piece if f == 0 else None, first).then_inc(chunk_used, 1)
                    if f == 0:
                        clear_acc()
                        sum_squares(norm_no)
                with pe.Fori(0, FFN_TURNS) as i:
                    for r in range(2):
                        c1 = c0 + 2 + 3 * r
                        for f in range(2):
                            arrived(i * 6 + (c1 + f + 1))
                            pe.wait_ge(ab_ready, i * 4 + (b + 2 * r + f + 1))
                            pair((c1 + f) % RING, TURN + f, x_h, x_l).then_inc(chunk_used, 1)
                        arrived(i * 6 + (c1 + 3))
                        pe.wait_ge(hid_lo, i * 4 + (b + 2 * r + 2))
                        down((c1 + 2) % RING, hidden[name], 2 * r)
                last = c0 + FF + FF // 2 - 1
                arrived(last + 1)
                pe.wait_ge(hid_lo, b + FF)
                down(last % RING, hidden[name], 0, True)

            def mlp(name, piece, norm_no):
                c0, b = C[name], HID[name]
                for j in range(2):
                    arrived(c0 + j + 1)
                    pair((c0 + j) % RING, TURN + j, x_h, x_l, piece if j == 0 else None).then_inc(chunk_used, 1)
                    if j == 0:
                        clear_acc()
                        sum_squares(norm_no)

                def step(r, i):
                    c = c0 + 2 + 2 * r
                    arrived(i * 6 + (c + 1))
                    pe.wait_ge(ab_ready, i * 3 + (b + r))
                    pair(c % RING, TURN + (r + 2) % 3, x_h, x_l).then_inc(chunk_used, 1)
                    arrived(i * 6 + (c + 2))
                    pe.wait_ge(hid_lo, i * 3 + (b + r + 1))
                    down((c + 1) % RING, hidden[name], 2 * r)

                with pe.Fori(0, MLP_TURNS) as i:
                    for r in range(3):
                        step(r, i)
                for j in range(3 * MLP_TURNS, MF - 2):
                    step(j % 3, j // 3)
                for j in range(MF - 2, MF):
                    c = c0 + MF + j
                    arrived(c + 1)
                    pe.wait_ge(hid_lo, b + j + 1)
                    down(c % RING, hidden[name], 2 * (j % 3), j == MF - 1)

            def project(name, banks, hi_, lo_, piece, waits=None):
                for j, bk in enumerate(banks):
                    c = C[name] + j
                    arrived(c + 1)
                    if waits is not None and waits[j] is not None:
                        pe.wait_ge(drained, waits[j])
                    pair(c % RING, bk, hi_, lo_, piece if j == 0 else None).then_inc(chunk_used, 1)

            ffn("ffn1", PC["ffn1"], x_h, x_l, 1)
            pe.wait_ge(con_in, 16)
            pe.wait_ge(relb_in, 16)
            mm(bank[0:16, 6, 0:384], relb[:, :], con[0:33, CN["bucket"]:CN["bucket"] + 384], start=True,
               stop=True).then_inc(bias_mm, 1)

            project("latent", [TURN], x_h, x_l, PC["mix"])
            sum_squares(2)
            for j in range(1, 3):
                c = C["latent"] + j
                arrived(c + 1)
                if j == 2:
                    pe.wait_ge(bias_ready, 1)
                pair(c % RING, TURN + j, x_h, x_l).then_inc(chunk_used, 1)
            project("sb_q", [TURN, TURN + 1], x_h, x_l, None, [1, 2])
            project("sb_k", [TURN + 2, TURN], x_h, x_l, None, [3, 4])
            sum_squares(3)
            sum_squares(4, 3, 3)
            for j in range(2):
                arrived(C["sb_v"] + j + 1)
                tokens((C["sb_v"] + j) % RING, lambda t: bank[:, t, :], 512, range(4 * j, 4 * j + 4), x_h, x_l, 0,
                       j == 0, j == 1).then_inc(chunk_used, 1)
            transposed_factors(1, r_sb, r_lat[:, 1, :])
            for j in range(2):
                arrived(C["q_up"] + j + 1)
                if j == 1:
                    pe.wait_ge(sv_done, 2)
                s = (C["q_up"] + j) % RING
                for hh in range(4):
                    o = bank[0:QK, 2 - 2 * j + hh // 2, (hh % 2) * S:(hh % 2) * S + S]
                    for k in range(3):
                        last = product(o, s, k * 384 + hh * QK, QK, y_h[:, k, :], y_l[:, k, :], k == 0, k == 2)
                last.then_inc(chunk_used, 1)
            arrived(C["kv_up"] + 1)
            s = C["kv_up"] % RING
            for t in range(4):
                for k in range(2):
                    product(bank[:, 4 + t // 2, (t % 2) * S:(t % 2) * S + S], s, k * D + t * P, P, y_h[:, 3 + k, :],
                            y_l[:, 3 + k, :], k == 0, k == 1)
            pe.wait_ge(qk_raw, 2)
            tokens(s, lambda t: bank[:, 2 + t, :], 512, (3, 4), y_h, y_l, [512, D + 512], True,
                   True).then_inc(chunk_used, 1)

            def gate_unit(u, ks=range(KT)):
                j, t = u // 2, u % 2
                c = C["gates"] + j
                if t == 0:
                    arrived(c + 1)
                    if j >= 2:
                        pe.wait_ge(drained, DRAIN["gates"] + j - 1)
                for k in ks:
                    last = product(bank[:, 6 + j % 2, t * S:(t + 1) * S], c % RING, k * 256 + t * P, P, x_h[:, k, :],
                                   x_l[:, k, :], k == 0, k == KT - 1)
                if t == 1 and k == KT - 1:
                    last.then_inc(chunk_used, 1)

            for u in range(4):
                gate_unit(u)

            for hd in range(16):
                p = hd // 2
                pe.wait_ge(sq_ready, SQ["head"] + p + 1)
                src = (sq if p < 4 else x_f)[0:QK, 2 * (p % 4) + hd % 2, :]
                pick = con[0:QK, CN["pick"] + 15 - hd:CN["pick"] + 31 - hd]
                ins = mm(bank[0:16, 0, 0:S], pick, src, start=hd == 0, stop=hd == 15)
            ins.then_inc(ss_ready, 1)

            def rotate(p):
                pe.wait_ge(normed, p + 1)
                mm(bank[64:96, pair_bank[p], :], con[64:96, CN["rot"]:CN["rot"] + 32],
                   heads[64:96, 2 * p:2 * p + 2, :].rearrange("p a b -> p (a b)"), start=True,
                   stop=True).then_inc(rot_ready, 1)

            for p in range(4):
                rotate(p)
            gate_unit(4)
            pe.wait_ge(r_head, 1)
            for t in range(2):
                ins = nc.tensor.transpose(bank[:, 0, 16 * t:16 * t + 16], t_b[0:16, P * t:P * t + P],
                                          con[0:16, CN["ident"]:CN["ident"] + 16])
            ins.then_inc(rq_mm, 1)

            def key_factors(p):
                for e in range(2):
                    hd = 2 * p + e
                    row = con[0:16, CN["ident"] + hd:CN["ident"] + hd + 1].to_broadcast([16, QK])
                    ins = mm(bank[0:QK, pair_bank[p], e * S:e * S + S], row, t_b[0:16, :], start=True, stop=True)
                ins.then_inc(bc_ready, 1)

            key_factors(4)
            pe.wait_ge(rq_done, 2)
            key_factors(5)
            for p in range(6, 8):
                pe.wait_ge(roped, p - 5)
                key_factors(p)
            gate_unit(5)
            for p in range(4, 8):
                rotate(p)
            gate_unit(6)

            pe.wait_ge(roped, 8)
            for hd in range(HEADS + 1):
                if hd < HEADS:
                    if hd >= 1:
                        pe.wait_ge(m_max, hd)
                    q, k = heads[0:QK, hd, :], heads[0:QK, 8 + hd, :]
                    mm(bank[:, 0, 0:128], q[:, 0:128], k[:, 0:128], start=True, stop=True)
                    mm(bank[:, 0, 128:384], q[:, 128:256], k, start=True, stop=True).then_inc(m_scores, 1)
                    if hd >= 2:
                        pe.wait_ge(s_x, hd - 1)
                    z = bank[:, z_bank[hd % 2], :]
                    r = slice(64 * (hd % 2), 64 * (hd % 2) + 64)
                    q, k = sb_q[r, hd // 2, :], sb_k[r, hd // 2, :]
                    kw = dict(skip_group_check=True)
                    mm(z[:, 0:256], k[:, 0:128], q, start=True, stop=False, **kw)
                    mm(z[:, 256:384], k[:, 128:256], q[:, 128:256], start=False, stop=False, **kw).then_inc(s_z, 1)
                if hd == 0:
                    gate_unit(7)
                if hd >= 1:
                    g = hd - 1
                    r = slice(64 * (g % 2), 64 * (g % 2) + 64)
                    pe.wait_ge(s_l, g + 1)
                    e = bank[:, z_bank[g % 2], :]
                    mm(e[:, 0:384], cst("tri", P), s_lm, start=False, stop=False, **kw)
                    mm(e[:, 128:256], ones[:, :], s_lm[:, 256:384], start=False, stop=True, **kw).then_inc(s_e, 1)
                    pe.wait_ge(m_prob, g + 1)
                    if g >= 1:
                        pe.wait_ge(m_ptc, g)
                    mp, b2 = m_p[g % 2], bank[:, 2, :]
                    for blk in range(3):
                        ins = nc.tensor.transpose(b2[:, blk * P:blk * P + P], mp[:, blk * P:blk * P + P], ident)
                    ins.then_inc(m_pt, 1)
                    gate_unit(8 + g, range(KT if g < HEADS - 1 else KT // 2))
                    cols = slice(g * 64, g * 64 + 64)
                    ob = 4 + g // 2 % 2
                    pe.wait_ge(m_ptc, g + 1)
                    if g >= 4 and g % 2 == 0:
                        pe.wait_ge(op_lo, PC["o"] + g // 2 - 1)
                    om, mt = bank[r, ob, 0:S], m_t[g % 2]
                    mm(om, mv[:, 0, cols], mt[:, 0:256], start=True, stop=False).then_inc(m_pv, 1)
                    mm(om[:, 128:256], mv[:, 1, cols], mt[:, 256:384], start=False, stop=True).then_inc(m_pv, 1)
                    pe.wait_ge(s_a, g + 1)
                    os, sp_ = bank[r, ob, S:2 * S], s_p[g % 2]
                    mm(os, sv[:, 0, cols], sp_[:, 0:256], start=True, stop=False)
                    mm(os[:, 128:256], sv[:, 1, cols], sp_[:, 256:384], start=False, stop=True).then_inc(s_pv, 1)
            gate_unit(15, range(KT // 2, KT))

            for half in range(2):
                for w in range(2):
                    c = C["branch"] + 2 * half + w
                    arrived(c + 1)
                    pe.wait_ge(op_lo, PC["o"] + 4)
                    for o in range(4):
                        dst = bank[:, 4 * half + 2 * w + o // 2, (o % 2) * S:(o % 2) * S + S]
                        for k in range(4):
                            last = product(dst, c % RING, k * 512 + o * P, P, y_h[:, 4 * w + k, :],
                                           y_l[:, 4 * w + k, :], k == 0, k == 3)
                    last.then_inc(chunk_used, 1)
            project("w_out", range(4), x_h, x_l, PC["merged"])

            ffn("ffn2", PC["ffn2"], y_h, y_l, 5)

            project("ple_gate0", [0], y_h, y_l, PC["ple"])
            sum_squares(6, 3)
            arrived(C["ple_proj"] + 1)
            for o in range(KT):
                for k in range(2):
                    last = product(bank[:, 4 + o // 2, (o % 2) * S:(o % 2) * S + S], C["ple_proj"] % RING,
                                   k * D + o * P, P, x_h[:, k, :], x_l[:, k, :], k == 0, k == 1)
            last.then_inc(chunk_used, 1)
            for j in range(1, 4):
                arrived(PLE_GATE[j] + 1)
                if j == 3:
                    pe.wait_ge(ms_ready, NO["ple"] + 1)
                pair(PLE_GATE[j] % RING, j, y_h, y_l).then_inc(chunk_used, 1)

            c = C["conv_in"]
            for j in range(3):
                arrived(c + j + 1)
                pair((c + j) % RING, TURN + j, x_h, x_l, PC["mix0"] if j == 0 else None).then_inc(chunk_used, 1)
                if j == 0:
                    sum_squares(7)
            with pe.Fori(1, 4) as i:
                for j in range(3):
                    arrived(i * 3 + (c + j + 1))
                    pe.wait_ge(drained, i * 3 + (DRAIN["conv"] + j - 2))
                    pair((c + j) % RING, TURN + j, x_h, x_l).then_inc(chunk_used, 1)
            project("conv_out", range(4), y_h, y_l, PC["conv"])
            mlp("mlp0", PC["mlp0"], 8)

            project("kv_raw", [TURN], x_h, x_l, PC["kv"])
            sum_squares(9)
            c = C["kv_raw"] + 1
            arrived(c + 1)
            pair(c % RING, TURN + 1, x_h, x_l).then_inc(chunk_used, 1)
            project("k_att", [6, 0], x_h, x_l, None)
            transposed_factors(2, r_sb)
            for w in range(2):
                c = C["v_att"] + w
                arrived(c + 1)
                tokens(c % RING, lambda t: bank[:, 1 + w, t * 256:t * 256 + 256], 256, range(KT), x_h, x_l, 0, True,
                       True).then_inc(chunk_used, 1)
            for j in range(4):
                c = C["nsa_q"] + j
                arrived(c + 1)
                if j == 0:
                    pe.wait_ge(blk_ready, 8)
                if j == 2:
                    pe.wait_ge(kv_done, 3)
                if j == 3:
                    pe.wait_ge(q_done, 1)
                pair(c % RING, TURN + j % 3, y_h, y_l, PC["mix1"] if j == 0 else None).then_inc(chunk_used, 1)
            arrived(C["nsa_gate"] + 1)
            tokens(C["nsa_gate"] % RING, lambda t: bank[:, SUMS, t * 48:t * 48 + 48], 48, range(KT), y_h, y_l, 0,
                   True, True).then_inc(chunk_used, 1)
            pe.wait_ge(op_lo, PC["blk_v"] + 1)
            pe.wait_ge(g_raw, 1)
            for w in range(2):
                for half in range(2):
                    c = C["phi"] + 2 * w + half
                    arrived(c + 1)
                    for l in range(8):
                        a, o = 960 * w + (8 * half + l) * 60, bank[0:120, (7, 3)[w], 0:256]
                        wh, wl = (t[:, c % RING, l * 256:l * 256 + 256] for t in (w_hi, w_lo))
                        mm(o, x_hf[:, a:a + 120], wh, start=half == 0 and l == 0, stop=False)
                        mm(o, x_hf[:, a:a + 120], wl, start=False, stop=False)
                        last = mm(o, x_lf[:, a:a + 120], wh, start=False, stop=half == 1 and l == 7)
                    last.then_inc(chunk_used, 1)
            pe.wait_ge(kv_done, 8)
            pe.wait_ge(q_done, 4)
            T = nc.tensor.transpose

            def n_score(k):
                if k >= 2:
                    pe.wait_ge(n_max, k - 1)
                t, e = k // 2, k % 2
                r, j = slice(64 * e, 64 * e + 64), t // 4
                keys = heads[r, 8 + j:12:2, :]
                mm(bank[:, 4 - 2 * e, :], n_q[r, t, 128:256], keys, start=True, stop=True)
                mm(bank[:, 5 - 2 * e, 0:256], n_q[r, t, 0:128], keys[:, :, 0:128], start=True,
                   stop=True).then_inc(n_scores, 1)

            for w in range(2):
                pe.wait_ge(phi_hid, w + 1)
                for k in range(2):
                    at = 120 * w + 60 * k
                    ins = T(bank[:, 0, at:at + 60], phi_h[:, w, P * k:P * k + P], con[0:60, CN["ident"]:CN["ident"] + 60])
            ins.then_inc(phi_t, 1)
            pe.wait_ge(phi_hid, 3)
            kw = dict(skip_group_check=True)
            for g in range(4):
                e = g % 2
                for k in range(2):
                    mm(bank[64 * e:64 * e + 64, 1, (g // 2) * 16:(g // 2) * 16 + NCMP],
                       col("phi_k2", k * 64, 64), cmp_hid[:, 0, k, g * NCMP:(g + 1) * NCMP],
                       start=k == 0, stop=k == 1, **kw)
            for g in range(4):
                for k in range(2):
                    ins = mm(bank[32 * g:32 * g + NCMP, 1, 64:128], cmp_hid[:, 1, k, g * NCMP:(g + 1) * NCMP],
                             col("phi_v2", k * 64, 64), start=k == 0, stop=k == 1, **kw)
            ins.then_inc(phi_mm, 1)

            b6, b7 = bank[:, 6, :], bank[:, 7, :]
            for k in range(G_HEADS + 3):
                if k < G_HEADS:
                    n_score(k)
                if k == 1:
                    pe.wait_ge(cmp_done, 2)
                    for t in range(KT):
                        at = (t % 4) * 128 + (t // 4) * 64
                        for q in range(2):
                            o = bank[:, q, at:at + 64].rearrange("p (e n) -> p e n", e=2)[:, :, 0:c_n[q]]
                            ins = mm(o, n_q[:, t, P * q:P * q + P], k_cmp[:, t // 4, :, 0:c_n[q]], start=True,
                                     stop=True)
                    ins.then_inc(c_scores, 1)
                if k == 3:
                    for q in range(2):
                        pe.wait_ge(c_prob, q + 1)
                        for t in range(4):
                            at = (t % 2) * S + q * P
                            ins = T(bank[:, t // 2, at:at + P],
                                    y_flat[:, 512 * q + 128 * t:512 * q + 128 * t + 128], ident)
                    ins.then_inc(c_pt, 1)
                if 2 <= k <= G_HEADS + 1:
                    (s1, w1, s0, w0) = n_parts(k - 2)
                    pe.wait_ge(n_prob, k - 1)
                    if k >= 3:
                        pe.wait_ge(n_ptc, k - 2)
                        pe.wait_ge(n_ptd, k - 2)
                    T(b6[:, 0:128], s0, ident)
                    T(b6[:, 128:256], s1[:, 0:128], ident)
                    T(b6[:, 256:384], w0, ident)
                    T(b6[:, 384:512], w1[:, 0:128], ident).then_inc(n_pt, 1)
                    T(b7[:, 0:128], s1[:, 128:256], ident)
                    T(b7[:, 128:256], w1[:, 128:256], ident).then_inc(n_pt, 1)
                if k == 3:
                    pe.wait_ge(c_ptc, 2)
                if k >= 3:
                    g = k - 3
                    nt = n_t[g % 2]
                    t, e = g // 2, g % 2
                    grp = 2 * (t // 4) + e
                    cols, own = slice(64 * grp, 64 * grp + 64), slice(32 * grp, 32 * grp + NCMP)
                    o = bank[64 * e:64 * e + 64, t // 2 % 2, (t % 2) * S:(t % 2) * S + S]
                    pe.wait_ge(n_ptc, g + 1)
                    if g >= 8 and g % 4 == 0:
                        pe.wait_ge(op_lo, PC["o_nsa"] + g // 4 - 1)
                    mm(o, n_vs[:, 0, cols], nt[:, 0:256], start=True, stop=False)
                    mm(o, n_vw[:, 0, cols], nt[:, 256:512], start=False, stop=False)
                    mm(o, v_cmp[own, :], c_t[own, (t % 4) * S:(t % 4) * S + S], start=False, stop=False)
                    pe.wait_ge(n_ptd, g + 1)
                    mm(o[:, 128:256], n_vs[:, 1, cols], nt[:, 512:640], start=False, stop=False)
                    mm(o[:, 128:256], n_vw[:, 1, cols], nt[:, 640:768], start=False, stop=True).then_inc(n_pv, 1)
            project("nsa_out", range(4), y_h, y_l, PC["o_nsa"])
            mlp("mlp1", PC["mlp1"], 10)
            sum_squares(11)


NSA_ORDER = [(2 * (t // 4) + e) * 4 + t % 4 for t in range(8) for e in range(2)]


def make_constants():
    c = np.zeros((P, N_CONST), np.float32)

    def put(name, a, row=0):
        c[row:row + a.shape[0], CN[name]:CN[name] + a.shape[1]] = a

    i, j = np.arange(P)[:, None], np.arange(P)[None, :]
    put("ident", np.eye(P, dtype=np.float32))
    put("tri", (i >= j).astype(np.float32))
    strict = np.where(i < j, 0.0, NEG).astype(np.float32)
    put("sb_neg", np.concatenate([strict, np.zeros((P, P), np.float32), strict], 1))
    put("mla_neg", np.concatenate([np.zeros((P, P)), np.where(j <= i, 0.0, NEG)], 1).astype(np.float32))
    rot = np.zeros((32, 32), np.float32)
    for m in range(16):
        rot[m + 16, m] = -1.0
        rot[m, m + 16] = 1.0
    put("rot", rot, 64)
    d = 255 - np.arange(384)
    large = 16 + np.floor(np.log(np.maximum(d, 1) / 16.0) / np.log(8.0) * 16 + 1e-9).astype(int)
    bucket = np.where(d < 16, d, np.minimum(large, 31))
    onehot = np.zeros((33, 384), np.float32)
    for n in range(384):
        onehot[32 if d[n] < 0 else bucket[n], n] = 1.0
    put("bucket", onehot)
    pick = np.zeros((P, 31), np.float32)
    pick[:, 15] = 1.0
    put("pick", pick)
    inv = np.float32(10000.0) ** (-np.arange(0, ROPE, 2, dtype=np.float32) / np.float32(ROPE))
    put("inv_freq", np.concatenate([inv, inv])[:, None].astype(np.float32), 64)
    put("has_any", (np.arange(P) >= 31).astype(np.float32)[:, None])
    return c


def pack_weights(w):
    chunks = []

    def add(a):
        a = a.reshape(P, -1)
        n = -(-a.shape[1] // CH) * CH
        a = np.concatenate([a, np.zeros((P, n - a.shape[1]), np.float32)], 1)
        chunks.extend(a[:, k:k + CH] for k in range(0, n, CH))

    def rows(a, kt=None):
        return a.reshape(-1, P, a.shape[1]).transpose(1, 0, 2)

    def pairs(a):
        for n in range(0, a.shape[1], 256):
            add(rows(a[:, n:n + 256]))

    def ffn(w_in, w_out):
        n = FF * P
        up = lambda f: add(rows(np.concatenate([w_in[:, f * P:f * P + P], w_in[:, n + f * P:n + f * P + P]], 1)))
        down = lambda i: add(rows(w_out[256 * i:256 * i + 256]))
        for i in range(FF // 2 + 1):
            if i < FF // 2:
                up(2 * i)
                up(2 * i + 1)
            if i >= 1:
                down(i - 1)

    def mlp(w1, w2):
        for j in range(MF + 2):
            if j < MF:
                add(rows(w1[:, 256 * j:256 * j + 256]))
            if j >= 2:
                add(rows(w2[256 * (j - 2):256 * (j - 1)]))

    ffn(w["ffn1_w_in"][0], w["ffn1_w_out"][0])
    w_in = w["w_in"][0]
    pairs(np.concatenate([w_in[:, 0:672], np.zeros((D, 96), np.float32)], 1))
    pairs(w_in[:, 672:672 + 1024])
    for j in range(2):
        add(rows(w_in[512 * j:512 * j + 512, 1696:2208]))
    for j in range(2):
        add(rows(w["w_q_up"][0][:, 384 * j:384 * j + 384]))
    kv = w["w_kv_up"][0].reshape(256, 8, 2, 64)
    add(rows(kv.transpose(0, 2, 1, 3).reshape(256, 1024)))
    pairs(w_in[:, 2208:])
    for half in range(2):
        for name in ("w_branch_mla", "w_branch_sb"):
            add(rows(w[name][0][:, 512 * half:512 * half + 512]))
    pairs(w["w_out"][0])
    ffn(w["ffn2_w_in"][0], w["ffn2_w_out"][0])
    gate = w["w_ple_gate"][0]
    pairs(gate[:, 0:256])
    add(rows(w["w_ple_proj"][0]))
    pairs(gate[:, 256:])
    a_in = w["a_w_in_2"][0]
    tile = lambda k, t: a_in[:, k * D + t * P:k * D + t * P + P]
    for i in range(4):
        for a, b in ((tile(1, 2 * i), tile(2, 2 * i)), (tile(1, 2 * i + 1), tile(2, 2 * i + 1)),
                     (tile(0, 2 * i), tile(0, 2 * i + 1))):
            add(rows(np.concatenate([a, b], 1)))
    pairs(w["a_w_out_2"][0])
    mlp(w["mlp_w1_2"][0], w["mlp_w2_2"][0])
    for k in (0, 1, 2, 4, 3, 5):
        add(rows(w["w_kv_2"][:, 256 * k:256 * k + 256]))
    qg = w["b_w_qg_2"][0]
    pairs(qg[:, :D].reshape(D, 16, 64)[:, NSA_ORDER].reshape(D, D))
    add(rows(qg[:, D:]))
    for name in ("phi_k_w1_2", "phi_v_w1_2"):
        add(w[name].reshape(2, 16, 64, 256).transpose(0, 2, 1, 3).reshape(P, 16 * 256))
    pairs(w["b_w_o_2"][0].reshape(16, 64, D)[NSA_ORDER].reshape(D, D))
    mlp(w["mlp_w1_2"][1], w["mlp_w2_2"][1])
    out = np.stack(chunks)
    assert out.shape == (N_CHUNKS, P, CH), out.shape
    return out


def pack_small(w):
    s = np.zeros((P, N_SMALL), np.float32)
    s_cols = lambda v: v.reshape(-1, P).T

    def put(name, a):
        s[:a.shape[0], SM[name]:SM[name] + a.shape[1]] = a

    for name, v in (("ffn1", w["ffn1_norm"][0]), ("mix", w["mix_norm"][0]), ("c_q", w["q_latent_norm"][0]),
                    ("c_kv", w["kv_latent_norm"][0]), ("ffn2", w["ffn2_norm"][0]), ("ple", w["ple_norm"][0]),
                    ("mix0", w["norm_mix_2"][0]), ("mlp0", w["norm_mlp_2"][0]), ("kv", w["kv_norm_2"]),
                    ("mix1", w["norm_mix_2"][1]), ("mlp1", w["norm_mlp_2"][1]), ("final", w["final_norm_2"])):
        put(name, s_cols(v))
    put("conv_w", np.concatenate([s_cols(w["a_conv_w_2"][0][k]) for k in range(3)], 1))
    put("q_head", w["q_head_norm"][0][:, None])
    put("k_head", w["k_head_norm"][0][:, None])
    for name in ("k", "v"):
        put("pe_" + name, w[f"cmp_pe_{name}_2"].reshape(2, 16, 64).transpose(0, 2, 1).reshape(P, 16))
        put(f"phi_{name}2", w[f"phi_{name}_w2_2"].reshape(2, P, 64).transpose(1, 0, 2).reshape(P, P))
    return s


def kernel(**inputs):
    import concourse.bacc as _bacc
    from concourse.bass_utils import run_bass_kernel_spmd as _run

    w = {k: np.asarray(v) for k, v in inputs.items()}
    tok = lambda a: np.ascontiguousarray(a.T.reshape(-1, P, S).transpose(1, 0, 2))
    arrays = {
        "x_t": tok(w["x"][0]),
        "p_t": tok(w["p"][0, 0]),
        "positions": np.ascontiguousarray(w["positions"][0]),
        "weights": pack_weights(w),
        "small": pack_small(w),
        "consts": make_constants(),
        "rel_bias": np.ascontiguousarray(w["rel_bias_2"]),
    }
    nc = _bacc.Bacc("TRN2", target_bir_lowering=False, num_devices=1)
    aps = {k: nc.dram_tensor(k, a.shape, mybir.dt.from_np(a.dtype), kind="ExternalInput").ap()
           for k, a in arrays.items()}
    bias_rows = nc.dram_tensor("bias_rows", (16, 384), F32)
    bias_skew = nc.dram_tensor("bias_skew", (G_HEADS, P * SKEW), F32)
    out = nc.dram_tensor("out_t", (P, KT, S), F32, kind="ExternalOutput").ap()
    program(nc, bias_rows=bias_rows, bias_skew=bias_skew, out=out, **aps)
    r = _run(nc, [arrays], core_ids=[0])
    y = r.results[0]["out_t"]
    return y.transpose(2, 1, 0).reshape(1, S, D)
```
